# Optimizing a Trainium2 kernel written in Bass

```python
import math
import jax, jax.numpy as jnp
from jax import lax
import numpy as np

D_MODEL = 1024
BATCH = 1
SEQ = 1024
DEPTH = 2
DEC_BATCH = 8
DEC_SEQ = 1
PAST_LEN = 8192
PAGE_SIZE = 128

N_EVEN = (DEPTH + 1) // 2
N_ODD = DEPTH // 2
POOL_WINDOWS = (2, 4, 8, 16)
N_POOL_GROUPS = len(POOL_WINDOWS)
D_POOL = D_MODEL
POOL_GROUP = D_POOL // N_POOL_GROUPS
POOL_BUF = max(POOL_WINDOWS) - 1
D_CONV = D_MODEL
CONV_K = 3
EVEN_IN = 2 * D_POOL + 4 * D_CONV
EVEN_MIX = D_POOL + D_CONV
SSM_EXPAND = 2
D_INNER = SSM_EXPAND * D_MODEL
SSM_HEAD_DIM = 64
SSM_HEADS = D_INNER // SSM_HEAD_DIM
SSM_GROUPS = 4
SSM_HEADS_PER_GROUP = SSM_HEADS // SSM_GROUPS
SSM_STATE = 128
SSM_CONV_K = 4
SSM_CONV_DIM = D_INNER + 2 * SSM_GROUPS * SSM_STATE
ODD_IN = D_INNER + SSM_CONV_DIM + SSM_HEADS
SSM_CHUNK = 128
N_MEM = 256
XA_HEADS = 4
XA_HEAD_DIM = D_MODEL // XA_HEADS
EPS = 1e-6

kernel_name = 'pool_conv_ssd_memxattn_decoder_step'

def rmsnorm(x, g):
    xf = x.astype(jnp.float32)
    y = xf * lax.rsqrt(jnp.mean(xf * xf, axis=-1, keepdims=True) + EPS)
    return (y * g.astype(jnp.float32)).astype(x.dtype)

def causal_dwconv(v, prefix, w):
    K = w.shape[0]
    L = v.shape[1]
    ext = jnp.concatenate([prefix.astype(v.dtype), v], axis=1)
    out = ext[:, 0:L] * w[0]
    for k in range(1, K):
        out = out + ext[:, k:k + L] * w[k]
    return out, ext[:, ext.shape[1] - (K - 1):]

def pool_mixer(u, prefix, pos0, w_grp, scale):
    b, L, _ = u.shape
    f32 = jnp.float32
    ext = jnp.concatenate([prefix.astype(u.dtype), u], axis=1).astype(f32)
    cs = jnp.concatenate([jnp.zeros((b, 1, D_POOL), f32), jnp.cumsum(ext, axis=1)], axis=1)
    pos = pos0 + jnp.arange(L)
    end = cs[:, POOL_BUF + 1:]
    uf = u.astype(f32)
    outs = []
    for g, w in enumerate(POOL_WINDOWS):
        sl = slice(g * POOL_GROUP, (g + 1) * POOL_GROUP)
        start = cs[:, POOL_BUF + 1 - w:POOL_BUF + 1 - w + L, sl]
        cnt = jnp.minimum(pos + 1, w).astype(f32)[None, :, None]
        diff = ((end[..., sl] - start) / cnt - uf[..., sl]).astype(u.dtype)
        outs.append(diff @ w_grp[g])
    y = jnp.concatenate(outs, axis=-1) * scale
    return y, ext[:, ext.shape[1] - POOL_BUF:].astype(u.dtype)

def even_mixer(h, pool_prefix, conv_prefix, pos0, w_in, pool_w, pool_scale, conv_w, w_out):
    proj = h @ w_in
    c0 = D_POOL
    c1 = c0 + D_POOL
    c2 = c1 + D_CONV
    c3 = c2 + D_CONV
    c4 = c3 + D_CONV
    u, g_pool = proj[..., :c0], proj[..., c0:c1]
    b_gate, c_gate, v, g_conv = proj[..., c1:c2], proj[..., c2:c3], proj[..., c3:c4], proj[..., c4:]
    y_pool, pool_buf = pool_mixer(u, pool_prefix, pos0, pool_w, pool_scale)
    y_pool = y_pool * jax.nn.silu(g_pool)
    conv_out, conv_buf = causal_dwconv(c_gate * v, conv_prefix, conv_w)
    y_conv = b_gate * conv_out * jax.nn.silu(g_conv)
    return jnp.concatenate([y_pool, y_conv], axis=-1) @ w_out, pool_buf, conv_buf

def ssd_scan(x, dt, A, Bm, Cm, s0):
    b, L = x.shape[:2]
    Q = SSM_CHUNK if L % SSM_CHUNK == 0 else L
    nc = L // Q
    x = x.reshape((b, nc, Q) + x.shape[2:])
    dt = dt.reshape((b, nc, Q) + dt.shape[2:])
    Bm = Bm.reshape((b, nc, Q) + Bm.shape[2:])
    Cm = Cm.reshape((b, nc, Q) + Cm.shape[2:])
    a_cs = jnp.cumsum(dt * A, axis=2)
    xdt = x * dt[..., None]
    causal = jnp.tril(jnp.ones((Q, Q), bool))[:, :, None, None]
    seg = a_cs[:, :, :, None] - a_cs[:, :, None, :]
    decay = jnp.exp(jnp.where(causal, seg, -jnp.inf))
    cb = jnp.einsum('bclgn,bcsgn->bclsg', Cm, Bm)
    y_diag = jnp.einsum('bclsge,bcsgep->bclgep', cb[..., None] * decay, xdt)
    to_end = jnp.exp(a_cs[:, :, -1:] - a_cs)
    chunk_states = jnp.einsum('bcsgn,bcsgep->bcgepn', Bm, xdt * to_end[..., None])
    chunk_decay = jnp.exp(a_cs[:, :, -1])

    def step(s, inp):
        dec, st = inp
        return dec[..., None, None] * s + st, s

    s_fin, s_in = lax.scan(step, s0, (jnp.moveaxis(chunk_decay, 1, 0), jnp.moveaxis(chunk_states, 1, 0)))
    s_in = jnp.moveaxis(s_in, 0, 1)
    y_off = jnp.einsum('bclgn,bcgepn->bclgep', Cm, s_in) * jnp.exp(a_cs)[..., None]
    y = (y_diag + y_off).reshape((b, L) + x.shape[3:])
    return y, s_fin

def mamba2_mixer(h, conv_prefix, s0, w_in, conv_w, conv_b, dt_bias, a_log, d_skip, norm_w, w_out):
    b, L, _ = h.shape
    f32 = jnp.float32
    G, E, P, N = SSM_GROUPS, SSM_HEADS_PER_GROUP, SSM_HEAD_DIM, SSM_STATE
    proj = h @ w_in
    z = proj[..., :D_INNER]
    xbc = proj[..., D_INNER:D_INNER + SSM_CONV_DIM]
    dt_raw = proj[..., D_INNER + SSM_CONV_DIM:]
    xbc_c, conv_buf = causal_dwconv(xbc, conv_prefix, conv_w)
    xbc_c = jax.nn.silu(xbc_c + conv_b).astype(f32)
    gn = G * N
    xs = xbc_c[..., :D_INNER].reshape(b, L, G, E, P)
    Bm = xbc_c[..., D_INNER:D_INNER + gn].reshape(b, L, G, N)
    Cm = xbc_c[..., D_INNER + gn:].reshape(b, L, G, N)
    dt = jax.nn.softplus(dt_raw.astype(f32) + dt_bias.astype(f32)).reshape(b, L, G, E)
    A = -jnp.exp(a_log.astype(f32)).reshape(G, E)
    y, s_fin = ssd_scan(xs, dt, A, Bm, Cm, s0.astype(f32).reshape(b, G, E, P, N))
    y = y + d_skip.astype(f32).reshape(G, E)[..., None] * xs
    yg = y.reshape(b, L, G, E * P) * jax.nn.silu(z.astype(f32)).reshape(b, L, G, E * P)
    yg = yg * lax.rsqrt(jnp.mean(yg * yg, axis=-1, keepdims=True) + EPS)
    yg = (yg.reshape(b, L, D_INNER) * norm_w.astype(f32)).astype(h.dtype)
    return yg @ w_out, conv_buf, s_fin.reshape(b, SSM_HEADS, P, N).astype(h.dtype)

def mem_xattn(h, mk, mv, wq, wo):
    b, L, _ = h.shape
    q = (h @ wq).reshape(b, L, XA_HEADS, XA_HEAD_DIM).astype(jnp.float32)
    s = jnp.einsum('blhd,bmhd->bhlm', q, mk.astype(jnp.float32)) * (XA_HEAD_DIM ** -0.5)
    p = jax.nn.softmax(s, axis=-1)
    o = jnp.einsum('bhlm,bmhd->blhd', p, mv.astype(jnp.float32)).astype(h.dtype).reshape(b, L, D_MODEL)
    return o @ wo

def run_trunk(x, mem_k, mem_v, pool_st, conv_st, sconv_st, ssm_st, pos0, weights):
    (norm_mix, norm_xa, norm_final, w_in_even, pool_w, pool_scale, conv_w, w_out_even,
     w_in_odd, ssm_conv_w, ssm_conv_b, dt_bias, a_log, d_skip, ssm_norm, w_out_odd,
     w_xa_q, w_xa_o) = weights
    new_pool, new_conv, new_sconv, new_ssm = [], [], [], []
    for l in range(DEPTH):
        i = l // 2
        h = rmsnorm(x, norm_mix[l])
        if l % 2 == 0:
            out, pb, cbuf = even_mixer(h, pool_st[i], conv_st[i], pos0, w_in_even[i], pool_w[i],
                                       pool_scale[i], conv_w[i], w_out_even[i])
            new_pool.append(pb)
            new_conv.append(cbuf)
        else:
            out, sb, ss = mamba2_mixer(h, sconv_st[i], ssm_st[i], w_in_odd[i], ssm_conv_w[i], ssm_conv_b[i],
                                       dt_bias[i], a_log[i], d_skip[i], ssm_norm[i], w_out_odd[i])
            new_sconv.append(sb)
            new_ssm.append(ss)
        x = x + out
        x = x + mem_xattn(rmsnorm(x, norm_xa[l]), mem_k[l], mem_v[l], w_xa_q[l], w_xa_o[l])
    y = rmsnorm(x, norm_final)
    return y, jnp.stack(new_pool), jnp.stack(new_conv), jnp.stack(new_sconv), jnp.stack(new_ssm)

def setup_inputs(seed: int = 0) -> dict:
    key = jax.random.key(seed)
    ks = iter(jax.random.split(key, 32))
    f32 = jnp.float32

    def nrm(shape, scale):
        return jax.random.normal(next(ks), shape, f32) * scale

    x_prompt = nrm((BATCH, SEQ, D_MODEL), 1.0)
    x_sample = nrm((DEC_BATCH, DEC_SEQ, D_MODEL), 1.0)
    mem_prompt = nrm((BATCH, N_MEM, D_MODEL), 1.0)
    cache_mem_k = nrm((DEPTH, DEC_BATCH, N_MEM, XA_HEADS, XA_HEAD_DIM), 1.0)
    cache_mem_v = nrm((DEPTH, DEC_BATCH, N_MEM, XA_HEADS, XA_HEAD_DIM), 1.0)
    state_pool = nrm((N_EVEN, DEC_BATCH, POOL_BUF, D_POOL), 1.0)
    state_conv = nrm((N_EVEN, DEC_BATCH, CONV_K - 1, D_CONV), 1.0)
    state_ssm_conv = nrm((N_ODD, DEC_BATCH, SSM_CONV_K - 1, SSM_CONV_DIM), 1.0)
    state_ssm = nrm((N_ODD, DEC_BATCH, SSM_HEADS, SSM_HEAD_DIM, SSM_STATE), 0.1)

    norm_mix = 1.0 + nrm((DEPTH, D_MODEL), 0.02)
    norm_xa = 1.0 + nrm((DEPTH, D_MODEL), 0.02)
    norm_final = 1.0 + nrm((D_MODEL,), 0.02)

    w_in_even = nrm((N_EVEN, D_MODEL, EVEN_IN), D_MODEL ** -0.5)
    pool_w = nrm((N_EVEN, N_POOL_GROUPS, POOL_GROUP, POOL_GROUP), POOL_GROUP ** -0.5)
    pool_scale = 1.0 + nrm((N_EVEN, D_POOL), 0.02)
    conv_w = nrm((N_EVEN, CONV_K, D_CONV), CONV_K ** -0.5)
    w_out_even = nrm((N_EVEN, EVEN_MIX, D_MODEL), EVEN_MIX ** -0.5)

    w_in_odd = nrm((N_ODD, D_MODEL, ODD_IN), D_MODEL ** -0.5)
    ssm_conv_w = nrm((N_ODD, SSM_CONV_K, SSM_CONV_DIM), SSM_CONV_K ** -0.5)
    ssm_conv_b = nrm((N_ODD, SSM_CONV_DIM), 0.02)
    log_dt = jax.random.uniform(next(ks), (N_ODD, SSM_HEADS), f32, math.log(1e-3), math.log(1e-1))
    dt0 = jnp.exp(log_dt)
    dt_bias = dt0 + jnp.log(-jnp.expm1(-dt0))
    a_log = jnp.log(jax.random.uniform(next(ks), (N_ODD, SSM_HEADS), f32, 1.0, 16.0))
    d_skip = 1.0 + nrm((N_ODD, SSM_HEADS), 0.1)
    ssm_norm = 1.0 + nrm((N_ODD, D_INNER), 0.02)
    w_out_odd = nrm((N_ODD, D_INNER, D_MODEL), D_INNER ** -0.5)

    w_xa_q = nrm((DEPTH, D_MODEL, D_MODEL), D_MODEL ** -0.5)
    w_xa_k = nrm((DEPTH, D_MODEL, D_MODEL), D_MODEL ** -0.5)
    w_xa_v = nrm((DEPTH, D_MODEL, D_MODEL), D_MODEL ** -0.5)
    w_xa_o = nrm((DEPTH, D_MODEL, D_MODEL), D_MODEL ** -0.5)

    return {'x_prompt': x_prompt, 'x_sample': x_sample, 'mem_prompt': mem_prompt,
            'cache_mem_k': cache_mem_k, 'cache_mem_v': cache_mem_v, 'state_pool': state_pool,
            'state_conv': state_conv, 'state_ssm_conv': state_ssm_conv, 'state_ssm': state_ssm,
            'norm_mix': norm_mix, 'norm_xa': norm_xa, 'norm_final': norm_final,
            'w_in_even': w_in_even, 'pool_w': pool_w, 'pool_scale': pool_scale, 'conv_w': conv_w,
            'w_out_even': w_out_even, 'w_in_odd': w_in_odd, 'ssm_conv_w': ssm_conv_w,
            'ssm_conv_b': ssm_conv_b, 'dt_bias': dt_bias, 'a_log': a_log, 'd_skip': d_skip,
            'ssm_norm': ssm_norm, 'w_out_odd': w_out_odd, 'w_xa_q': w_xa_q, 'w_xa_k': w_xa_k,
            'w_xa_v': w_xa_v, 'w_xa_o': w_xa_o}

def reference(x_prompt, x_sample, mem_prompt, cache_mem_k, cache_mem_v, state_pool, state_conv,
              state_ssm_conv, state_ssm, norm_mix, norm_xa, norm_final, w_in_even, pool_w, pool_scale,
              conv_w, w_out_even, w_in_odd, ssm_conv_w, ssm_conv_b, dt_bias, a_log, d_skip, ssm_norm,
              w_out_odd, w_xa_q, w_xa_k, w_xa_v, w_xa_o):
    weights = (norm_mix, norm_xa, norm_final, w_in_even, pool_w, pool_scale, conv_w, w_out_even,
               w_in_odd, ssm_conv_w, ssm_conv_b, dt_bias, a_log, d_skip, ssm_norm, w_out_odd,
               w_xa_q, w_xa_o)
    bp = x_prompt.shape[0]
    dtype = x_prompt.dtype
    mem_k_prompt = jnp.einsum('bmd,lde->lbme', mem_prompt, w_xa_k).reshape(DEPTH, bp, N_MEM, XA_HEADS, XA_HEAD_DIM)
    mem_v_prompt = jnp.einsum('bmd,lde->lbme', mem_prompt, w_xa_v).reshape(DEPTH, bp, N_MEM, XA_HEADS, XA_HEAD_DIM)
    zero_pool = jnp.zeros((N_EVEN, bp, POOL_BUF, D_POOL), dtype)
    zero_conv = jnp.zeros((N_EVEN, bp, CONV_K - 1, D_CONV), dtype)
    zero_sconv = jnp.zeros((N_ODD, bp, SSM_CONV_K - 1, SSM_CONV_DIM), dtype)
    zero_ssm = jnp.zeros((N_ODD, bp, SSM_HEADS, SSM_HEAD_DIM, SSM_STATE), dtype)
    y_prompt, pool_prompt, conv_prompt, ssm_conv_prompt, ssm_prompt = run_trunk(
        x_prompt, mem_k_prompt, mem_v_prompt, zero_pool, zero_conv, zero_sconv, zero_ssm, 0, weights)
    y_sample, pool_sample, conv_sample, ssm_conv_sample, ssm_sample = run_trunk(
        x_sample, cache_mem_k, cache_mem_v, state_pool, state_conv, state_ssm_conv, state_ssm, PAST_LEN, weights)
    return (y_prompt, y_sample, mem_k_prompt, mem_v_prompt, pool_prompt, pool_sample, conv_prompt, conv_sample,
            ssm_conv_prompt, ssm_conv_sample, ssm_prompt, ssm_sample)


_drawn_inputs = setup_inputs


def setup_inputs(seed=0):
    import zlib

    import numpy as np

    out = dict(_drawn_inputs(seed))
    spreads = {}
    factors = {'norm_xa': 8.0, 'norm_final': 2.819, 'pool_scale': 5.466, 'ssm_norm': 4.444}
    for name, (base, spread) in spreads.items():
        noise = np.random.default_rng([zlib.crc32(name.encode()), seed]).standard_normal(out[name].shape)
        drawn = base * np.exp(spread * noise) if base else spread * noise
        out[name] = __import__('jax').numpy.asarray(drawn.astype(out[name].dtype))
    for name, factor in factors.items():
        out[name] = (out[name] * factor).astype(out[name].dtype)
    return out
```

```python
from contextlib import ExitStack, contextmanager

import numpy as np

import concourse.bass as bass
from concourse import mybir

F32 = mybir.dt.float32
F32R = mybir.dt.float32r
ALU = mybir.AluOpType
ACT = mybir.ActivationFunctionType
AX = mybir.AxisListType.X
ds = bass.ds

P = 128
D = 1024
KT = D // P
TP = 1024
NB = 8
T = TP + NB
NCH = 3
CH = T // NCH
TT = TP // P
NM = 256
MT = NM // P
HEADS, HD = 4, 256
POOL_BUF = 15
WINDOWS = (2, 4, 8, 16)
G, E, N = 4, 8, 128
D_INNER = 2048
CONV_DIM = D_INNER + 2 * G * N
XT = 4
EPS = 1e-6
NEG = -1e30
WARM = 16

PRM_MIX, PRM_XA, PRM_FIN, PRM_PSC, PRM_CW, PRM_SB, PRM_NW, PRM_SW = 0, 16, 32, 40, 48, 72, 96, 112
PRM_N = 208
C_ID, C_TRI, C_MASK, C_INV, C_ONE, C_N = 0, 128, 256, 768, 832, 834


def constants():
    c = np.zeros((P, C_N), np.float32)
    s, l = np.arange(P)[:, None], np.arange(P)[None, :]
    c[:, C_ID:C_ID + P] = s == l
    c[:, C_TRI:C_TRI + P] = s <= l
    for i in range(4):
        c[:, C_MASK + i * P:C_MASK + (i + 1) * P] = np.where(s <= l, 0.0, NEG)
    for g, w in enumerate(WINDOWS):
        c[:, C_INV + 16 * g:C_INV + 16 * g + 16] = w / np.minimum(np.arange(16) + 1, w)
    c[:, C_ONE] = 1.0
    return c


class Tally:

    def __init__(self):
        self.slot = [0, 0]
        self.result = 0
        self.taken = [0, 0]
        self.turn = 0
        self.made = [0, 0, 0]

    def unit(self):
        s = self.turn
        self.turn = 1 - s
        self.slot[s] += 1
        self.made[0] += 1
        return s, self.slot[s]

    def next(self, a):
        self.result += 1
        self.taken[a] += 1
        self.made[1 + a] += 1
        return a, self.result, self.taken[a]

    @contextmanager
    def loop(self, eng, lo, hi, units, results):
        was = [*self.slot], self.result, [*self.taken]
        with eng.Fori(lo, hi) as g:
            n = g - lo if lo else g
            self.slot = [v + n * (units // 2) for v in was[0]]
            self.result = was[1] + n * sum(results)
            self.taken = [v + n * r for v, r in zip(was[2], results)]
            self.made = [0, 0, 0]
            yield g
            assert self.made[0] in (0, units) and self.made[1:] in ([0, 0], [*results]), (self.made, units, results)
        n = hi - lo
        self.slot = [v + n * (units // 2) for v in was[0]]
        self.result = was[1] + n * sum(results)
        self.taken = [v + n * r for v, r in zip(was[2], results)]


def build(nc, ins, outs, scratch):
    ctx = ExitStack()
    with ctx:
        def sb(name, shape, dt=F32):
            return ctx.enter_context(nc.sbuf_tensor(name, shape, dt))

        def sem(name):
            return ctx.enter_context(nc.semaphore(name))

        table = sb("table", [P, C_INV], F32R)
        cst = sb("cst", [P, C_N - C_INV])
        prm = sb("prm", [P, PRM_N])
        zero = sb("zero", [P, 2])
        credit = sb("credit", [P, 10])
        u_keep = sb("u_keep", [P, KT, 23])
        c_keep = sb("c_keep", [P, KT, 10])
        x = sb("x", [P, KT, T])
        HPAD = KT * T + P
        h_hi_f = sb("h_hi", [P, HPAD], F32R)
        h_lo_f = sb("h_lo", [P, HPAD], F32R)
        w_raw = sb("w_raw", [P, 2, 1024])
        w_hi = sb("w_hi", [P, 2, 1024], F32R)
        w_lo = sb("w_lo", [P, 2, 1024], F32R)
        ms = sb("ms", [P, 9])
        sd = sb("sd", [P, 9])
        rstd = sb("rstd", [P, 9])

        class Area:

            def __init__(self, at):
                self.at = at

            def __call__(self, name, shape, dt=F32):
                t = nc.alloc_sbuf_tensor_at(name, shape, dt, offset=self.at)
                self.at += -(-int(np.prod(shape[1:])) * 4 // 32) * 32
                assert self.at <= work_end, name
                return t

        work = (nc.sbuf_base + 31) // 32 * 32
        work_end = nc.sbuf_usable_end

        h_hi = h_hi_f[:, 0:KT * T].rearrange("p (k t) -> p k t", k=KT)
        h_lo = h_lo_f[:, 0:KT * T].rearrange("p (k t) -> p k t", k=KT)

        a = Area(work)
        x_in = a("x_in", [P, 2, D])
        m_hi = a("m_hi", [P, KT, NM], F32R)
        m_lo = a("m_lo", [P, KT, NM], F32R)
        p_in = a("p_in", [P, 2, P])
        kt_out = a("kt_out", [P, 2, NM])
        kv_nat_sb = a("kv_nat_sb", [P, 2, MT, D])
        assert a.at <= work + 48 * 1024
        late = work + 69 * 1024
        a = Area(work + 48 * 1024)
        st_rows = a("st_rows", [P, D])
        cst_rows = a("cst_rows", [P, D])
        a = Area(late)
        st_pool = a("st_pool", [P, KT, NB * POOL_BUF])
        st_conv = a("st_conv", [P, KT, NB * 2])
        row_out = a("row_out", [P, D])
        table_in = Area(work + 60 * 1024)("table_in", [P, C_N])
        a = Area(work + 48 * 1024)
        sq = a("sq", [P, 2, T])
        sq_sum = a("sq_sum", [P, T])
        h32 = a("h32", [P, 2, T])
        a = Area(work)
        y_hi = a("y_hi", [P, 2, T], F32R)
        y_lo = a("y_lo", [P, 2, T], F32R)
        after_y = a.at
        pw_raw = a("pw_raw", [P, 512])
        pw_hi = a("pw_hi", [P, 512], F32R)
        pw_lo = a("pw_lo", [P, 512], F32R)
        u_pad = a("u_pad", [P, 2, WARM + T])
        win_a = a("win_a", [P, WARM + T])
        win_b = a("win_b", [P, WARM + T])
        d_hi = a("d_hi", [P, 2, T], F32R)
        d_lo = a("d_lo", [P, 2, T], F32R)
        gate = a("gate", [P, 2, T])
        y32 = a("y32", [P, T])
        a = Area(after_y)
        c_sb = a("c_sb", [P, T])
        cv = a("cv", [P, 2, 2 + T])
        cc = a("cc", [P, T])
        c_gate = a("c_gate", [P, 2, T])
        cy32 = a("cy32", [P, 2, T])
        a = Area(after_y)
        q_hi = a("q_hi", [P, 2, T], F32R)
        q_lo = a("q_lo", [P, 2, T], F32R)
        kv_raw = a("kv_raw", [P, 2, 512])
        kv_hi = a("kv_hi", [P, 2, 512], F32R)
        kv_lo = a("kv_lo", [P, 2, 512], F32R)
        prob = a("prob", [P, 2, NM])
        pt_hi = a("pt_hi", [P, MT, 512], F32R)
        pt_lo = a("pt_lo", [P, MT, 512], F32R)
        cache = a("cache", [P, NB * MT, HD])
        q_bc = a("q_bc", [P, NB, HD])
        mx = a("mx", [P, 8])
        nmx = a("nmx", [P, 8])
        rsum = a("rsum", [P, 8])
        rinv = a("rinv", [P, 8])
        ss = a("ss", [P, MT, NB])
        sp = a("sp", [P, NM])
        spt = a("spt", [P, MT, NB])
        s4 = a("s4", [P, 4])
        a = Area(work)
        dt_all = a("dt_all", [P, 9, G * E])
        dta = a("dta", [P, 9, G * E])
        acs_n = a("acs_n", [P, TT, G * E])
        acs_e = a("acs_e", [P, TT, G * E])
        dta_hi = a("dta_hi", [P, TT, G * E], F32R)
        dta_lo = a("dta_lo", [P, TT, G * E], F32R)
        dtb = a("dtb", [P, 16, NB])
        dab = a("dab", [P, 16, NB])
        dsk = a("dsk", [P, 16])
        st_sc = a("st_sc", [P, 24, NB * 3])
        s_keep = a("s_keep", [P, 24, 11])
        g_dt = a("g_dt", [P, TT, E])
        g_acn = a("g_acn", [P, TT, E])
        g_ace = a("g_ace", [P, TT, E])
        g_dhi = a("g_dhi", [P, TT, E], F32R)
        g_dlo = a("g_dlo", [P, TT, E], F32R)
        g_dtb = a("g_dtb", [P, XT, NB])
        g_dab = a("g_dab", [P, XT, NB])
        g_prm = a("g_prm", [P, 56])
        g_st = a("g_st", [P, 6, NB * 3])
        bc = a("bc", [P, 2, T])
        xb_at = a.at
        xb = a("xb", [P, XT, T])
        zb_at = a.at
        zb = a("zb", [P, XT, T])
        after_z = a.at
        b2 = Area(xb_at)
        o_lo = b2("o_lo", [P, XT, T], F32R)
        b2 = Area(zb_at)
        o_hi = b2("o_hi", [P, XT, T], F32R)
        raw = a("raw", [P, 3 + T])
        t_sq = a("t_sq", [P, T])
        t_sum = a("t_sum", [P, T])
        b2 = Area(after_z + 32)
        dec = b2("dec", [P, E, P])
        xdt = b2("xdt", [P, 512])
        xde = b2("xde", [P, 512])
        b2 = Area(a.at - 4 * T)
        bx = b2("bx", [P, 2, XT, N])
        a = Area(max(a.at, b2.at))
        b_nat = a("b_nat", [P, P])
        y_nat = a("y_nat", [P, 512])
        S = a("S", [P, 512])
        s_out = y_nat
        aend = a("aend", [P, E])
        te = a("te", [P, E])
        toe = a("toe", [P, E])
        cdec = a("cdec", [P, E])
        st = a("st", [P, 2, 2, XT, N])
        bcs = a("bcs", [P, 2, 2, N])
        xd = a("xd", [P, XT, NB])
        yss = a("yss", [P, XT, NB])
        a = Area(xb_at)
        dw_raw = a("dw_raw", [P, KT, 32])
        dw_hi = a("dw_hi", [P, KT, 32], F32R)
        dw_lo = a("dw_lo", [P, KT, 32], F32R)
        dtx = a("dtx", [P, 9, 32])
        dte = a("dte", [P, 9, 32])
        dtl = a("dtl", [P, 9, 32])
        bias_bc = a("bias_bc", [P, 3, 32])
        sc_rows = a("sc_rows", [P, CONV_DIM])
        a = Area(work)
        y_out = a("y_out", [P, 2, D])

        acc = [ctx.enter_context(nc.psum_tensor(f"acc{i}", [P, NCH * 512], F32)) for i in range(2)]
        M0 = ctx.enter_context(nc.psum_tensor("M0", [P, 512], F32))
        M1 = ctx.enter_context(nc.psum_tensor("M1", [P, 512], F32))
        MS = [M0, M1]

        def a3(s):
            return acc[s][:, :].rearrange("p (n c) -> p n c", c=512)[:, :, 0:CH]

        def t3(ap):
            return ap.rearrange("p (n c) -> p n c", c=CH)

        ident_r, tri_r, mask_r = table[:, C_ID:C_ID + P], table[:, C_TRI:C_TRI + P], table[:, C_MASK:C_MASK + 512]
        ident, tri = ident_r.bitcast(F32), tri_r.bitcast(F32)
        one = cst[:, C_ONE - C_INV:C_ONE - C_INV + 1]

        w_loaded = [sem("w_loaded0"), sem("w_loaded1")]
        w_hi_done = sem("w_hi_done")
        w_split = [sem("w_split0"), sem("w_split1")]
        w_used = [sem("w_used0"), sem("w_used1")]
        result = sem("result")
        moved = [sem("moved0"), sem("moved1")]
        stored = sem("stored")
        a_ready = sem("a_ready")
        a_spread = sem("a_spread")
        acs_done = sem("acs_done")
        acs_e_ready = sem("acs_e_ready")
        aend_ready = sem("aend_ready")
        attended = sem("attended")
        bc_ready = sem("bc_ready")
        bc_spread = sem("bc_spread")
        bnat_ready = sem("bnat_ready")
        cb_done = sem("cb_done")
        cdec_ready = sem("cdec_ready")
        conved = sem("conved")
        cv_ready = sem("cv_ready")
        cy32_ready = sem("cy32_ready")
        d32_ready = sem("d32_ready")
        d_hi_ready = sem("d_hi_ready")
        d_ready = sem("d_ready")
        dab_ready = sem("dab_ready")
        dec_ready = sem("dec_ready")
        dhi_ready = sem("dhi_ready")
        dlo_ready = sem("dlo_ready")
        dp_loaded = sem("dp_loaded")
        dt_done = sem("dt_done")
        dt_step = sem("dt_step")
        dta_ready = sem("dta_ready")
        dtb_done = sem("dtb_done")
        dtx_ready = sem("dtx_ready")
        dve_step = sem("dve_step")
        dw_loaded = sem("dw_loaded")
        dw_split = sem("dw_split")
        exped = sem("exped")
        fin_ready = sem("fin_ready")
        g_ready = sem("g_ready")
        h32_ready = sem("h32_ready")
        hi_ready = sem("hi_ready")
        k_loaded = sem("k_loaded")
        kt_stored = [sem("kt_stored0"), sem("kt_stored1")]
        kv_loaded = sem("kv_loaded")
        kv_nat = sem("kv_nat")
        kv_split = sem("kv_split")
        kv_stored = [sem("kv_stored0"), sem("kv_stored1")]
        kv_turned = sem("kv_turned")
        lo_ready = sem("lo_ready")
        m_hi_ready = sem("m_hi_ready")
        mix_done = sem("mix_done")
        mixed_out = sem("mixed_out")
        mm_ready = sem("mm_ready")
        ms_ready = sem("ms_ready")
        ms_scaled = sem("ms_scaled")
        mx_ready = sem("mx_ready")
        nmx_ready = sem("nmx_ready")
        o_hi_ready = sem("o_hi_ready")
        o_ready = sem("o_ready")
        padded = sem("padded")
        prob_ready = sem("prob_ready")
        prob_turned = sem("prob_turned")
        pt_hi_ready = sem("pt_hi_ready")
        pt_ready = sem("pt_ready")
        pw_loaded = sem("pw_loaded")
        pw_split = sem("pw_split")
        pw_used = sem("pw_used")
        q_hi_ready = sem("q_hi_ready")
        qbc_done = sem("qbc_done")
        qbc_ready = sem("qbc_ready")
        rinv_ready = sem("rinv_ready")
        rstd_ready = sem("rstd_ready")
        s_decayed = sem("s_decayed")
        s_done = sem("s_done")
        s_exped = sem("s_exped")
        s_out_ready = sem("s_out_ready")
        s_ready = sem("s_ready")
        s_stored = sem("s_stored")
        s_turned = sem("s_turned")
        sc_loaded = sem("sc_loaded")
        scored = sem("scored")
        sd_ready = sem("sd_ready")
        smix_done = sem("smix_done")
        smx_ready = sem("smx_ready")
        snmx_ready = sem("snmx_ready")
        sp_ready = sem("sp_ready")
        sp_turned = sem("sp_turned")
        spt_ready = sem("spt_ready")
        sq_added = sem("sq_added")
        sq_ready = sem("sq_ready")
        srinv_ready = sem("srinv_ready")
        ss_ready = sem("ss_ready")
        ss_turned = sem("ss_turned")
        st_loaded = [sem("st_loaded0"), sem("st_loaded1")]
        st_new = sem("st_new")
        st_part = sem("st_part")
        st_read = sem("st_read")
        st_rows_in = sem("st_rows_in")
        st_stored = [sem("st_stored0"), sem("st_stored1")]
        sy_hi_ready = sem("sy_hi_ready")
        t_added = sem("t_added")
        t_sq_ready = sem("t_sq_ready")
        table_r = sem("table_r")
        tables = sem("tables")
        tapped = sem("tapped")
        te_ready = sem("te_ready")
        toe_ready = sem("toe_ready")
        v_loaded = sem("v_loaded")
        x_loaded = [sem("x_loaded0"), sem("x_loaded1")]
        x_turned = sem("x_turned")
        xd_ready = sem("xd_ready")
        xde_ready = sem("xde_ready")
        xdt_ready = sem("xdt_ready")
        xy_ready = sem("xy_ready")
        y_back = sem("y_back")
        y_hi_ready = sem("y_hi_ready")
        y_ready = sem("y_ready")
        y_ready2 = sem("y_ready2")
        y_stored = [sem("y_stored0"), sem("y_stored1")]
        y_turned = sem("y_turned")
        ydiag_done = sem("ydiag_done")
        yn_ready = sem("yn_ready")
        ynat_ready = sem("ynat_ready")
        yoff_done = sem("yoff_done")
        yz_ready = sem("yz_ready")
        zeroed = sem("zeroed")

        block = ctx.enter_context(nc.Block())

        @block.sync
        def _(sp):
            t = Tally()

            def load(src, kb):
                s, n = t.unit()
                if not isinstance(n, int) or n > 1:
                    sp.wait_ge(w_split[s], n - 1)
                sp.dma_start(w_raw[:, s].rearrange("p (k n) -> p k n", k=kb), src).then_inc(w_loaded[s], 16)

            def columns(w, at):
                load(w.rearrange("(k p) n -> p k n", p=P)[:, :, ds(at, P)], KT)

            def out_rows(w, chunk, kb):
                wide = 1024 // kb
                for i in range(D // wide):
                    load(w.rearrange("(k p) n -> p k n", p=P)[:, ds(chunk * kb, kb), i * wide:(i + 1) * wide], kb)

            sp.dma_start(table_in[:, :], ins["constants"]).then_inc(tables, 16)
            row = 0
            for src, n in ((ins["norm_mix"].rearrange("l (j p) -> (l j) p", p=P), 16),
                           (ins["norm_xa"].rearrange("l (j p) -> (l j) p", p=P), 16),
                           (ins["norm_final"].rearrange("(j p) -> j p", p=P), 8),
                           (ins["pool_scale"].rearrange("l (j p) -> (l j) p", p=P), 8),
                           (ins["conv_w"].rearrange("l k (j p) -> (l k j) p", p=P), 24),
                           (ins["ssm_conv_b"].rearrange("l (j p) -> (l j) p", p=P), 24),
                           (ins["ssm_norm"].rearrange("l (j p) -> (l j) p", p=P), 16)):
                sp.dma_start(p_in[row:row + n, 0, :], src).then_inc(tables, 16)
                row += n
            sp.dma_start(p_in[0:96, 1, :], ins["ssm_conv_w"].rearrange("l k (j p) -> (l k j) p", p=P)).then_inc(tables, 16)
            for i in range(MT):
                sp.dma_start(x_in[:, i, :], ins["mem_prompt"][0, i * P:(i + 1) * P, :]).then_inc(x_loaded[i], 16)
            with sp.Fori(0, TT // 2) as m:
                for i in range(2):
                    sp.wait_ge(result, 2 * m + i + 2)
                    sp.dma_start(x_in[:, i, :], ins["x_prompt"][0].rearrange("(a p) d -> a p d", p=P)[ds(2 * m + i, 1)]
                                 .rearrange("a p d -> (a p) d")).then_inc(x_loaded[i], 16)
            sp.wait_ge(result, TT + 2)
            sp.dma_start(x_in[0:NB, 0, :], ins["x_sample"].rearrange("b s d -> (b s) d")).then_inc(x_loaded[0], 16)
            for l in range(2):
                for w in (ins["w_xa_k"], ins["w_xa_v"]):
                    if l == 0 and w is ins["w_xa_k"]:
                        columns(w[0], 0)
                        columns(w[0], P)
                        with t.loop(sp, 1, 4, 2, (1, 1)) as i:
                            for s in range(2):
                                columns(w[0], (2 * i + s) * P)
                    else:
                        with t.loop(sp, 0, 4, 2, (1, 1)) as i:
                            for s in range(2):
                                columns(w[l], (2 * i + s) * P)

            def cross(l):
                wq, wo = ins["w_xa_q"][l], ins["w_xa_o"][l]
                columns(wq, 0)
                columns(wq, P)
                with t.loop(sp, 1, HEADS, 4, (5, 5)) as h:
                    columns(wq, h * HD)
                    columns(wq, h * HD + P)
                    out_rows(wo, h - 1, 2)
                out_rows(wo, HEADS - 1, 2)

            we, wo = ins["w_in_even"][0], ins["w_out_even"][0]

            def pool_units(g, first):
                columns(we, g * 256)
                columns(we, g * 256 + P)
                if first:
                    sp.wait_ge(sq_ready, 1)
                else:
                    sp.wait_ge(pw_split, g)
                sp.dma_start(pw_raw[:, :].rearrange("p (k n) -> p k n", k=2),
                             ins["pool_w"][0].rearrange("g (k p) n -> p (g k) n", p=P)[:, ds(2 * g, 2), :]).then_inc(pw_loaded, 16)
                if not first:
                    out_rows(wo, g - 1, 2)
                columns(we, D + g * 256)
                columns(we, D + g * 256 + P)

            pool_units(0, True)
            with t.loop(sp, 1, 4, 6, (7, 7)) as g:
                pool_units(g, False)
            with t.loop(sp, 0, 4, 10, (8, 8)) as g:
                def conv_col(part, i):
                    columns(we, part * D + g * 256 + i * P)
                for part in (3, 4, 5):
                    conv_col(part, 0)
                out_rows(wo, g + 3, 2)
                conv_col(2, 0)
                for part in (3, 4, 5, 2):
                    conv_col(part, 1)
            out_rows(wo, 7, 2)
            cross(0)

            wi, wo = ins["w_in_odd"][0], ins["w_out_odd"][0]
            st_in = ins["state_ssm"][0].rearrange("b h p n -> b (h p) n").rearrange("b (a p) n -> b p a n", p=P)
            st_to = outs["ssm_sample"][0].rearrange("b h p n -> b (h p) n").rearrange("b (a p) n -> b p a n", p=P)

            def state_load(g, q):
                for b in range(2):
                    sp.dma_start(st[:, q % 2, b], st_in[2 * q + b, :, ds(XT * g, XT), :]).then_inc(st_loaded[q % 2], 16)

            def state_store(g, q):
                sp.wait_ge(st_new, NB // 2 * g + q + 1)
                for b in range(2):
                    sp.dma_start(st_to[2 * q + b, :, ds(XT * g, XT), :], st[:, q % 2, b]).then_inc(st_stored[q % 2], 16)

            def ssm_units(g, last):
                for i in range(XT):
                    columns(wi, D_INNER + g * 512 + i * P)
                for q in range(2):
                    sp.wait_ge(st_stored[q], 64 * g + 1)
                    sp.wait_ge(st_read, 4 * g + 1)
                    state_load(g, q)
                for i in range(2):
                    columns(wi, (g + 1) * 512 + (i * P - 512))
                for q in range(4):
                    state_store(g, q)
                    if q < 2:
                        sp.wait_ge(st_read, 4 * g + q + 2)
                        sp.wait_ge(st_stored[q % 2], (g + 1) * 64 - 31)
                        state_load(g, q + 2)
                        columns(wi, g * 512 + (q + 2) * P)
                    elif not last:
                        columns(wi, D_INNER + D_INNER + (q - 2) * 512 + (g + 1) * P)
                out_rows(wo, g, 4)

            columns(wi, 2 * D_INNER)
            columns(wi, 2 * D_INNER + 512)
            with t.loop(sp, 0, G - 1, 14, (11, 8)) as g:
                ssm_units(g, False)
            ssm_units(G - 1, True)
            cross(1)
            for i in range(TT + 1):
                rows = P if i < TT else NB
                sp.wait_ge(y_ready, i + 1)
                dst = outs["y_prompt"][0, i * P:(i + 1) * P, :] if i < TT else outs["y_sample"].rearrange("b s d -> (b s) d")
                sp.dma_start(dst, y_out[0:rows, i % 2, :]).then_inc(y_stored[i % 2], 16)
            for q in range(2):
                sp.wait_ge(y_stored[q], 16 * ((TT + 2 - q) // 2))
                sp.wait_ge(st_stored[q], 64 * G + 1)

        @block.gpsimd
        def _(pool):
            t = Tally()
            zcol = zero[:, 0:1]

            def split_to(raw_ap, hi, lo, width, done):
                pool.tensor_tensor(hi, raw_ap, zcol.to_broadcast([P, width]), ALU.add).then_inc(w_hi_done, 1)
                halves[0] += 1
                pool.wait_ge(w_hi_done, halves[0])
                pool.tensor_tensor(lo, raw_ap, hi.bitcast(F32), ALU.subtract).then_inc(done, 1)

            halves = [0]

            @contextmanager
            def loop(lo, hi, units, results, splits):
                was = halves[0]
                with t.loop(pool, lo, hi, units, results) as i:
                    halves[0] = was + (i - lo if lo else i) * splits
                    yield i
                halves[0] = was + (hi - lo) * splits

            def split(count=1):
                for _ in range(count):
                    s, n = t.unit()
                    pool.wait_ge(w_loaded[s], 16 * n)
                    pool.wait_ge(w_used[s], n)
                    split_to(w_raw[:, s, :], w_hi[:, s, :], w_lo[:, s, :], 1024, w_split[s])

            def cross(l):
                def memory(h):
                    pool.wait_ge(kv_loaded, 32 * (HEADS * l + h + 1))
                    pool.wait_ge(attended, HEADS * l + h + 1)
                    for i in range(2):
                        split_to(kv_raw[:, i, :], kv_hi[:, i, :], kv_lo[:, i, :], 512, kv_split)

                split(2)
                memory(0)
                with loop(1, HEADS, 4, (5, 5), 6) as h:
                    split(2)
                    memory(h)
                    split(2)
                split(2)

            pool.memset(zero[:, :], 0.0).then_inc(zeroed, 1)
            pool.wait_ge(zeroed, 1)
            with loop(0, 16, 2, (1, 1), 2) as _:
                split(2)

            def pool_group(g, first):
                split(2)
                pool.wait_ge(pw_loaded, 16 * (g + 1))
                pool.wait_ge(pw_used, g + 1)
                split_to(pw_raw[:, :], pw_hi[:, :], pw_lo[:, :], 512, pw_split)
                split(2 if first else 4)

            pool_group(0, True)
            with loop(1, 4, 6, (7, 7), 7) as g:
                pool_group(g, False)
            with loop(0, 4, 10, (8, 8), 10) as _:
                split(10)
            split(2)
            cross(0)

            pool.wait_ge(dw_loaded, 16)
            split_to(dw_raw[:, :, :].rearrange("p k n -> p (k n)"), dw_hi[:, :, :].rearrange("p k n -> p (k n)"),
                     dw_lo[:, :, :].rearrange("p k n -> p (k n)"), KT * 32, dw_split)
            split(2)

            def ssm_group(g, last):
                def chunk(c):
                    n = 8 * g + c + 1
                    pool.wait_ge(aend_ready, n)
                    pool.tensor_tensor(te[:, :], aend[:, :], g_acn[:, c, :], ALU.add).then_inc(te_ready, 1)
                    pool.wait_ge(cdec_ready, n)
                    pool.wait_ge(yoff_done, n)
                    pool.tensor_tensor(v8(S), v8(S), cdec[:, :].unsqueeze(2).to_broadcast([P, E, 64]), ALU.mult)\
                        .then_inc(s_decayed, 1)
                    pool.wait_ge(xdt_ready, n)
                    pool.wait_ge(toe_ready, n)
                    pool.tensor_tensor(v8(xde), v8(xdt), toe[:, :].unsqueeze(2).to_broadcast([P, E, 64]), ALU.mult)\
                        .then_inc(xde_ready, 1)

                def sample(q):
                    n = 4 * g + q + 1
                    b = q % 2
                    pool.wait_ge(st_loaded[b], 64 * g + 32 * (q // 2 + 1))
                    pool.wait_ge(g_ready, g + 1)
                    d = g_dab[:, :, 2 * q:2 * q + 2].rearrange("p a b -> p b a")
                    pool.tensor_tensor(st[:, b], st[:, b], d.unsqueeze(3).to_broadcast([P, 2, XT, N]), ALU.mult)\
                        .then_inc(st_part, 1)
                    pool.wait_ge(bc_ready, n)
                    pool.wait_ge(st_read, n)
                    pool.wait_ge(xd_ready, g + 1)
                    for i in range(2):
                        pool.tensor_tensor(bx[:, i], bcs[:, 0, i, :].unsqueeze(1).to_broadcast([P, XT, N]),
                                           xd[:, :, 2 * q + i].unsqueeze(2).to_broadcast([P, XT, N]), ALU.mult)\
                            .then_inc(st_part, 1)
                    pool.wait_ge(st_part, 3 * n)
                    pool.tensor_tensor(st[:, b], st[:, b], bx[:, :], ALU.add).then_inc(st_new, 1)

                split(5)
                for c in range(TT):
                    chunk(c)
                    if c % 2 == 1:
                        sample(c // 2)
                    if c in (0, 2, 4):
                        split()
                if not last:
                    split(2)
                split(4)

            def v8(b):
                return b[:, :].rearrange("p (e c) -> p e c", e=E)

            with loop(0, G - 1, 14, (11, 8), 14) as g:
                ssm_group(g, False)
            ssm_group(G - 1, True)
            cross(1)

        @block.tensor
        def _(pe):
            t = Tally()
            ALL = ds(0, T)

            def three(w_h, w_l, m_h, m_l):
                return ((w_h, m_h), (w_h, m_l), (w_l, m_h))

            def take(extra=None):
                s, n = t.unit()
                pe.wait_ge(w_split[s], n)
                marks = [w_used[1 - s]] + ([extra] if extra is not None else [])
                return s, marks

            def begin(a):
                a, r, k = t.next(a)
                pe.wait_ge(moved[a], k)
                return a

            def mark(ins, marks):
                if marks:
                    ins.then_inc(marks.pop(0), 1)

            def project(a, extra=None, wait_k=None):
                s, marks = take(extra)
                begin(a)
                project_part(a, s, marks, range(KT), wait_k)

            def project_part(a, s, marks, ks, wait_k=None):
                for k in ks:
                    if wait_k is not None:
                        pe.wait_ge(lo_ready, wait_k + k + 1)
                    w = slice(k * P, (k + 1) * P)
                    for j, (wt, mv) in enumerate(three(w_hi, w_lo, h_hi, h_lo)):
                        for n in range(NCH):
                            ins = pe.matmul(acc[a][:, n * 512:n * 512 + CH], wt[:, s, w], mv[:, k, n * CH:(n + 1) * CH],
                                            start=(k == 0 and j == 0), stop=(k == KT - 1 and j == 2))
                            if k == KT - 1 and j == 2 and n == NCH - 1:
                                ins.then_inc(result, 1)
                            else:
                                mark(ins, marks)

            def out_project(kb, hi, lo, first=None, sets=(0, 1)):
                wide = 1024 // kb
                if first is not None:
                    pe.wait_ge(*first)
                m = 0
                for i in range(D // wide):
                    s, marks = take()
                    for j in range(wide // P):
                        a = begin(sets[m % 2])
                        m += 1
                        for k in range(kb):
                            at = k * wide + j * P
                            for q, (wt, mv) in enumerate(three(w_hi, w_lo, hi, lo)):
                                for n in range(NCH):
                                    ins = pe.matmul(acc[a][:, n * 512:n * 512 + CH], wt[:, s, at:at + P],
                                                    mv[:, k, n * CH:(n + 1) * CH],
                                                    start=(k == 0 and q == 0), stop=(k == kb - 1 and q == 2))
                                    if k == kb - 1 and q == 2 and n == NCH - 1:
                                        ins.then_inc(result, 1)
                                    else:
                                        mark(ins, marks)

            def all_moved(a):
                pe.wait_ge(moved[a], t.taken[a] + 1)

            def norm_sums(n_th, src, into):
                for i in range(TT + 1):
                    rows = P if i < TT else NB
                    ins = pe.matmul(into[0:rows, i:i + 1], src[:, i * P:i * P + rows], one, start=True, stop=True)
                ins.then_inc(ms_ready, 1)

            def norm_spread(n_th, a):
                a = begin(a)
                pe.wait_ge(rstd_ready, n_th)
                for i in range(TT + 1):
                    rows = P if i < TT else NB
                    ins = pe.matmul(acc[a][:, i * P:i * P + rows], rstd[0:rows, i:i + 1].to_broadcast([rows, P]),
                                    ident[0:rows, 0:rows], start=True, stop=True)
                ins.then_inc(result, 1)

            def norm(n_th, adds):
                pe.wait_ge(sq_added, adds)
                norm_sums(n_th, sq_sum, M0)
                norm_spread(n_th, 0)

            pe.wait_ge(tables, 16 * 9)
            pe.wait_ge(table_r, 2)
            begin(0)
            pe.transpose(acc[0][:, 0:112], p_in[0:112, 0, :], ident[0:112, 0:112]).then_inc(w_used[0], 1)
            pe.transpose(acc[0][:, 112:208], p_in[0:96, 1, :], ident[0:96, 0:96]).then_inc(result, 1)

            def rows_in(i, n, rows, a):
                pe.wait_ge(x_loaded[i], 16 * n)
                begin(a)
                for k in range(KT):
                    ins = pe.transpose(acc[a][:, k * P:k * P + rows], x_in[0:rows, i, k * P:(k + 1) * P], ident[0:rows, 0:rows])
                ins.then_inc(result, 1)

            rows_in(0, 1, P, 1)
            rows_in(1, 1, P, 0)
            with t.loop(pe, 0, TT // 2, 0, (1, 1)) as m:
                rows_in(0, m + 2, P, 1)
                rows_in(1, m + 2, P, 0)
            rows_in(0, TT // 2 + 2, NB, 1)

            def state_rows(src, rows, lo, a):
                begin(a)
                for i in range(lo, lo + 8):
                    ins = pe.transpose(acc[a][:, (i - lo) * P:(i - lo) * P + rows], src[0:rows, i * P:(i + 1) * P],
                                       ident[0:rows, 0:rows])
                ins.then_inc(result, 1)

            pe.wait_ge(st_rows_in, 32)
            state_rows(st_rows, NB * POOL_BUF, 0, 0)
            state_rows(cst_rows, NB * 2, 0, 1)

            all_moved(0)
            all_moved(1)

            def memory_tile(a):
                s, marks = take()
                begin(a)
                for k in range(KT):
                    w = slice(k * P, (k + 1) * P)
                    for j, (wt, mv) in enumerate(three(w_hi, w_lo, m_hi, m_lo)):
                        ins = pe.matmul(acc[a][:, 0:NM], wt[:, s, w], mv[:, k, :],
                                        start=(k == 0 and j == 0), stop=(k == KT - 1 and j == 2))
                        mark(ins, marks)
                ins.then_inc(result, 1)

            def memory_rows(s, n):
                all_moved(s)
                pe.wait_ge(kv_nat, n)
                for i in range(MT):
                    ins = pe.transpose(MS[s][:, i * P:(i + 1) * P], kt_out[:, s, i * P:(i + 1) * P], ident)
                ins.then_inc(kv_turned, 1)

            memory_tile(0)
            memory_tile(1)
            memory_rows(0, 1)
            with t.loop(pe, 1, 16, 2, (1, 1)) as i:
                memory_tile(0)
                memory_rows(1, 2 * i - 1)
                memory_tile(1)
                memory_rows(0, 2 * i)
            memory_rows(1, 31)

            norm(1, 7)

            def pool_products(g):
                for i in range(2):
                    a = begin(i)
                    if i == 0:
                        pe.wait_ge(pw_split, g + 1)
                        pe.wait_ge(d_ready, 2 * g + 2)
                    for k in range(2):
                        at = k * 256 + i * P
                        for j, (wt, mv) in enumerate(three(pw_hi, pw_lo, d_hi, d_lo)):
                            for n in range(NCH):
                                ins = pe.matmul(acc[a][:, n * 512:n * 512 + CH], wt[:, at:at + P],
                                                mv[:, k, n * CH:(n + 1) * CH],
                                                start=(k == 0 and j == 0), stop=(k == 1 and j == 2))
                    ins.then_inc(result, 1)

            project(0, pw_used, 0)
            project(1)
            project(0)
            project(1)
            pool_products(0)
            with t.loop(pe, 1, 4, 6, (7, 7)) as g:
                project(0, pw_used)
                project(1)
                out_project(2, y_hi, y_lo, (y_ready2, 2 * g))
                project(0)
                project(1)
                pool_products(g)
            with t.loop(pe, 0, 4, 10, (8, 8)) as g:
                project(0)
                project(1)
                project(0)
                out_project(2, y_hi, y_lo, (y_ready2, 2 * g + 8), (1, 0))
                for a in (1, 0, 1, 0, 1):
                    project(a)
            out_project(2, y_hi, y_lo, (y_ready2, 16))

            def rows_out(src, width, lo):
                begin(1)
                for i in range(lo, lo + 8):
                    ins = pe.transpose(acc[1][0:width, (i - lo) * P:(i - lo + 1) * P], src[:, i, :], ident)
                ins.then_inc(result, 1)

            def attention(l, h):
                n = HEADS * l + h
                pe.wait_ge(kv_split, 2 * n + 2)
                all_moved(0)
                all_moved(1)
                score = [acc[0][:, 0:NM], acc[0][:, 512:512 + NM]]
                turned = [acc[1][:, 0:NM], acc[1][:, 512:512 + NM]]
                mixed = [acc[0][:, 1024:1536], acc[1][:, 1024:1536]]

                def scores(i):
                    if i >= 2:
                        pe.wait_ge(exped, 8 * n + i - 1)
                    for k in range(2):
                        for j, (a, b) in enumerate(three(q_hi, q_lo, kv_hi, kv_lo)):
                            ins = pe.matmul(score[i % 2], a[:, k, i * P:(i + 1) * P], b[:, 0, k * NM:(k + 1) * NM],
                                            start=(k == 0 and j == 0), stop=(k == 1 and j == 2))
                    ins.then_inc(scored, 1)

                def turn(i):
                    pe.wait_ge(prob_ready, 8 * n + i + 1)
                    if i >= 2:
                        pe.wait_ge(pt_ready, 8 * n + i - 1)
                    for j in range(MT):
                        ins = pe.transpose(turned[i % 2][:, j * P:(j + 1) * P], prob[:, i % 2, j * P:(j + 1) * P], ident)
                    ins.then_inc(prob_turned, 1)

                def mix(half):
                    pe.wait_ge(pt_ready, 8 * n + 4 * half + 4)
                    for k in range(2):
                        if half:
                            pe.wait_ge(mixed_out, 4 * n + k + 1)
                        for m in range(MT):
                            for j, (a, b) in enumerate(three(kv_hi, kv_lo, pt_hi, pt_lo)):
                                at = m * HD + k * P
                                ins = pe.matmul(mixed[k], a[:, 1, at:at + P], b[:, m, :],
                                                start=(m == 0 and j == 0), stop=(m == 1 and j == 2))
                        ins.then_inc(mix_done, 1)

                for r in range(4):
                    if r >= 2:
                        pe.wait_ge(qbc_ready, 4 * n + r - 1)
                    for b in range(2):
                        for k in range(2):
                            at = b * HD + k * P
                            for j, src in enumerate((q_hi, q_lo)):
                                ins = pe.matmul(MS[r % 2][:, at:at + P],
                                                src[:, k, TP + 2 * r + b:TP + 2 * r + b + 1].to_broadcast([P, P]), ident_r,
                                                start=(j == 0), stop=(j == 1))
                    ins.then_inc(qbc_done, 1)
                for i in range(TT + 2):
                    if i < TT:
                        scores(i)
                    if i >= 2:
                        turn(i - 2)
                    if i == 5:
                        mix(0)
                mix(1)
                pe.wait_ge(mixed_out, 4 * n + 4)

            def sample_turn(n):
                pe.wait_ge(ss_ready, n + 1)
                for m in range(MT):
                    ins = pe.transpose(M0[0:NB, m * P:(m + 1) * P], ss[:, m, :], ident)
                ins.then_inc(ss_turned, 1)

            def sample_mix(n):
                pe.wait_ge(sp_ready, n + 1)
                for m in range(MT):
                    ins = pe.matmul(M1[:, m * NB:(m + 1) * NB], sp[0:NB, m * P:(m + 1) * P], ident[0:NB, 0:NB],
                                    start=True, stop=True)
                ins.then_inc(sp_turned, 1)
                pe.wait_ge(spt_ready, n + 1)
                pe.wait_ge(v_loaded, 16 * n + 16)
                for k in range(2):
                    for b in range(NB):
                        for m in range(MT):
                            ins = pe.matmul(M0[:, k * NB + b:k * NB + b + 1], cache[:, b * MT + m, k * P:(k + 1) * P],
                                            spt[:, m, b:b + 1], start=(m == 0), stop=(m == 1))
                ins.then_inc(smix_done, 1)

            def cross(l, norm_no, adds, tiles):
                norm(norm_no, adds)
                project(0, attended, tiles)
                project(1)
                attention(l, 0)
                with t.loop(pe, 1, HEADS, 4, (5, 5)) as h:
                    n = HEADS * l + h - 1
                    project(0, attended)
                    sample_turn(n)
                    project(1)
                    sample_mix(n)
                    out_project(2, y_hi, y_lo, (xy_ready, n + 1))
                    attention(l, h)
                n = HEADS * l + HEADS - 1
                sample_turn(n)
                sample_mix(n)
                out_project(2, y_hi, y_lo, (xy_ready, n + 1))

            rows_out(u_keep, 23, 0)
            rows_out(c_keep, 10, 0)
            cross(0, 2, 14, 8)

            norm(3, 21)
            pe.wait_ge(lo_ready, 24)
            pe.wait_ge(dw_split, 1)
            pe.wait_ge(padded, 2)
            for i in range(TT + 1):
                for k in range(KT):
                    at = k * T + i * P
                    for j, (a, b) in enumerate(three(h_hi_f, h_lo_f, dw_hi, dw_lo)):
                        ins = pe.matmul(M0[:, i * 32:(i + 1) * 32], a[:, at:at + P], b[:, k, :],
                                        start=(k == 0 and j == 0), stop=(k == KT - 1 and j == 2))
            ins.then_inc(dt_done, 1)
            pe.wait_ge(sc_loaded, 16)
            for i in range(2):
                state_rows(sc_rows, 24, 8 * i, i % 2)
            pe.wait_ge(dta_ready, 1)
            pe.matmul(M1[:, 0:256], tri, dta[:, 0:TT, :].rearrange("p c h -> p (c h)"), start=True, stop=True).then_inc(acs_done, 1)
            for j, src in enumerate((dt_all, dta)):
                for i in range(16):
                    at = j * P + i * NB
                    for half in range(2):
                        head = 2 * i + half
                        ins = pe.matmul(M0[64 * half:64 * half + 64, at:at + NB],
                                        src[0:NB, TT, head:head + 1].to_broadcast([NB, 64]),
                                        ident[0:NB, 0:NB], start=True, stop=True)
            ins.then_inc(dtb_done, 1)
            state_rows(sc_rows, 24, 16, 0)
            project(1)
            project(0)

            def ssm_group(g, last):
                def first_stage(c):
                    n = 8 * g + c
                    cs = slice(c * P, (c + 1) * P)
                    if c == 0:
                        pe.wait_ge(conved, 6 * g + 6)
                        pe.wait_ge(g_ready, g + 1)
                        all_moved(1)
                    else:
                        pe.wait_ge(y_back, n)
                        if c % 2 == 0:
                            pe.wait_ge(bc_ready, 4 * g + c // 2)
                    for i in range(XT):
                        ins = pe.transpose(M0[:, i * P:(i + 1) * P], xb[:, i, cs], ident)
                    ins.then_inc(x_turned, 1)
                    if c:
                        pe.wait_ge(mm_ready, n)
                    pe.matmul(M1[:, 0:P], bc[:, 0, cs], bc[:, 1, cs], start=True, stop=True)
                    pe.transpose(M1[:, P:2 * P], bc[:, 0, cs], ident).then_inc(cb_done, 1)
                    if c:
                        pe.wait_ge(s_ready, 9 * g + c + 1)
                    for q in range(2):
                        pe.matmul(acc[1][:, q * 512:(q + 1) * 512], ident_r, mask_r, start=True, stop=False,
                                  skip_group_check=True)
                        for e in range(4 * q, 4 * q + 4):
                            for j, src in enumerate((g_dhi, g_dlo)):
                                ins = pe.matmul(acc[1][:, e * P:(e + 1) * P], src[:, c, e:e + 1].to_broadcast([P, P]), tri_r,
                                                start=False, stop=(e % 4 == 3 and j == 1), skip_group_check=True)
                    ins.then_inc(a_spread, 1)
                    pe.wait_ge(s_ready, 9 * g + c + 1)
                    pe.matmul(acc[1][:, 1024:1536], bc[:, 1, cs], S[:, :], start=True, stop=True).then_inc(yoff_done, 1)

                def second_stage(c):
                    n = 8 * g + c + 1
                    pe.wait_ge(mm_ready, n)
                    pe.wait_ge(xdt_ready, n)
                    for e in range(E):
                        ins = pe.matmul(acc[1][:, e * 64:(e + 1) * 64], dec[:, e, :], xdt[:, e * 64:(e + 1) * 64],
                                        start=True, stop=True)
                    ins.then_inc(ydiag_done, 1)
                    pe.wait_ge(xde_ready, n)
                    pe.wait_ge(bnat_ready, n)
                    pe.matmul(acc[1][:, 512:1024], b_nat[:, :], xde[:, :], start=True, stop=True).then_inc(s_done, 1)

                def third_stage(c):
                    n = 8 * g + c + 1
                    pe.wait_ge(ynat_ready, n)
                    for i in range(XT):
                        ins = pe.transpose(M0[:, i * P:(i + 1) * P], y_nat[:, i * P:(i + 1) * P], ident)
                    ins.then_inc(y_turned, 1)

                def sample_spread(q):
                    pe.wait_ge(y_back, 8 * g + 2 * q + 2)
                    for j in range(2):
                        for b in range(2):
                            at = (2 * j + b) * P
                            ins = pe.matmul(M0[:, at:at + P], bc[:, j, TP + 2 * q + b:TP + 2 * q + b + 1].to_broadcast([P, P]),
                                            ident, start=True, stop=True)
                    ins.then_inc(bc_spread, 1)

                for a in (0, 1, 0, 1):
                    project(a)
                for c in range(TT):
                    first_stage(c)
                    if c % 2 == 0:
                        s, marks = take()
                        begin(0)
                    project_part(0, s, marks, range(0, 2) if c % 2 == 0 else range(4, 6))
                    second_stage(c)
                    project_part(0, s, marks, range(2, 4) if c % 2 == 0 else range(6, 8))
                    third_stage(c)
                    if c % 2:
                        sample_spread(c // 2)
                pe.wait_ge(s_ready, 9 * g + 9)
                pe.wait_ge(bc_ready, 4 * g + 4)
                for i in range(XT):
                    ins = pe.transpose(M0[:, i * P:(i + 1) * P], S[:, i * P:(i + 1) * P], ident)
                ins.then_inc(s_turned, 1)
                if not last:
                    pe.wait_ge(ynat_ready, 8 * g + 8)
                    project(1)
                pe.wait_ge(t_added, XT * g + XT)
                pe.wait_ge(s_out_ready, g + 1)
                norm_sums(0, t_sum, M1)
                if not last:
                    project(0)
                norm_spread(g + 4, 1)
                out_project(4, o_hi, o_lo, (o_ready, XT * g + XT))

            with t.loop(pe, 0, G - 1, 14, (11, 8)) as g:
                ssm_group(g, False)
            ssm_group(G - 1, True)
            for i in range(3):
                rows_out(s_keep, 11, 8 * i)
            cross(1, 8, 28, 24)
            norm(9, 35)
            for i in range(TT + 1):
                rows = P if i < TT else NB
                if i < 2:
                    a = begin(i % 2 ^ 1)
                    pe.wait_ge(fin_ready, KT)
                else:
                    a, _, _ = t.next(i % 2 ^ 1)
                    pe.wait_ge(y_ready, i - 1)
                for k in range(KT):
                    ins = pe.transpose(acc[a][0:rows, k * P:(k + 1) * P], x[:, k, i * P:i * P + rows], ident)
                ins.then_inc(result, 1)

        @block.scalar
        def _(act):
            t = Tally()

            def copy(out, in_, done):
                return act.activation(out, in_, ACT.Copy).then_inc(done, 1)

            act.dma_start(st_rows[0:NB * POOL_BUF, :], ins["state_pool"][0].rearrange("b t c -> (b t) c")).then_inc(st_rows_in, 16)
            act.dma_start(cst_rows[0:NB * 2, :], ins["state_conv"][0].rearrange("b t c -> (b t) c")).then_inc(st_rows_in, 16)
            act.dma_start(outs["pool_sample"][0, :, 0:POOL_BUF - 1, :], ins["state_pool"][0, :, 1:POOL_BUF, :]).then_inc(stored, 16)
            act.dma_start(outs["conv_sample"][0, :, 0:1, :], ins["state_conv"][0, :, 1:2, :]).then_inc(stored, 16)
            act.dma_start(outs["ssm_conv_sample"][0, :, 0:2, :], ins["state_ssm_conv"][0, :, 1:3, :]).then_inc(stored, 16)
            act.wait_ge(tables, 16 * 9)
            copy(table[:, :], table_in[:, 0:C_INV], table_r)
            copy(cst[:, :], table_in[:, C_INV:C_N], table_r)
            t.next(0)

            for i in range(MT):
                a, r, _ = t.next((i + 1) % 2)
                act.wait_ge(result, r)
                copy(m_hi[:, :, i * P:(i + 1) * P], acc[a][:, 0:1024].rearrange("p (k m) -> p k m", k=KT), m_hi_ready)
            for i in range(TT + 1):
                t.next((i + 1) % 2)
            t.next(0)
            t.next(1)

            def memory_pair(row, i, first, keys):
                for s in range(2):
                    a, r, _ = t.next(s)
                    act.wait_ge(result, r)
                    if not first:
                        act.wait_ge(kt_stored[s], row)
                    copy(kt_out[:, s, :], acc[a][:, 0:NM], moved[a])
                    if keys is not None:
                        act.wait_ge(moved[a], t.taken[a] + 1)
                        act.dma_start(keys[ds(2 * i + s, 1)].rearrange("a p m -> (a p) m"), kt_out[:, s, :]).then_inc(kt_stored[s], 16)

            for l in range(2):
                keys = scratch[l].rearrange("(j p) m -> j p m", p=P)
                if l == 0:
                    memory_pair(0, 0, True, keys)
                with t.loop(act, 1 - l, 4, 2, (1, 1)) as i:
                    memory_pair(64 * l + 16 * i if l == 0 else 64 + 16 * i, i, False, keys)
                with t.loop(act, 0, 4, 2, (1, 1)) as i:
                    memory_pair(64 * (l + 1), i, False, None)
                for j, name in enumerate(("mem_k", "mem_v")):
                    act.wait_ge(kv_nat, 16 * l + 8 * j + 9)
                    act.dma_start(outs[name][l, 0].rearrange("(m p) h d -> p m (h d)", p=P), kv_nat_sb[:, j]).then_inc(kv_stored[j], 16)

            def square_tiles(n_th, waits):
                for j in range(KT):
                    if waits:
                        act.wait_ge(*waits[j])
                    if j >= 2:
                        act.wait_ge(sq_added, 7 * (n_th - 1) + j - 1)
                    act.activation(sq[:, j % 2, :], x[:, j, :], ACT.Square).then_inc(sq_ready, 1)

            def root(n_all):
                act.wait_ge(ms_scaled, n_all)
                act.activation(sd[:, :], ms[:, :], ACT.Sqrt).then_inc(sd_ready, 1)

            def norm(n_th, n_all, waits, split=True):
                square_tiles(n_th, waits)
                root(n_all)
                t.next(0)
                if split:
                    for j in range(KT):
                        act.wait_ge(h32_ready, 8 * (n_th - 1) + j + 1)
                        copy(h_hi[:, j, :], h32[:, j % 2, :], hi_ready)

            def out_chunk():
                for m in range(KT):
                    t.next(m % 2)

            def x_tiles():
                base = [t.taken[0] - 4, t.taken[1] - 4]
                return [(moved[j % 2], base[j % 2] + j // 2 + 2) for j in range(KT)]

            for s in range(2):
                act.wait_ge(kt_stored[s], 128)
                act.wait_ge(kv_stored[s], 32)
            act.wait_ge(moved[0], t.taken[0] + 1)
            act.wait_ge(moved[1], t.taken[1] + 1)
            norm(1, 1, None)

            def pool_group(g, first):
                for i in range(2):
                    a, r, _ = t.next(i)
                    act.wait_ge(result, r)
                    if not first:
                        act.wait_ge(d_ready, 2 * g)
                    copy(t3(u_pad[:, i, WARM:WARM + T]), a3(a), moved[a])
                for i in range(2):
                    act.wait_ge(d32_ready, 2 * g + i + 1)
                    copy(d_hi[:, i, :], y32[:, :], d_hi_ready)
                if not first:
                    out_chunk()
                for i in range(2):
                    a, r, _ = t.next(i)
                    act.wait_ge(result, r)
                    act.activation(t3(gate[:, i, :]), a3(a), ACT.Silu).then_inc(moved[a], 1)
                for i in range(2):
                    t.next(i)
                    act.wait_ge(moved[i], t.taken[i] + 1)
                    copy(y_hi[:, i, :], y32[:, :], y_hi_ready)

            pool_group(0, True)
            with t.loop(act, 1, 4, 6, (7, 7)) as g:
                pool_group(g, False)

            def conv_pair(g):
                for i in range(2):
                    a, r, _ = t.next(0)
                    act.wait_ge(result, r)
                    act.wait_ge(cv_ready, 2 * g + i + 1)
                    copy(t3(c_sb[:, :]), a3(a), moved[a])
                    t.next(1)
                    a, r, _ = t.next(0)
                    act.wait_ge(result, r)
                    act.activation(t3(c_gate[:, i, :]), a3(a), ACT.Silu).then_inc(moved[a], 1)
                    if i == 0:
                        for m in range(KT):
                            t.next((m + 1) % 2)
                    t.next(1)
                    act.wait_ge(cy32_ready, 2 * g + i + 1)
                    copy(y_hi[:, i, :], cy32[:, i, :], y_hi_ready)

            act.wait_ge(y_ready2, 8)
            with t.loop(act, 0, 4, 10, (8, 8)) as g:
                conv_pair(g)
            out_chunk()
            waits = x_tiles()
            def rows_from(a_width, dsts, n):
                a, r, _ = t.next(1)
                act.wait_ge(result, r)
                if n:
                    act.wait_ge(stored, 16 * (3 + 2 * n))
                copy(row_out[0:a_width, :], acc[a][0:a_width, 0:D], moved[a])
                act.wait_ge(moved[a], t.taken[a] + 1)
                for dst, lo, hi in dsts:
                    act.dma_start(dst, row_out[lo:hi, :]).then_inc(stored, 16)

            rows_from(23, ((outs["pool_prompt"][0, 0], 0, 15), (outs["pool_sample"][0, :, 14, :], 15, 23)), 0)
            rows_from(10, ((outs["conv_prompt"][0, 0], 0, 2), (outs["conv_sample"][0, :, 1, :], 2, 10)), 1)

            def cross(l, n_th, n_all, waits):
                act.wait_ge(stored, 16 * (7 if l == 0 else 13))
                norm(n_th, n_all, waits)
                kt = scratch[l].rearrange("(a p) m -> p a m", p=P)
                vn = outs["mem_v"][l, 0].rearrange("(a p) h d -> p a h d", p=P)
                ck = ins["cache_mem_k"][l].rearrange("b (m p) h d -> p (b m) h d", p=P)
                cv_ = ins["cache_mem_v"][l].rearrange("b (m p) h d -> p (b m) h d", p=P)

                def load_memory(h):
                    act.dma_start(kv_raw[:, 0, :].rearrange("p (a m) -> p a m", a=2), kt[:, ds(2 * h, 2), :]).then_inc(kv_loaded, 16)
                    act.dma_start(kv_raw[:, 1, :].rearrange("p (a d) -> p a d", a=2),
                                  vn[:, :, ds(h, 1), :].rearrange("p a h d -> p a (h d)")).then_inc(kv_loaded, 16)

                def load_cache(src, h, done):
                    act.dma_start(cache[:, :, :], src[:, :, ds(h, 1), :].rearrange("p b h d -> p b (h d)")).then_inc(done, 16)

                def queries(h, before):
                    for i in range(2):
                        a, r, _ = t.next(i)
                        act.wait_ge(result, r)
                        copy(t3(q_hi[:, i, :]), a3(a), q_hi_ready)
                        before(i)

                def attention(h):
                    n = HEADS * l + h
                    for r in range(4):
                        act.wait_ge(qbc_done, 4 * n + r + 1)
                        copy(q_bc[:, 2 * r:2 * r + 2, :], MS[r % 2][:, :].rearrange("p (b d) -> p b d", b=2), qbc_ready)

                    def mix_out(half):
                        for k in range(2):
                            act.wait_ge(mix_done, 4 * n + 2 * half + k + 1)
                            copy(y_hi[:, k, half * 512:half * 512 + 512],
                                 (acc[0] if k == 0 else acc[1])[:, 1024:1536], y_hi_ready)

                    for i in range(TT + 2):
                        if i < TT:
                            if i >= 2:
                                act.wait_ge(prob_turned, 8 * n + i - 1)
                            act.wait_ge(nmx_ready, 8 * n + i + 1)
                            act.activation(prob[:, i % 2, :], acc[0][:, (i % 2) * 512:(i % 2) * 512 + NM], ACT.Exp,
                                           bias=nmx[:, i:i + 1], scale=HD ** -0.5, accum_out=rsum[:, i:i + 1]).then_inc(exped, 1)
                        if i >= 2:
                            j = i - 2
                            act.wait_ge(prob_turned, 8 * n + j + 1)
                            if j >= 4:
                                act.wait_ge(mix_done, 4 * n + 2)
                            copy(pt_hi[:, :, (j % 4) * P:(j % 4 + 1) * P],
                                 acc[1][:, (j % 2) * 512:(j % 2) * 512 + NM].rearrange("p (m t) -> p m t", m=2), pt_hi_ready)
                        if i == 7:
                            mix_out(0)
                    mix_out(1)

                def sample_exp(n):
                    act.wait_ge(snmx_ready, n + 1)
                    act.activation(sp[0:NB, :], M0[0:NB, 0:NM], ACT.Exp, bias=s4[0:NB, 1:2], scale=HD ** -0.5,
                                   accum_out=s4[0:NB, 2:3]).then_inc(s_exped, 1)

                def sample_out(n):
                    act.wait_ge(smix_done, n + 1)
                    copy(y_hi[:, :, TP:T], M0[:, 0:2 * NB].rearrange("p (k b) -> p k b", k=2), sy_hi_ready)

                load_memory(0)
                act.wait_ge(lo_ready, 8 * n_th)
                load_cache(ck, 0, k_loaded)
                queries(0, lambda i: None)
                attention(0)
                with t.loop(act, 1, HEADS, 4, (5, 5)) as h:
                    n = HEADS * l + h - 1
                    act.wait_ge(kv_split, 2 * n + 2)
                    load_memory(h)
                    act.wait_ge(ss_ready, n + 1)
                    load_cache(cv_, h - 1, v_loaded)
                    queries(h, lambda i: sample_exp(n) if i == 0 else None)
                    sample_out(n)
                    load_cache(ck, h, k_loaded)
                    out_chunk()
                    attention(h)
                n = HEADS * l + HEADS - 1
                act.wait_ge(ss_ready, n + 1)
                load_cache(cv_, HEADS - 1, v_loaded)
                sample_exp(n)
                sample_out(n)
                out_chunk()

            cross(0, 2, 2, waits)

            waits = x_tiles()
            act.dma_start(dw_raw[:, :, :], ins["w_in_odd"][0].rearrange("(k p) n -> p k n", p=P)[:, :, 5120:5152]).then_inc(dw_loaded, 16)
            act.dma_start(bias_bc[:, 0, :], ins["dt_bias"].partition_broadcast(P).rearrange("p a h -> p (a h)")).then_inc(dp_loaded, 16)
            act.dma_start(bias_bc[:, 1, :], ins["a_log"].partition_broadcast(P).rearrange("p a h -> p (a h)")).then_inc(dp_loaded, 16)
            act.dma_start(sc_rows[0:24, :], ins["state_ssm_conv"][0].rearrange("b t c -> (b t) c")).then_inc(sc_loaded, 16)
            act.dma_start(bias_bc[:, 2, :], ins["d_skip"].partition_broadcast(P).rearrange("p a h -> p (a h)")).then_inc(dp_loaded, 16)
            norm(3, 3, waits)
            act.wait_ge(dp_loaded, 48)
            act.activation(bias_bc[:, 1, :], bias_bc[:, 1, :], ACT.Exp).then_inc(a_ready, 1)
            act.wait_ge(dtx_ready, 1)
            act.activation(dte[:, :, :], dtx[:, :, :], ACT.Abs).then_inc(dt_step, 1)
            act.wait_ge(dt_step, 1)
            act.activation(dte[:, :, :], dte[:, :, :], ACT.Exp, scale=-1.0).then_inc(dt_step, 1)
            act.wait_ge(dt_step, 2)
            act.activation(dtl[:, :, :], dte[:, :, :], ACT.Ln, bias=one).then_inc(dt_step, 1)
            act.wait_ge(dta_ready, 1)
            copy(dta_hi[:, :, :], dta[:, 0:TT, :], dhi_ready)
            act.wait_ge(acs_done, 1)
            act.activation(acs_e[:, :, :], M1[:, 0:256].rearrange("p (c h) -> p c h", c=TT), ACT.Exp).then_inc(acs_e_ready, 1)
            act.wait_ge(dtb_done, 1)
            act.activation(dab[:, :, :], M0[:, P:2 * P].rearrange("p (a b) -> p a b", b=NB), ACT.Exp).then_inc(dab_ready, 1)
            for i in range(3):
                t.next(i % 2)

            def conv_tile(a, dst, bias_col, n):
                a, r, _ = t.next(a)
                act.wait_ge(result, r)
                act.wait_ge(tapped, n)
                copy(t3(raw[:, 3:3 + T]), a3(a), moved[a])
                act.wait_ge(tapped, n + 1)
                act.activation(dst, dst, ACT.Silu, bias=g_prm[:, bias_col:bias_col + 1]).then_inc(conved, 1)

            conv_tile(1, bc[:, 0, :], 36, 1)
            conv_tile(0, bc[:, 1, :], 37, 2)

            def ssm_group(g, last):
                def chunk(c):
                    n = 8 * g + c + 1
                    act.wait_ge(cb_done, n)
                    copy(b_nat[:, :], M1[:, P:2 * P], bnat_ready)
                    act.wait_ge(a_spread, n)
                    if c:
                        act.wait_ge(ydiag_done, n - 1)
                    copy(aend[:, :], acc[1][:, P - 1:1024:P], aend_ready)
                    for e in range(E):
                        ins = act.activation(dec[:, e, :], acc[1][:, e * P:(e + 1) * P], ACT.Exp, bias=g_acn[:, c, e:e + 1])
                    ins.then_inc(dec_ready, 1)
                    act.wait_ge(aend_ready, n)
                    act.activation(cdec[:, :], aend[:, :], ACT.Exp).then_inc(cdec_ready, 1)
                    act.wait_ge(te_ready, n)
                    act.activation(toe[:, :], te[:, :], ACT.Exp).then_inc(toe_ready, 1)

                for i, a in enumerate((0, 1, 0, 1)):
                    conv_tile(a, xb[:, i, :], 16 + i, 6 * g + 3 + i)
                for c in range(TT):
                    chunk(c)
                    if c % 2:
                        a, r, _ = t.next(0)
                        act.wait_ge(result, r)
                        act.activation(t3(zb[:, c // 2, :]), a3(a), ACT.Silu).then_inc(moved[a], 1)
                        act.wait_ge(bc_spread, 4 * g + c // 2 + 1)
                        act.wait_ge(st_read, 4 * g + c // 2 + 1)
                        copy(bcs[:, :, :, :], M0[:, :].rearrange("p (j b n) -> p j b n", j=2, b=2), bc_ready)
                act.wait_ge(s_turned, g + 1)
                act.wait_ge(s_stored, 16 * g + 1)
                copy(s_out[:, :], M0[:, :], s_out_ready)
                act.wait_ge(s_out_ready, g + 1)
                act.dma_start(outs["ssm_prompt"][0, 0].rearrange("h p n -> (h p) n").rearrange("(a p) n -> p a n", p=P)[:, ds(XT * g, XT), :],
                              s_out[:, :].rearrange("p (a n) -> p a n", a=XT)).then_inc(s_stored, 16)
                for i in range(XT):
                    act.wait_ge(yz_ready, XT * g + i + 1)
                    if i:
                        act.wait_ge(t_added, XT * g + i)
                    act.activation(t_sq[:, :], xb[:, i, :], ACT.Square).then_inc(t_sq_ready, 1)
                if not last:
                    conv_tile(1, bc[:, 0, :], 36, 6 * g + 7)
                root(g + 4)
                if not last:
                    conv_tile(0, bc[:, 1, :], 37, 6 * g + 8)
                t.next(1)
                for i in range(XT):
                    act.wait_ge(yn_ready, XT * g + i + 1)
                    copy(o_hi[:, i, :], xb[:, i, :], o_hi_ready)
                for m in range(KT):
                    t.next(m % 2)

            with t.loop(act, 0, G - 1, 14, (11, 8)) as g:
                ssm_group(g, False)
            ssm_group(G - 1, True)
            waits = x_tiles()
            for q in range(2):
                act.wait_ge(st_stored[q], 64 * G + 1)
            act.wait_ge(s_stored, 16 * G + 1)
            for i in range(3):
                rows_from(11, ((outs["ssm_conv_prompt"][0, 0, :, i * D:(i + 1) * D], 0, 3),
                               (outs["ssm_conv_sample"][0, :, 2, i * D:(i + 1) * D], 3, 11)), 2 + i)
            cross(1, 4, 8, waits)
            norm(5, 9, x_tiles(), split=False)
            for i in range(TT + 1):
                a, r, _ = t.next(i % 2 ^ 1)
                rows = P if i < TT else NB
                act.wait_ge(result, r)
                if i >= 2:
                    act.wait_ge(y_stored[i % 2], 16 * (i // 2))
                act.activation(y_out[0:rows, i % 2, :], acc[a][0:rows, 0:D], ACT.Copy).then_inc(y_ready, 1)
            act.wait_ge(stored, 16 * (3 + 10))
            act.wait_ge(s_stored, 16 * G + 1)

        @block.vector
        def _(dve):
            t = Tally()
            steps, made = [0], [0]

            def step(ins):
                ins.then_inc(dve_step, 1)
                steps[0] += 1
                made[0] += 1
                dve.wait_ge(dve_step, steps[0])

            @contextmanager
            def loop(lo, hi, units, results, per):
                was, made[0] = steps[0], 0
                with t.loop(dve, lo, hi, units, results) as i:
                    steps[0] = was + (i - lo if lo else i) * per
                    yield i
                    assert made[0] == per, made
                steps[0] = was + (hi - lo) * per

            def prm_col(c):
                return prm[:, c:c + 1]

            for i, s in enumerate((moved[0], moved[1], kv_nat, cv_ready, tapped, st_read, st_stored[0], st_stored[1], s_stored)):
                dve.memset(credit[:, i:i + 1], 0.0).then_inc(s, 1)
            step(dve.memset(ms[:, :], 1.0))
            dve.memset(h_hi_f[:, KT * T:HPAD].bitcast(F32), 0.0).then_inc(padded, 1)
            dve.memset(h_lo_f[:, KT * T:HPAD].bitcast(F32), 0.0).then_inc(padded, 1)
            _, r, _ = t.next(0)
            dve.wait_ge(result, r)
            dve.tensor_copy(prm[:, :], acc[0][:, 0:PRM_N]).then_inc(moved[0], 1)
            dve.wait_ge(moved[0], 2)
            for i in range(MT):
                a, r, _ = t.next((i + 1) % 2)
                dve.wait_ge(m_hi_ready, i + 1)
                at = slice(i * P, (i + 1) * P)
                dve.tensor_tensor(m_lo[:, :, at], acc[a][:, 0:1024].rearrange("p (k m) -> p k m", k=KT),
                                  m_hi[:, :, at].bitcast(F32), ALU.subtract).then_inc(moved[a], 1)
            for i in range(TT + 1):
                rows = P if i < TT else NB
                a, r, _ = t.next((i + 1) % 2)
                dve.wait_ge(result, r)
                dve.tensor_copy(x[:, :, i * P:i * P + rows], acc[a][:, 0:1024].rearrange("p (k m) -> p k m", k=KT)[:, :, 0:rows])\
                   .then_inc(moved[a], 1)

            def take_rows(dst, rows, a):
                a, r, _ = t.next(a)
                dve.wait_ge(result, r)
                dve.tensor_copy(dst, acc[a][:, 0:1024].rearrange("p (k m) -> p k m", k=KT)[:, :, 0:rows]).then_inc(moved[a], 1)

            take_rows(st_pool[:, :, :], NB * POOL_BUF, 0)
            take_rows(st_conv[:, :, :], NB * 2, 1)

            def natural(l, j, i, s, n):
                dve.wait_ge(kv_turned, n)
                dve.tensor_scalar(kv_nat_sb[:, j, :, ds((2 * i + s) * P, P)], MS[s][:, 0:MT * P].rearrange("p (m d) -> p m d", m=MT),
                                  1.0, None, ALU.mult).then_inc(kv_nat, 1)

            for l in range(2):
                for j in range(2):
                    if l:
                        dve.wait_ge(kv_stored[j], 16)
                    with t.loop(dve, 0, 4, 2, (1, 1)) as i:
                        for s in range(2):
                            natural(l, j, i, s, 2 * i + s + 1 + 8 * (2 * l + j))

            def scales(src, n_all, inv):
                dve.wait_ge(ms_ready, n_all)
                step(dve.tensor_scalar(ms[:, 0:TT], src[:, 0:TT], inv, EPS, ALU.mult, ALU.add))
                dve.tensor_scalar(ms[0:NB, TT:TT + 1], src[0:NB, TT:TT + 1], inv, EPS, ALU.mult, ALU.add).then_inc(ms_scaled, 1)
                dve.wait_ge(sd_ready, n_all)
                dve.reciprocal(rstd[:, :], sd[:, :]).then_inc(rstd_ready, 1)

            def norm(n_th, n_all, gain):
                b = 7 * (n_th - 1)
                dve.wait_ge(sq_ready, 8 * (n_th - 1) + 2)
                dve.tensor_tensor(sq_sum[:, :], sq[:, 0, :], sq[:, 1, :], ALU.add).then_inc(sq_added, 1)
                for j in range(2, KT):
                    dve.wait_ge(sq_ready, 8 * (n_th - 1) + j + 1)
                    dve.wait_ge(sq_added, b + j - 1)
                    dve.tensor_tensor(sq_sum[:, :], sq_sum[:, :], sq[:, j % 2, :], ALU.add).then_inc(sq_added, 1)
                scales(M0, n_all, 1.0 / D)
                a, r, _ = t.next(0)
                dve.wait_ge(result, r)
                split = n_th < 5
                for j in range(KT):
                    if split and j >= 2:
                        dve.wait_ge(lo_ready, 8 * (n_th - 1) + j - 1)
                    ins = dve.scalar_tensor_tensor(out=h32[:, j % 2, :] if split else x[:, j, :], in0=x[:, j, :],
                                                   scalar=prm_col(gain + j), in1=acc[a][:, 0:T], op0=ALU.mult, op1=ALU.mult)
                    if split:
                        ins.then_inc(h32_ready, 1)
                        if j:
                            lo_half(n_th, j - 1)
                    else:
                        ins.then_inc(fin_ready, 1)
                if split:
                    lo_half(n_th, KT - 1)
                dve.wait_ge(fin_ready if not split else lo_ready, KT if not split else 8 * n_th)
                dve.memset(credit[:, 0:1], 0.0).then_inc(moved[a], 1)

            def lo_half(n_th, j):
                dve.wait_ge(hi_ready, 8 * (n_th - 1) + j + 1)
                dve.tensor_tensor(h_lo[:, j, :], h32[:, j % 2, :], h_hi[:, j, :].bitcast(F32), ALU.subtract).then_inc(lo_ready, 1)

            def add_chunk(sets=(0, 1)):
                for m in range(KT):
                    a, r, _ = t.next(sets[m % 2])
                    dve.wait_ge(result, r)
                    dve.tensor_tensor(t3(x[:, m, :]), a3(a), t3(x[:, m, :]), ALU.add).then_inc(moved[a], 1)

            norm(1, 1, PRM_MIX)

            step(dve.memset(u_pad[:, :, 0:WARM], 0.0))
            step(dve.memset(win_a[:, 0:WARM], 0.0))
            step(dve.memset(win_b[:, 0:WARM], 0.0))

            def window(g, i):
                w = WINDOWS[g]
                j = 2 * g + i
                k_in = t.taken[i]
                dve.wait_ge(moved[i], k_in + 1)
                step(dve.tensor_copy(u_keep[:, j, :], u_pad[:, i, WARM + TP - 15:WARM + T]))
                src, dst, other = u_pad[:, i, :], win_a, win_b
                for d in range(g + 1):
                    step(dve.tensor_tensor(dst[:, WARM:WARM + TP], src[:, WARM:WARM + TP],
                                           src[:, WARM - (1 << d):WARM + TP - (1 << d)], ALU.add))
                    src, dst, other = dst, other, dst
                state = st_pool[:, j, :].rearrange("p (b s) -> p b s", b=NB)
                step(dve.tensor_reduce(src[:, WARM + TP:WARM + T], state[:, :, POOL_BUF - w + 1:POOL_BUF], AX, ALU.add))
                step(dve.tensor_tensor(src[:, WARM + TP:WARM + T], src[:, WARM + TP:WARM + T], u_pad[:, i, WARM + TP:WARM + T], ALU.add))
                step(dve.tensor_tensor(src[:, WARM:WARM + 16], src[:, WARM:WARM + 16], cst[:, 16 * g:16 * g + 16], ALU.mult))
                dve.scalar_tensor_tensor(out=y32[:, :], in0=src[:, WARM:WARM + T], scalar=1.0 / w, in1=u_pad[:, i, WARM:WARM + T],
                                         op0=ALU.mult, op1=ALU.subtract).then_inc(d32_ready, 1)
                dve.wait_ge(d_hi_ready, j + 1)
                dve.tensor_tensor(d_lo[:, i, :], y32[:, :], d_hi[:, i, :].bitcast(F32), ALU.subtract).then_inc(d_ready, 1)
                dve.wait_ge(d_ready, j + 1)

            for g in range(4):
                t.next(0)
                t.next(1)
                for i in range(2):
                    window(g, i)
                if g:
                    add_chunk()
                t.next(0)
                t.next(1)
                for i in range(2):
                    j = 2 * g + i
                    dve.wait_ge(moved[i], t.taken[i] + 1)
                    a, r, _ = t.next(i)
                    dve.wait_ge(result, r)
                    dve.scalar_tensor_tensor(out=t3(y32[:, :]), in0=a3(a), scalar=prm_col(PRM_PSC + j), in1=t3(gate[:, i, :]),
                                             op0=ALU.mult, op1=ALU.mult).then_inc(moved[a], 1)
                    dve.wait_ge(y_hi_ready, j + 1)
                    dve.tensor_tensor(y_lo[:, i, :], y32[:, :], y_hi[:, i, :].bitcast(F32), ALU.subtract).then_inc(y_ready2, 1)
                    dve.wait_ge(y_ready2, j + 1)

            step(dve.memset(cv[:, :, 0:2], 0.0))

            def conv_tile(i, j):
                t.next(0)
                a, r, _ = t.next(1)
                dve.wait_ge(moved[0], t.taken[0] + 1)
                dve.wait_ge(result, r)
                dve.tensor_tensor(t3(cv[:, i, 2:2 + T]), a3(a), t3(c_sb[:, :]), ALU.mult).then_inc(moved[a], 1)
                dve.wait_ge(moved[a], t.taken[a] + 1)
                taps = [prm_col(PRM_CW + 8 * k + j) for k in range(3)]
                state = st_conv[:, j, :].rearrange("p (b s) -> p b s", b=NB)
                dve.tensor_scalar(cc[:, 0:TP], cv[:, i, 0:TP], taps[0], None, ALU.mult).then_inc(cv_ready, 1)
                step(dve.tensor_copy(c_keep[:, j, :], cv[:, i, 2 + TP - 2:2 + T]))
                step(dve.tensor_scalar(cc[:, TP:T], state[:, :, 0], taps[0], None, ALU.mult))
                dve.wait_ge(cv_ready, j + 2)
                for k in (1, 2):
                    step(dve.scalar_tensor_tensor(out=cc[:, 0:TP], in0=cv[:, i, k:k + TP], scalar=taps[k], in1=cc[:, 0:TP],
                                                  op0=ALU.mult, op1=ALU.add))
                    step(dve.scalar_tensor_tensor(out=cc[:, TP:T], in0=state[:, :, 1] if k == 1 else cv[:, i, 2 + TP:2 + T],
                                                  scalar=taps[k], in1=cc[:, TP:T], op0=ALU.mult, op1=ALU.add))
                t.next(0)
                gate_moved = t.taken[0] + 1
                if i == 0:
                    add_chunk((1, 0))
                a, r, _ = t.next(1)
                dve.wait_ge(result, r)
                dve.wait_ge(moved[0], gate_moved)
                dve.tensor_tensor(t3(cy32[:, i, :]), a3(a), t3(cc[:, :]), ALU.mult).then_inc(moved[a], 1)
                dve.wait_ge(moved[a], t.taken[a] + 1)
                dve.tensor_tensor(cy32[:, i, :], cy32[:, i, :], c_gate[:, i, :], ALU.mult).then_inc(cy32_ready, 1)
                dve.wait_ge(y_hi_ready, 8 + j + 1)
                dve.tensor_tensor(y_lo[:, i, :], cy32[:, i, :], y_hi[:, i, :].bitcast(F32), ALU.subtract).then_inc(y_ready2, 1)

            for g in range(4):
                for i in range(2):
                    conv_tile(i, 2 * g + i)
            add_chunk()
            t.next(1)
            t.next(1)

            def cross(l, n_th, n_all, gain):
                norm(n_th, n_all, gain)

                def queries():
                    for i in range(2):
                        n = q_at[0] + i + 1
                        a, r, _ = t.next(i)
                        dve.wait_ge(q_hi_ready, n)
                        dve.tensor_tensor(t3(q_lo[:, i, :]), a3(a), t3(q_hi[:, i, :].bitcast(F32)), ALU.subtract).then_inc(moved[a], 1)
                        yield i

                def attention(n):
                    def mix_out(half):
                        for k in range(2):
                            cols = slice(half * 512, half * 512 + 512)
                            dve.wait_ge(y_hi_ready, 16 + 4 * n + 2 * half + k + 1)
                            dve.tensor_tensor(y_lo[:, k, cols], (acc[0] if k == 0 else acc[1])[:, 1024:1536],
                                              y_hi[:, k, cols].bitcast(F32), ALU.subtract).then_inc(mixed_out, 1)

                    for i in range(TT + 2):
                        if i < TT:
                            dve.wait_ge(scored, 8 * n + i + 1)
                            dve.tensor_reduce(mx[:, i:i + 1], acc[0][:, (i % 2) * 512:(i % 2) * 512 + NM], AX, ALU.max).then_inc(mx_ready, 1)
                            dve.wait_ge(mx_ready, 8 * n + i + 1)
                            dve.tensor_scalar(nmx[:, i:i + 1], mx[:, i:i + 1], -HD ** -0.5, None, ALU.mult).then_inc(nmx_ready, 1)
                        if 1 <= i <= TT:
                            j = i - 1
                            dve.wait_ge(exped, 8 * n + j + 1)
                            dve.reciprocal(rinv[:, j:j + 1], rsum[:, j:j + 1]).then_inc(rinv_ready, 1)
                            dve.wait_ge(rinv_ready, 8 * n + j + 1)
                            dve.tensor_scalar(prob[:, j % 2, :], prob[:, j % 2, :], rinv[:, j:j + 1], None, ALU.mult).then_inc(prob_ready, 1)
                        if i >= 2:
                            j = i - 2
                            dve.wait_ge(pt_hi_ready, 8 * n + j + 1)
                            cols = slice((j % 4) * P, (j % 4 + 1) * P)
                            dve.tensor_tensor(pt_lo[:, :, cols], acc[1][:, (j % 2) * 512:(j % 2) * 512 + NM].rearrange("p (m t) -> p m t", m=2),
                                              pt_hi[:, :, cols].bitcast(F32), ALU.subtract).then_inc(pt_ready, 1)
                        if i == 7:
                            mix_out(0)
                    mix_out(1)
                    dve.wait_ge(k_loaded, 16 * n + 16)
                    dve.wait_ge(qbc_ready, 4 * n + 4)
                    for b in range(NB):
                        for m in range(MT):
                            kb = cache[:, b * MT + m, :]
                            ins = dve.tensor_tensor_reduce(out=kb, in0=kb, in1=q_bc[:, b, :], scale=1.0, scalar=0.0,
                                                           op0=ALU.mult, op1=ALU.add, accum_out=ss[:, m, b:b + 1])
                    ins.then_inc(ss_ready, 1)

                def sample_max(n):
                    dve.wait_ge(ss_turned, n + 1)
                    dve.tensor_reduce(s4[0:NB, 0:1], M0[0:NB, 0:NM], AX, ALU.max).then_inc(smx_ready, 1)
                    dve.wait_ge(smx_ready, n + 1)
                    dve.tensor_scalar(s4[0:NB, 1:2], s4[0:NB, 0:1], -HD ** -0.5, None, ALU.mult).then_inc(snmx_ready, 1)
                    dve.wait_ge(s_exped, n + 1)
                    dve.reciprocal(s4[0:NB, 3:4], s4[0:NB, 2:3]).then_inc(srinv_ready, 1)
                    dve.wait_ge(srinv_ready, n + 1)
                    dve.tensor_scalar(sp[0:NB, :], sp[0:NB, :], s4[0:NB, 3:4], None, ALU.mult).then_inc(sp_ready, 1)

                def sample_out(n):
                    dve.wait_ge(sp_turned, n + 1)
                    dve.tensor_copy(spt[:, :, :], M1[:, 0:MT * NB].rearrange("p (m b) -> p m b", m=MT)).then_inc(spt_ready, 1)
                    dve.wait_ge(sy_hi_ready, n + 1)
                    dve.tensor_tensor(y_lo[:, :, TP:T], M0[:, 0:2 * NB].rearrange("p (k b) -> p k b", k=2),
                                      y_hi[:, :, TP:T].bitcast(F32), ALU.subtract).then_inc(xy_ready, 1)

                n = HEADS * l
                q_at = [2 * n]
                for _ in queries():
                    pass
                attention(n)
                with t.loop(dve, 1, HEADS, 4, (5, 5)) as h:
                    n = HEADS * l + h
                    q_at[0] = 2 * n
                    for i in queries():
                        if i == 0:
                            sample_max(n - 1)
                    sample_out(n - 1)
                    add_chunk()
                    attention(n)
                n = HEADS * l + HEADS - 1
                sample_max(n)
                sample_out(n)
                add_chunk()

            cross(0, 2, 2, PRM_XA)

            norm(3, 3, PRM_MIX + KT)
            step(dve.memset(raw[:, 0:3], 0.0))
            dve.wait_ge(a_ready, 1)
            for i in range(2):
                step(dve.tensor_copy(dsk[64 * i:64 * i + 64, :], bias_bc[64 * i:64 * i + 64, 2, i:32:2]))
            dve.wait_ge(dt_done, 1)
            dve.tensor_tensor(dtx[:, :, :], M0[:, 0:9 * 32].rearrange("p (i h) -> p i h", h=32),
                              bias_bc[:, 0, :].unsqueeze(1).to_broadcast([P, 9, 32]), ALU.add).then_inc(dtx_ready, 1)
            dve.wait_ge(dt_step, 3)
            step(dve.scalar_tensor_tensor(out=dt_all[:, :, :], in0=dtx[:, :, :], scalar=0.0, in1=dtl[:, :, :],
                                          op0=ALU.max, op1=ALU.add))
            dve.scalar_tensor_tensor(out=dta[:, :, :], in0=dt_all[:, :, :], scalar=-1.0,
                                     in1=bias_bc[:, 1, :].unsqueeze(1).to_broadcast([P, 9, 32]),
                                     op0=ALU.mult, op1=ALU.mult).then_inc(dta_ready, 1)
            dve.wait_ge(dta_ready, 1)
            dve.wait_ge(dhi_ready, 1)
            dve.tensor_tensor(dta_lo[:, :, :], dta[:, 0:TT, :], dta_hi[:, :, :].bitcast(F32), ALU.subtract).then_inc(dlo_ready, 1)
            dve.wait_ge(acs_e_ready, 1)
            step(dve.tensor_scalar(acs_n[:, :, :], M1[:, 0:256].rearrange("p (c h) -> p c h", c=TT), -1.0, None, ALU.mult))
            dve.wait_ge(dab_ready, 1)
            step(dve.tensor_copy(dtb[:, :, :], M0[:, 0:P].rearrange("p (a b) -> p a b", b=NB)))
            dve.wait_ge(dlo_ready, 1)
            for i in range(3):
                take_rows(st_sc[:, 8 * i:8 * i + 8, :], NB * 3, i % 2)

            sw = prm[:, PRM_SW:PRM_SW + 96].rearrange("p (k j) -> p k j", k=4)

            def gather(lo, n, taps, bias, state, src):
                step(dve.tensor_copy(g_prm[:, taps:taps + 4 * n].rearrange("p (k j) -> p k j", k=4), sw[:, :, ds(src, n)]))
                step(dve.tensor_copy(g_prm[:, bias:bias + n], prm[:, ds(PRM_SB + src, n)]))
                step(dve.tensor_copy(g_st[:, state:state + n, :], st_sc[:, ds(src, n), :]))

            def taps_of(a, dst, taps, n_tiles, i, state, keep, n):
                t.next(a)
                dve.wait_ge(moved[a], t.taken[a] + 1)
                tap = [g_prm[:, taps + k * n_tiles + i:taps + k * n_tiles + i + 1] for k in range(4)]
                st3 = g_st[:, state, :].rearrange("p (b s) -> p b s", b=NB)
                step(dve.tensor_copy(s_keep[:, ds(keep, 1), :], raw[:, 3 + TP - 3:3 + T].unsqueeze(1)))
                step(dve.tensor_scalar(dst[:, 0:TP], raw[:, 0:TP], tap[0], None, ALU.mult))
                step(dve.tensor_scalar(dst[:, TP:T], st3[:, :, 0], tap[0], None, ALU.mult))
                for k in (1, 2, 3):
                    ins = dve.scalar_tensor_tensor(out=dst[:, TP:T], in0=st3[:, :, k] if k < 3 else raw[:, 3 + TP:3 + T],
                                                   scalar=tap[k], in1=dst[:, TP:T], op0=ALU.mult, op1=ALU.add)
                    step(ins)
                    ins = dve.scalar_tensor_tensor(out=dst[:, 0:TP], in0=raw[:, k:k + TP], scalar=tap[k], in1=dst[:, 0:TP],
                                                   op0=ALU.mult, op1=ALU.add)
                    if k < 3:
                        step(ins)
                    else:
                        ins.then_inc(tapped, 1)

            def v8(b):
                return b.rearrange("p (e c) -> p e c", e=E)

            gather(0, 1, 28, 36, 4, 16)
            gather(0, 1, 32, 37, 5, 20)
            taps_of(1, bc[:, 0, :], 28, 1, 0, 4, 16, 1)
            taps_of(0, bc[:, 1, :], 32, 1, 0, 5, 20, 2)

            def ssm_group(g, last):
                gather(0, XT, 0, 16, 0, XT * g)
                step(dve.tensor_copy(g_prm[:, 20:24], dsk[:, ds(XT * g, XT)]))
                step(dve.tensor_copy(g_prm[:, 24:28], prm[:, ds(PRM_NW + XT * g, XT)]))
                for dst, src in ((g_dt, dt_all), (g_acn, acs_n), (g_ace, acs_e), (g_dhi, dta_hi), (g_dlo, dta_lo)):
                    s = src[:, 0:TT, ds(E * g, E)]
                    step(dve.tensor_copy(dst[:, :, :], s.bitcast(F32) if src.dtype == F32R else s))
                step(dve.tensor_copy(g_dtb[:, :, :], dtb[:, ds(XT * g, XT), :]))
                dve.memset(S[:, :], 0.0).then_inc(s_ready, 1)
                dve.tensor_copy(g_dab[:, :, :], dab[:, ds(XT * g, XT), :]).then_inc(g_ready, 1)
                for i, a in enumerate((0, 1, 0, 1)):
                    taps_of(a, xb[:, i, :], 0, XT, i, i, XT * g + i, 0)
                dve.wait_ge(conved, 6 * g + 6)
                if not last:
                    gather(0, 1, 28, 36, 4, 17 + g)
                    gather(0, 1, 32, 37, 5, 21 + g)
                dve.tensor_tensor(xd[:, :, :], xb[:, :, TP:T], g_dtb[:, :, :], ALU.mult).then_inc(xd_ready, 1)

                def sample(q):
                    b = q % 2
                    dve.wait_ge(st_new, 4 * g + q + 1)
                    for i in range(2):
                        step(dve.tensor_tensor(bx[:, i], st[:, b, i], bcs[:, 1, i, :].unsqueeze(1).to_broadcast([P, XT, N]), ALU.mult))
                    dve.tensor_reduce(yss[:, :, 2 * q:2 * q + 2].rearrange("p a b -> p b a"), bx[:, :], AX, ALU.add).then_inc(st_read, 1)

                for c in range(TT):
                    n = 8 * g + c + 1
                    cs = slice(c * P, (c + 1) * P)
                    dve.wait_ge(x_turned, n)
                    if c:
                        dve.wait_ge(xde_ready, n - 1)
                        dve.wait_ge(ydiag_done, n - 1)
                    dve.tensor_tensor(v8(xdt[:, :]), v8(M0[:, :]), g_dt[:, c, :].unsqueeze(2).to_broadcast([P, E, 64]), ALU.mult)\
                       .then_inc(xdt_ready, 1)
                    dve.wait_ge(dec_ready, n)
                    dve.tensor_tensor(dec[:, :, :], M1[:, 0:P].unsqueeze(1).to_broadcast([P, E, P]), dec[:, :, :], ALU.mult)\
                       .then_inc(mm_ready, 1)
                    if c:
                        dve.wait_ge(y_turned, n - 1)
                    else:
                        dve.wait_ge(s_stored, 16 * g + 1)
                    dve.wait_ge(yoff_done, n)
                    step(dve.tensor_tensor(v8(y_nat[:, :]), v8(acc[1][:, 1024:1536]), g_ace[:, c, :].unsqueeze(2).to_broadcast([P, E, 64]),
                                           ALU.mult))
                    dve.wait_ge(ydiag_done, n)
                    dve.tensor_tensor(y_nat[:, :], acc[1][:, 0:512], y_nat[:, :], ALU.add).then_inc(ynat_ready, 1)
                    dve.wait_ge(s_done, n)
                    dve.wait_ge(s_decayed, n)
                    dve.tensor_tensor(S[:, :], acc[1][:, 512:1024], S[:, :], ALU.add).then_inc(s_ready, 1)
                    dve.wait_ge(y_turned, n)
                    for i in range(XT):
                        ins = dve.scalar_tensor_tensor(out=xb[:, i, cs], in0=xb[:, i, cs], scalar=g_prm[:, 20 + i:21 + i],
                                                       in1=M0[:, i * P:(i + 1) * P], op0=ALU.mult, op1=ALU.add)
                    ins.then_inc(y_back, 1)
                    if c % 2:
                        t.next(0)
                    if c % 2 == 0 and c:
                        sample(c // 2 - 1)
                sample(3)
                dve.wait_ge(st_read, 4 * g + 5)
                for i in range(XT):
                    step(dve.scalar_tensor_tensor(out=xb[:, i, TP:T], in0=xb[:, i, TP:T], scalar=g_prm[:, 20 + i:21 + i],
                                                  in1=yss[:, i, :], op0=ALU.mult, op1=ALU.add))
                dve.wait_ge(moved[0], t.taken[0] + 1)
                dve.wait_ge(y_back, 8 * g + 8)
                for i in range(XT):
                    dve.tensor_tensor(xb[:, i, :], xb[:, i, :], zb[:, i, :], ALU.mult).then_inc(yz_ready, 1)
                    if i:
                        t_add(g, i - 1)
                t_add(g, XT - 1)
                if not last:
                    taps_of(1, bc[:, 0, :], 28, 1, 0, 4, 17 + g, 0)
                scales(M1, g + 4, 1.0 / 512)
                if not last:
                    taps_of(0, bc[:, 1, :], 32, 1, 0, 5, 21 + g, 0)
                a, r, _ = t.next(1)
                dve.wait_ge(result, r)
                for i in range(XT):
                    dve.scalar_tensor_tensor(out=xb[:, i, :], in0=xb[:, i, :], scalar=g_prm[:, 24 + i:25 + i], in1=acc[a][:, 0:T],
                                             op0=ALU.mult, op1=ALU.mult).then_inc(yn_ready, 1)
                    if i:
                        o_half(g, i - 1)
                o_half(g, XT - 1)
                dve.memset(credit[:, 0:1], 0.0).then_inc(moved[a], 1)
                add_chunk()

            def t_add(g, i):
                dve.wait_ge(t_sq_ready, XT * g + i + 1)
                if i == 0:
                    dve.tensor_copy(t_sum[:, :], t_sq[:, :]).then_inc(t_added, 1)
                else:
                    dve.wait_ge(t_added, XT * g + i)
                    dve.tensor_tensor(t_sum[:, :], t_sum[:, :], t_sq[:, :], ALU.add).then_inc(t_added, 1)

            def o_half(g, i):
                dve.wait_ge(o_hi_ready, XT * g + i + 1)
                dve.tensor_tensor(o_lo[:, i, :], xb[:, i, :], o_hi[:, i, :].bitcast(F32), ALU.subtract).then_inc(o_ready, 1)

            with loop(0, G - 1, 14, (11, 8), 86) as g:
                ssm_group(g, False)
            ssm_group(G - 1, True)
            for _ in range(3):
                t.next(1)
            cross(1, 4, 8, PRM_XA + KT)
            norm(5, 9, PRM_FIN)


_INS = ['x_prompt', 'x_sample', 'mem_prompt', 'cache_mem_k', 'cache_mem_v', 'state_pool', 'state_conv',
        'state_ssm_conv', 'state_ssm', 'norm_mix', 'norm_xa', 'norm_final', 'w_in_even', 'pool_w', 'pool_scale',
        'conv_w', 'w_out_even', 'w_in_odd', 'ssm_conv_w', 'ssm_conv_b', 'dt_bias', 'a_log', 'd_skip', 'ssm_norm',
        'w_out_odd', 'w_xa_q', 'w_xa_k', 'w_xa_v', 'w_xa_o']
_OUTS = [('y_prompt', (1, 1024, 1024)), ('y_sample', (8, 1, 1024)), ('mem_k', (2, 1, 256, 4, 256)),
         ('mem_v', (2, 1, 256, 4, 256)), ('pool_prompt', (1, 1, 15, 1024)), ('pool_sample', (1, 8, 15, 1024)),
         ('conv_prompt', (1, 1, 2, 1024)), ('conv_sample', (1, 8, 2, 1024)), ('ssm_conv_prompt', (1, 1, 3, 3072)),
         ('ssm_conv_sample', (1, 8, 3, 3072)), ('ssm_prompt', (1, 1, 32, 64, 128)), ('ssm_sample', (1, 8, 32, 64, 128))]


def kernel(**inputs):
    import numpy as _np
    import concourse.bacc as _bacc
    from concourse import mybir as _mybir
    from concourse.bass_utils import run_bass_kernel_spmd as _run

    nc = _bacc.Bacc("TRN2", target_bir_lowering=False, num_devices=1)
    arrays, ins, outs = {}, {}, {}
    for name in _INS:
        a = _np.ascontiguousarray(inputs[name])
        arrays[f"in_{name}"] = a
        ins[name] = nc.dram_tensor(f"in_{name}", a.shape, _mybir.dt.from_np(a.dtype), kind="ExternalInput").ap()
    arrays["in_constants"] = constants()
    ins["constants"] = nc.dram_tensor("in_constants", (P, C_N), _mybir.dt.float32, kind="ExternalInput").ap()
    for name, shape in _OUTS:
        outs[name] = nc.dram_tensor(f"out_{name}", shape, _mybir.dt.float32, kind="ExternalOutput").ap()
    mem_kt = nc.dram_tensor("mem_kt", (2, D, NM), _mybir.dt.float32).ap()
    build(nc, ins, outs, mem_kt)
    r = _run(nc, [arrays], core_ids=[0])
    return tuple(r.results[0][f"out_{name}"] for name, _ in _OUTS)
```

```python
from contextlib import ExitStack, contextmanager

import numpy as np

import concourse.bass as bass
from concourse import mybir

F32 = mybir.dt.float32
F32R = mybir.dt.float32r
ALU = mybir.AluOpType
ACT = mybir.ActivationFunctionType
AX = mybir.AxisListType.X
ds = bass.ds

P = 128
D = 1024
KT = D // P
TP = 1024
NB = 8
T = TP + NB
NCH = 3
CH = T // NCH
TT = TP // P
NM = 256
MT = NM // P
HEADS, HD = 4, 256
POOL_BUF = 15
WINDOWS = (2, 4, 8, 16)
G, E, N = 4, 8, 128
D_INNER = 2048
CONV_DIM = D_INNER + 2 * G * N
DT_AT = D_INNER + CONV_DIM + G * E - P
XT = 4
EPS = 1e-6
NEG = -1e30
WARM = 16

PRM_MIX, PRM_XA, PRM_FIN, PRM_PSC, PRM_CW, PRM_SB, PRM_NW, PRM_SW = 0, 16, 32, 40, 48, 72, 96, 112
PRM_N = 208
C_ID, C_TRI, C_MASK, C_INV, C_ONE, C_N = 0, 128, 256, 768, 832, 834


def constants():
    c = np.zeros((P, C_N), np.float32)
    s, l = np.arange(P)[:, None], np.arange(P)[None, :]
    c[:, C_ID:C_ID + P] = s == l
    c[:, C_TRI:C_TRI + P] = s <= l
    for i in range(4):
        c[:, C_MASK + i * P:C_MASK + (i + 1) * P] = np.where(s <= l, 0.0, NEG)
    for g, w in enumerate(WINDOWS):
        c[:, C_INV + 16 * g:C_INV + 16 * g + 16] = w / np.minimum(np.arange(16) + 1, w)
    c[:, C_ONE] = 1.0
    c[:, C_ONE + 1] = EPS
    return c


class Tally:

    def __init__(self):
        self.slot = [0, 0]
        self.result = 0
        self.taken = [0, 0]
        self.turn = 0
        self.made = [0, 0, 0]

    def unit(self):
        s = self.turn
        self.turn = 1 - s
        self.slot[s] += 1
        self.made[0] += 1
        return s, self.slot[s]

    def next(self, a):
        self.result += 1
        self.taken[a] += 1
        self.made[1 + a] += 1
        return a, self.result, self.taken[a]

    @contextmanager
    def loop(self, eng, lo, hi, units, results):
        was = [*self.slot], self.result, [*self.taken]
        with eng.Fori(lo, hi) as g:
            n = g - lo if lo else g
            self.slot = [v + n * (units // 2) for v in was[0]]
            self.result = was[1] + n * sum(results)
            self.taken = [v + n * r for v, r in zip(was[2], results)]
            self.made = [0, 0, 0]
            yield g
            assert self.made[0] in (0, units) and self.made[1:] in ([0, 0], [*results]), (self.made, units, results)
        n = hi - lo
        self.slot = [v + n * (units // 2) for v in was[0]]
        self.result = was[1] + n * sum(results)
        self.taken = [v + n * r for v, r in zip(was[2], results)]


def build(nc, ins, outs, scratch):
    ctx = ExitStack()
    with ctx:
        def sb(name, shape, dt=F32):
            return ctx.enter_context(nc.sbuf_tensor(name, shape, dt))

        def sem(name):
            return ctx.enter_context(nc.semaphore(name))

        table = sb("table", [P, C_INV], F32R)
        cst = sb("cst", [P, C_N - C_INV])
        prm = sb("prm", [P, PRM_N])
        zero = sb("zero", [P, 2])
        credit = sb("credit", [P, 10])
        u_keep = sb("u_keep", [P, KT, 23])
        c_keep = sb("c_keep", [P, KT, 10])
        x = sb("x", [P, KT, T])
        h_hi = sb("h_hi", [P, KT, T], F32R)
        h_lo = sb("h_lo", [P, KT, T], F32R)
        sd = sb("sd", [P, TT + 1])
        rstd = sb("rstd", [P, TT + 1])
        w_raw = sb("w_raw", [P, 2, 1024])
        w_hi = sb("w_hi", [P, 2, 1024], F32R)
        w_lo = sb("w_lo", [P, 2, 1024], F32R)

        class Area:

            def __init__(self, at):
                self.at = at

            def __call__(self, name, shape, dt=F32):
                t = nc.alloc_sbuf_tensor_at(name, shape, dt, offset=self.at)
                self.at += -(-int(np.prod(shape[1:])) * 4 // 32) * 32
                assert self.at <= work_end, name
                return t

        work = (nc.sbuf_base + 31) // 32 * 32
        work_end = nc.sbuf_usable_end

        a = Area(work)
        x_in = a("x_in", [P, 2, D])
        m_hi = a("m_hi", [P, KT, NM], F32R)
        m_lo = a("m_lo", [P, KT, NM], F32R)
        p_in = a("p_in", [P, 2, P])
        kt_out = a("kt_out", [P, 2, NM])
        kv_nat_sb = a("kv_nat_sb", [P, 2, MT, D])
        assert a.at <= work + 43 * 1024
        norm_at = work + 54496
        late = norm_at + 5 * 4128
        a = Area(work + 43 * 1024)
        st_rows = a("st_rows", [P, D])
        cst_rows = a("cst_rows", [P, D])
        a = Area(late)
        st_pool = a("st_pool", [P, KT, NB * POOL_BUF])
        st_conv = a("st_conv", [P, KT, NB * 2])
        row_out = a("row_out", [P, D])
        table_in = Area(work + 60 * 1024)("table_in", [P, C_N])
        a = Area(norm_at)
        sq = a("sq", [P, 2, T])
        sq_sum = a("sq_sum", [P, T])
        h32 = a("h32", [P, 2, T])
        a = Area(work)
        y_hi = a("y_hi", [P, 2, T], F32R)
        y_lo = a("y_lo", [P, 2, T], F32R)
        after_y = a.at
        pw_raw = a("pw_raw", [P, 512])
        pw_hi = a("pw_hi", [P, 512], F32R)
        pw_lo = a("pw_lo", [P, 512], F32R)
        u_pad = a("u_pad", [P, 2, WARM + T])
        win_a = a("win_a", [P, WARM + T])
        win_b = a("win_b", [P, WARM + T])
        d_hi = a("d_hi", [P, 2, T], F32R)
        d_lo = a("d_lo", [P, 2, T], F32R)
        gate = a("gate", [P, 2, T])
        y32 = a("y32", [P, T])
        a = Area(after_y)
        c_sb = a("c_sb", [P, T])
        cv = a("cv", [P, 2, 2 + T])
        cc = a("cc", [P, T])
        c_gate = a("c_gate", [P, 2, T])
        cy32 = a("cy32", [P, 2, T])
        a = Area(after_y)
        q_hi = a("q_hi", [P, 2, T], F32R)
        q_lo = a("q_lo", [P, 2, T], F32R)
        kv_raw = a("kv_raw", [P, 2, 512])
        kv_hi = a("kv_hi", [P, 2, 512], F32R)
        kv_lo = a("kv_lo", [P, 2, 512], F32R)
        prob = a("prob", [P, 2, NM])
        pt_hi = a("pt_hi", [P, MT, 512], F32R)
        pt_lo = a("pt_lo", [P, MT, 512], F32R)
        cache = a("cache", [P, NB * MT, HD])
        q_bc = a("q_bc", [P, NB, HD])
        mx = a("mx", [P, 8])
        nmx = a("nmx", [P, 8])
        rsum = a("rsum", [P, 8])
        rinv = a("rinv", [P, 8])
        ss = a("ss", [P, MT, NB])
        sp = a("sp", [P, NM])
        spt = a("spt", [P, MT, NB * NB])
        s4 = a("s4", [P, 4])
        a = Area(work)
        dt_all = a("dt_all", [P, 9, G * E])
        dta = a("dta", [P, 9, G * E])
        acs_n = a("acs_n", [P, TT, G * E])
        acs_e = a("acs_e", [P, TT, G * E])
        dta_hi = a("dta_hi", [P, TT, G * E], F32R)
        dta_lo = a("dta_lo", [P, TT, G * E], F32R)
        dtb = a("dtb", [P, 16, NB])
        dab = a("dab", [P, 16, NB])
        dsk = a("dsk", [P, 16])
        st_sc = a("st_sc", [P, 24, NB * 3])
        s_keep = a("s_keep", [P, 24, 11])
        g_dt = a("g_dt", [P, TT, E])
        g_acn = a("g_acn", [P, TT, E])
        g_ace = a("g_ace", [P, TT, E])
        g_dhi = a("g_dhi", [P, TT, E], F32R)
        g_dlo = a("g_dlo", [P, TT, E], F32R)
        g_dtb = a("g_dtb", [P, XT, NB])
        g_dab = a("g_dab", [P, XT, NB])
        g_prm = a("g_prm", [P, 56])
        g_st = a("g_st", [P, 6, NB * 3])
        bc = a("bc", [P, 2, T])
        xb_at = a.at
        xb = a("xb", [P, XT, T])
        zb_at = a.at
        zb = a("zb", [P, XT, T])
        after_z = a.at
        b2 = Area(xb_at)
        o_lo = b2("o_lo", [P, XT, T], F32R)
        b2 = Area(zb_at)
        o_hi = b2("o_hi", [P, XT, T], F32R)
        raw = a("raw", [P, 3 + T])
        t_sq = a("t_sq", [P, T])
        t_sum = a("t_sum", [P, T])
        b2 = Area(after_z + 32)
        dec = b2("dec", [P, E, P])
        xdt = b2("xdt", [P, 512])
        xde = b2("xde", [P, 512])
        b2 = Area(a.at - 4 * T)
        bx = b2("bx", [P, 2, XT, N])
        a = Area(max(a.at, b2.at))
        b_nat = a("b_nat", [P, P])
        y_nat = a("y_nat", [P, 512])
        S = a("S", [P, 512])
        s_out = y_nat
        aend = a("aend", [P, E])
        te = a("te", [P, E])
        toe = a("toe", [P, E])
        cdec = a("cdec", [P, E])
        st = a("st", [P, 2, 2, XT, N])
        bcs = a("bcs", [P, 2, 2, N])
        xd = a("xd", [P, XT, NB])
        yss = a("yss", [P, XT, NB])
        a = Area(xb_at)
        dt_rows = a("dt_rows", [P, 9 * P])
        dtx = a("dtx", [P, 9, 32])
        dte = a("dte", [P, 9, 32])
        dtl = a("dtl", [P, 9, 32])
        bias_bc = a("bias_bc", [P, 3, 32])
        sc_rows = a("sc_rows", [P, CONV_DIM])
        a = Area(work)
        y_out = a("y_out", [P, 4, D])

        acc = [ctx.enter_context(nc.psum_tensor(f"acc{i}", [P, NCH * 512], F32)) for i in range(2)]
        M0 = ctx.enter_context(nc.psum_tensor("M0", [P, 512], F32))
        M1 = ctx.enter_context(nc.psum_tensor("M1", [P, 512], F32))
        MS = [M0, M1]

        def a3(s):
            return acc[s][:, :].rearrange("p (n c) -> p n c", c=512)[:, :, 0:CH]

        def t3(ap):
            return ap.rearrange("p (n c) -> p n c", c=CH)

        ident_r, tri_r, mask_r = table[:, C_ID:C_ID + P], table[:, C_TRI:C_TRI + P], table[:, C_MASK:C_MASK + 512]
        ident, tri = ident_r.bitcast(F32), tri_r.bitcast(F32)
        one = cst[:, C_ONE - C_INV:C_ONE - C_INV + 1]
        eps = cst[:, C_ONE - C_INV + 1:C_ONE - C_INV + 2]

        w_loaded = [sem("w_loaded0"), sem("w_loaded1")]
        w_hi_done = sem("w_hi_done")
        w_split = [sem("w_split0"), sem("w_split1")]
        w_used = [sem("w_used0"), sem("w_used1")]
        result = sem("result")
        moved = [sem("moved0"), sem("moved1")]
        stored = sem("stored")
        a_ready = sem("a_ready")
        a_spread = sem("a_spread")
        acs_done = sem("acs_done")
        acs_e_ready = sem("acs_e_ready")
        aend_ready = sem("aend_ready")
        attended = sem("attended")
        bc_ready = sem("bc_ready")
        bc_spread = sem("bc_spread")
        bnat_ready = sem("bnat_ready")
        cb_done = sem("cb_done")
        cdec_ready = sem("cdec_ready")
        conved = sem("conved")
        cv_ready = sem("cv_ready")
        cy32_ready = sem("cy32_ready")
        d32_ready = sem("d32_ready")
        d_hi_ready = sem("d_hi_ready")
        d_ready = sem("d_ready")
        dab_ready = sem("dab_ready")
        dec_ready = sem("dec_ready")
        dhi_ready = sem("dhi_ready")
        dlo_ready = sem("dlo_ready")
        dp_loaded = sem("dp_loaded")
        dt_done = sem("dt_done")
        dt_padded = sem("dt_padded")
        mw_hi_done = sem("mw_hi_done")
        dt_step = sem("dt_step")
        dta_ready = sem("dta_ready")
        dtb_done = sem("dtb_done")
        dtx_ready = sem("dtx_ready")
        dve_step = sem("dve_step")
        exped = sem("exped")
        fin_ready = sem("fin_ready")
        g_ready = sem("g_ready")
        h32_ready = sem("h32_ready")
        hi_ready = sem("hi_ready")
        k_loaded = sem("k_loaded")
        kt_stored = [sem("kt_stored0"), sem("kt_stored1")]
        kv_loaded = sem("kv_loaded")
        kv_nat = sem("kv_nat")
        kv_split = sem("kv_split")
        kv_stored = [sem("kv_stored0"), sem("kv_stored1")]
        kv_turned = sem("kv_turned")
        lo_ready = sem("lo_ready")
        m_hi_ready = sem("m_hi_ready")
        mix_done = sem("mix_done")
        mixed_out = sem("mixed_out")
        mm_ready = sem("mm_ready")
        mx_ready = sem("mx_ready")
        nmx_ready = sem("nmx_ready")
        o_hi_ready = sem("o_hi_ready")
        o_ready = sem("o_ready")
        prob_ready = sem("prob_ready")
        prob_turned = sem("prob_turned")
        pt_hi_ready = sem("pt_hi_ready")
        pt_ready = sem("pt_ready")
        pw_loaded = sem("pw_loaded")
        pw_split = sem("pw_split")
        pw_used = sem("pw_used")
        q_hi_ready = sem("q_hi_ready")
        qbc_done = sem("qbc_done")
        qbc_ready = sem("qbc_ready")
        rinv_ready = sem("rinv_ready")
        s_decayed = sem("s_decayed")
        s_done = sem("s_done")
        s_exped = sem("s_exped")
        s_out_ready = sem("s_out_ready")
        s_ready = sem("s_ready")
        s_stored = sem("s_stored")
        s_turned = sem("s_turned")
        sc_loaded = sem("sc_loaded")
        scored = sem("scored")
        smix_done = sem("smix_done")
        smx_ready = sem("smx_ready")
        snmx_ready = sem("snmx_ready")
        sp_ready = sem("sp_ready")
        sp_turned = sem("sp_turned")
        spt_ready = sem("spt_ready")
        sq_added = sem("sq_added")
        sq_ready = sem("sq_ready")
        srinv_ready = sem("srinv_ready")
        ss_ready = sem("ss_ready")
        ss_turned = sem("ss_turned")
        st_loaded = [sem("st_loaded0"), sem("st_loaded1")]
        st_new = sem("st_new")
        st_part = sem("st_part")
        st_read = sem("st_read")
        st_rows_in = sem("st_rows_in")
        st_stored = [sem("st_stored0"), sem("st_stored1")]
        sy_hi_ready = sem("sy_hi_ready")
        t_added = sem("t_added")
        t_sq_ready = sem("t_sq_ready")
        table_r = sem("table_r")
        tables = sem("tables")
        tapped = sem("tapped")
        te_ready = sem("te_ready")
        toe_ready = sem("toe_ready")
        v_loaded = sem("v_loaded")
        x_loaded = [sem("x_loaded0"), sem("x_loaded1")]
        x_turned = sem("x_turned")
        xd_ready = sem("xd_ready")
        xde_ready = sem("xde_ready")
        xdt_ready = sem("xdt_ready")
        xy_ready = sem("xy_ready")
        y_back = sem("y_back")
        y_hi_ready = sem("y_hi_ready")
        y_ready = sem("y_ready")
        y_ready2 = sem("y_ready2")
        y_stored = [sem(f"y_stored{i}") for i in range(4)]
        y_turned = sem("y_turned")
        ydiag_done = sem("ydiag_done")
        yn_ready = sem("yn_ready")
        ynat_ready = sem("ynat_ready")
        yoff_done = sem("yoff_done")
        yz_ready = sem("yz_ready")
        zeroed = sem("zeroed")

        rows_copied = sem("rows_copied")
        sq1_ready = sem("sq1_ready")
        sq1_added = sem("sq1_added")
        summed = sem("summed")
        root_ready = sem("root_ready")
        rstd_ready = sem("rstd_ready")
        so_ready = sem("so_ready")
        so_turned = sem("so_turned")

        def scales_at(n_th):
            return n_th if n_th <= 3 else n_th + G

        block = ctx.enter_context(nc.Block())

        @block.sync
        def _(sp):
            t = Tally()

            def load(src, kb):
                s, n = t.unit()
                if not isinstance(n, int) or n > 1:
                    sp.wait_ge(w_split[s], n - 1)
                sp.dma_start(w_raw[:, s].rearrange("p (k n) -> p k n", k=kb), src).then_inc(w_loaded[s], 16)

            def columns(w, at):
                load(w.rearrange("(k p) n -> p k n", p=P)[:, :, ds(at, P)], KT)

            def out_rows(w, chunk, kb):
                wide = 1024 // kb
                for i in range(D // wide):
                    load(w.rearrange("(k p) n -> p k n", p=P)[:, ds(chunk * kb, kb), i * wide:(i + 1) * wide], kb)

            sp.dma_start(table_in[:, :], ins["constants"]).then_inc(tables, 16)
            row = 0
            for src, n in ((ins["norm_mix"].rearrange("l (j p) -> (l j) p", p=P), 16),
                           (ins["norm_xa"].rearrange("l (j p) -> (l j) p", p=P), 16),
                           (ins["norm_final"].rearrange("(j p) -> j p", p=P), 8),
                           (ins["pool_scale"].rearrange("l (j p) -> (l j) p", p=P), 8),
                           (ins["conv_w"].rearrange("l k (j p) -> (l k j) p", p=P), 24),
                           (ins["ssm_conv_b"].rearrange("l (j p) -> (l j) p", p=P), 24),
                           (ins["ssm_norm"].rearrange("l (j p) -> (l j) p", p=P), 16)):
                sp.dma_start(p_in[row:row + n, 0, :], src).then_inc(tables, 16)
                row += n
            sp.dma_start(p_in[0:96, 1, :], ins["ssm_conv_w"].rearrange("l k (j p) -> (l k j) p", p=P)).then_inc(tables, 16)
            for i in range(MT):
                sp.dma_start(x_in[:, i, :], ins["mem_prompt"][0, i * P:(i + 1) * P, :]).then_inc(x_loaded[i], 16)
            with sp.Fori(0, TT // 2) as m:
                for i in range(2):
                    sp.wait_ge(result, 2 * m + i + 2)
                    sp.dma_start(x_in[:, i, :], ins["x_prompt"][0].rearrange("(a p) d -> a p d", p=P)[ds(2 * m + i, 1)]
                                 .rearrange("a p d -> (a p) d")).then_inc(x_loaded[i], 16)
            sp.wait_ge(result, TT + 2)
            sp.dma_start(x_in[0:NB, 0, :], ins["x_sample"].rearrange("b s d -> (b s) d")).then_inc(x_loaded[0], 16)
            for l in range(2):
                for w in (ins["w_xa_k"], ins["w_xa_v"]):
                    if l == 0 and w is ins["w_xa_k"]:
                        columns(w[0], 0)
                        columns(w[0], P)
                        with t.loop(sp, 1, 4, 2, (1, 1)) as i:
                            for s in range(2):
                                columns(w[0], (2 * i + s) * P)
                    else:
                        with t.loop(sp, 0, 4, 2, (1, 1)) as i:
                            for s in range(2):
                                columns(w[l], (2 * i + s) * P)

            def cross(l):
                wq, wo = ins["w_xa_q"][l], ins["w_xa_o"][l]
                columns(wq, 0)
                columns(wq, P)
                with t.loop(sp, 0, HEADS - 1, 4, (6, 4)) as h:
                    columns(wq, (h + 1) * HD)
                    columns(wq, (h + 1) * HD + P)
                    out_rows(wo, h, 2)
                out_rows(wo, HEADS - 1, 2)

            we, wo = ins["w_in_even"][0], ins["w_out_even"][0]

            def pool_units(g, first):
                columns(we, g * 256)
                columns(we, g * 256 + P)
                if first:
                    sp.wait_ge(h32_ready, 1)
                else:
                    sp.wait_ge(pw_split, g)
                sp.dma_start(pw_raw[:, :].rearrange("p (k n) -> p k n", k=2),
                             ins["pool_w"][0].rearrange("g (k p) n -> p (g k) n", p=P)[:, ds(2 * g, 2), :]).then_inc(pw_loaded, 16)
                columns(we, D + g * 256)
                columns(we, D + g * 256 + P)
                if not first:
                    out_rows(wo, g - 1, 2)

            pool_units(0, True)
            with t.loop(sp, 1, 4, 6, (7, 7)) as g:
                pool_units(g, False)
            with t.loop(sp, 0, 4, 10, (8, 8)) as g:
                def conv_col(part, i):
                    columns(we, part * D + g * 256 + i * P)
                for part in (3, 4, 5):
                    conv_col(part, 0)
                out_rows(wo, g + 3, 2)
                conv_col(2, 0)
                for part in (3, 4, 5, 2):
                    conv_col(part, 1)
            out_rows(wo, 7, 2)
            cross(0)

            wi, wo = ins["w_in_odd"][0], ins["w_out_odd"][0]
            st_in = ins["state_ssm"][0].rearrange("b h p n -> b (h p) n").rearrange("b (a p) n -> b p a n", p=P)
            st_to = outs["ssm_sample"][0].rearrange("b h p n -> b (h p) n").rearrange("b (a p) n -> b p a n", p=P)

            def state_load(g, q):
                for b in range(2):
                    sp.dma_start(st[:, q % 2, b], st_in[2 * q + b, :, ds(XT * g, XT), :]).then_inc(st_loaded[q % 2], 16)

            def state_store(g, q):
                sp.wait_ge(st_new, NB // 2 * g + q + 1)
                for b in range(2):
                    sp.dma_start(st_to[2 * q + b, :, ds(XT * g, XT), :], st[:, q % 2, b]).then_inc(st_stored[q % 2], 16)

            def ssm_units(g, last):
                for i in range(XT):
                    columns(wi, D_INNER + g * 512 + i * P)
                for q in range(2):
                    sp.wait_ge(st_stored[q], 64 * g + 1)
                    sp.wait_ge(st_read, 4 * g + 1)
                    state_load(g, q)
                for i in range(2):
                    columns(wi, (g + 1) * 512 + (i * P - 512))
                for q in range(4):
                    state_store(g, q)
                    if q < 2:
                        sp.wait_ge(st_read, 4 * g + q + 2)
                        sp.wait_ge(st_stored[q % 2], (g + 1) * 64 - 31)
                        state_load(g, q + 2)
                        columns(wi, g * 512 + (q + 2) * P)
                    elif not last:
                        columns(wi, D_INNER + D_INNER + (q - 2) * 512 + (g + 1) * P)
                out_rows(wo, g, 4)

            columns(wi, DT_AT)
            columns(wi, 2 * D_INNER)
            columns(wi, 2 * D_INNER + 512)
            with t.loop(sp, 0, G - 1, 14, (10, 9)) as g:
                ssm_units(g, False)
            ssm_units(G - 1, True)
            cross(1)
            for i in range(TT + 1):
                rows = P if i < TT else NB
                sp.wait_ge(y_ready, i + 1)
                dst = outs["y_prompt"][0, i * P:(i + 1) * P, :] if i < TT else outs["y_sample"].rearrange("b s d -> (b s) d")
                sp.dma_start(dst, y_out[0:rows, i % 4, :]).then_inc(y_stored[i % 4], 16)
            for q in range(4):
                sp.wait_ge(y_stored[q], 16 * ((TT + 4 - q) // 4))
            for q in range(2):
                sp.wait_ge(st_stored[q], 64 * G + 1)

        @block.gpsimd
        def _(pool):
            t = Tally()
            zcol = zero[:, 0:1]

            def split_to(raw_ap, hi, lo, width, done):
                pool.tensor_tensor(hi, raw_ap, zcol.to_broadcast([P, width]), ALU.add).then_inc(w_hi_done, 1)
                halves[0] += 1
                pool.wait_ge(w_hi_done, halves[0])
                pool.tensor_tensor(lo, raw_ap, hi.bitcast(F32), ALU.subtract).then_inc(done, 1)

            halves = [0]

            @contextmanager
            def loop(lo, hi, units, results, splits):
                was = halves[0]
                with t.loop(pool, lo, hi, units, results) as i:
                    halves[0] = was + (i - lo if lo else i) * splits
                    yield i
                halves[0] = was + (hi - lo) * splits

            def split(count=1):
                for _ in range(count):
                    s, n = t.unit()
                    pool.wait_ge(w_loaded[s], 16 * n)
                    pool.wait_ge(w_used[s], n)
                    split_to(w_raw[:, s, :], w_hi[:, s, :], w_lo[:, s, :], 1024, w_split[s])

            def cross(l):
                def memory(h):
                    pool.wait_ge(kv_loaded, 32 * (HEADS * l + h + 1))
                    pool.wait_ge(attended, HEADS * l + h + 1)
                    for i in range(2):
                        split_to(kv_raw[:, i, :], kv_hi[:, i, :], kv_lo[:, i, :], 512, kv_split)

                split(2)
                memory(0)
                with loop(0, HEADS - 1, 4, (6, 4), 6) as h:
                    split(3)
                    memory(h + 1)
                    split()
                split(2)

            pool.memset(zero[:, :], 0.0).then_inc(zeroed, 1)
            pool.wait_ge(zeroed, 1)
            with loop(0, 16, 2, (1, 1), 0) as _:
                t.unit()
                t.unit()

            def pool_group(g, first):
                split(2)
                pool.wait_ge(pw_loaded, 16 * (g + 1))
                pool.wait_ge(pw_used, g + 1)
                split_to(pw_raw[:, :], pw_hi[:, :], pw_lo[:, :], 512, pw_split)
                split(2 if first else 4)

            pool_group(0, True)
            with loop(1, 4, 6, (7, 7), 7) as g:
                pool_group(g, False)
            with loop(0, 4, 10, (8, 8), 10) as _:
                split(10)
            split(2)
            cross(0)

            split(3)

            def ssm_group(g, last):
                def sample(q):
                    n = 4 * g + q + 1
                    b = q % 2
                    pool.wait_ge(st_loaded[b], 64 * g + 32 * (q // 2 + 1))
                    pool.wait_ge(g_ready, g + 1)
                    d = g_dab[:, :, 2 * q:2 * q + 2].rearrange("p a b -> p b a")
                    pool.tensor_tensor(st[:, b], st[:, b], d.unsqueeze(3).to_broadcast([P, 2, XT, N]), ALU.mult)\
                        .then_inc(st_part, 1)
                    pool.wait_ge(bc_ready, n)
                    pool.wait_ge(st_read, n)
                    pool.wait_ge(xd_ready, g + 1)
                    for i in range(2):
                        pool.tensor_tensor(bx[:, i], bcs[:, 0, i, :].unsqueeze(1).to_broadcast([P, XT, N]),
                                           xd[:, :, 2 * q + i].unsqueeze(2).to_broadcast([P, XT, N]), ALU.mult)\
                            .then_inc(st_part, 1)
                    pool.wait_ge(st_part, 3 * n)
                    pool.tensor_tensor(st[:, b], st[:, b], bx[:, :], ALU.add).then_inc(st_new, 1)

                split(5)
                for q in range(3):
                    split()
                    sample(q)
                if not last:
                    split()
                sample(3)
                split(4 if last else 5)

            with loop(0, G - 1, 14, (10, 9), 14) as g:
                ssm_group(g, False)
            ssm_group(G - 1, True)
            cross(1)

        @block.tensor
        def _(pe):
            t = Tally()
            ALL = ds(0, T)

            def three(w_h, w_l, m_h, m_l):
                return ((w_h, m_h), (w_h, m_l), (w_l, m_h))

            def take(extra=None):
                s, n = t.unit()
                pe.wait_ge(w_split[s], n)
                marks = [w_used[1 - s]] + ([extra] if extra is not None else [])
                return s, marks

            def begin(a):
                a, r, k = t.next(a)
                pe.wait_ge(moved[a], k)
                return a

            def mark(ins, marks):
                if marks:
                    ins.then_inc(marks.pop(0), 1)

            def project(a, extra=None, wait_k=None):
                s, marks = take(extra)
                begin(a)
                project_part(a, s, marks, range(KT), wait_k)

            def project_part(a, s, marks, ks, wait_k=None):
                for k in ks:
                    if wait_k is not None:
                        pe.wait_ge(lo_ready, wait_k + k + 1)
                    w = slice(k * P, (k + 1) * P)
                    for j, (wt, mv) in enumerate(three(w_hi, w_lo, h_hi, h_lo)):
                        for n in range(NCH):
                            ins = pe.matmul(acc[a][:, n * 512:n * 512 + CH], wt[:, s, w], mv[:, k, n * CH:(n + 1) * CH],
                                            start=(k == 0 and j == 0), stop=(k == KT - 1 and j == 2))
                            if k == KT - 1 and j == 2 and n == NCH - 1:
                                ins.then_inc(result, 1)
                            else:
                                mark(ins, marks)

            def out_project(kb, hi, lo, first=None, sets=(0, 1), by_tile=None):
                wide = 1024 // kb
                if first is not None:
                    pe.wait_ge(*first)
                m = 0
                for i in range(D // wide):
                    s, marks = take()
                    for j in range(wide // P):
                        a = begin(sets[m % 2])
                        m += 1
                        for k in range(kb):
                            if by_tile is not None and m == 1:
                                pe.wait_ge(by_tile[0], by_tile[1] + k + 1)
                            at = k * wide + j * P
                            for q, (wt, mv) in enumerate(three(w_hi, w_lo, hi, lo)):
                                for n in range(NCH):
                                    ins = pe.matmul(acc[a][:, n * 512:n * 512 + CH], wt[:, s, at:at + P],
                                                    mv[:, k, n * CH:(n + 1) * CH],
                                                    start=(k == 0 and q == 0), stop=(k == kb - 1 and q == 2))
                                    if k == kb - 1 and q == 2 and n == NCH - 1:
                                        ins.then_inc(result, 1)
                                    else:
                                        mark(ins, marks)

            def all_moved(a):
                pe.wait_ge(moved[a], t.taken[a] + 1)

            def token_sums(src, into):
                for i in range(TT + 1):
                    rows = P if i < TT else NB
                    ins = pe.matmul(into[0:rows, i:i + 1], src[:, i * P:i * P + rows], one, start=True, stop=True)
                ins.then_inc(summed, 1)

            def spread_scales(n_all, a):
                a = begin(a)
                pe.wait_ge(rstd_ready, n_all)
                for i in range(TT + 1):
                    rows = P if i < TT else NB
                    ins = pe.matmul(acc[a][:, i * P:i * P + rows], rstd[0:rows, i:i + 1].to_broadcast([rows, P]),
                                    ident[0:rows, 0:rows], start=True, stop=True)
                ins.then_inc(result, 1)

            def norm(n_th, rows=None):
                pe.wait_ge(sq_added, 7 * (n_th - 1))
                token_sums(sq_sum, M0)
                spread_scales(scales_at(n_th), 0)
                if rows:
                    rows_out(rows)

            def project_pair(sets, extra=None, wait_k=None):
                s0, marks0 = take(extra)
                begin(sets[0])
                project_part(sets[0], s0, marks0, (0,), wait_k)
                s1, marks1 = take()
                begin(sets[1])
                project_part(sets[1], s1, [], (0,))
                for k in range(1, KT - 2):
                    project_part(sets[0], s0, [], (k,), wait_k)
                    project_part(sets[1], s1, [], (k,))
                project_part(sets[0], s0, [], (KT - 2, KT - 1), wait_k)
                project_part(sets[1], s1, marks1, (KT - 2, KT - 1))

            pe.wait_ge(tables, 16 * 9)
            pe.wait_ge(table_r, 2)
            begin(0)
            pe.transpose(acc[0][:, 0:112], p_in[0:112, 0, :], ident[0:112, 0:112]).then_inc(w_used[0], 1)
            pe.transpose(acc[0][:, 112:208], p_in[0:96, 1, :], ident[0:96, 0:96]).then_inc(result, 1)

            def rows_in(i, n, rows, a):
                pe.wait_ge(x_loaded[i], 16 * n)
                begin(a)
                for k in range(KT):
                    ins = pe.transpose(acc[a][:, k * P:k * P + rows], x_in[0:rows, i, k * P:(k + 1) * P], ident[0:rows, 0:rows])
                ins.then_inc(result, 1)

            rows_in(0, 1, P, 1)
            rows_in(1, 1, P, 0)
            with t.loop(pe, 0, TT // 2, 0, (1, 1)) as m:
                rows_in(0, m + 2, P, 1)
                rows_in(1, m + 2, P, 0)
            rows_in(0, TT // 2 + 2, NB, 1)

            def state_rows(src, rows, lo, a):
                begin(a)
                for i in range(lo, lo + 8):
                    ins = pe.transpose(acc[a][:, (i - lo) * P:(i - lo) * P + rows], src[0:rows, i * P:(i + 1) * P],
                                       ident[0:rows, 0:rows])
                ins.then_inc(result, 1)

            pe.wait_ge(st_rows_in, 32)
            state_rows(st_rows, NB * POOL_BUF, 0, 0)
            state_rows(cst_rows, NB * 2, 0, 1)

            pe.wait_ge(sq1_added, TT + 1)
            token_sums(sq_sum, M0)
            spread_scales(1, 0)

            all_moved(0)
            all_moved(1)

            def memory_tile(a):
                s, marks = take()
                begin(a)
                for k in range(KT):
                    w = slice(k * P, (k + 1) * P)
                    for j, (wt, mv) in enumerate(three(w_hi, w_lo, m_hi, m_lo)):
                        ins = pe.matmul(acc[a][:, 0:NM], wt[:, s, w], mv[:, k, :],
                                        start=(k == 0 and j == 0), stop=(k == KT - 1 and j == 2))
                        mark(ins, marks)
                ins.then_inc(result, 1)

            def memory_rows(s, n):
                all_moved(s)
                pe.wait_ge(kv_nat, n)
                for i in range(MT):
                    ins = pe.transpose(MS[s][:, i * P:(i + 1) * P], kt_out[:, s, i * P:(i + 1) * P], ident)
                ins.then_inc(kv_turned, 1)

            memory_tile(0)
            memory_tile(1)
            memory_rows(0, 1)
            with t.loop(pe, 1, 16, 2, (1, 1)) as i:
                memory_tile(0)
                memory_rows(1, 2 * i - 1)
                memory_tile(1)
                memory_rows(0, 2 * i)
            memory_rows(1, 31)

            def pool_products(g):
                for i in range(2):
                    a = begin(i)
                    if i == 0:
                        pe.wait_ge(pw_split, g + 1)
                        pe.wait_ge(d_ready, 2 * g + 2)
                    for k in range(2):
                        at = k * 256 + i * P
                        for j, (wt, mv) in enumerate(three(pw_hi, pw_lo, d_hi, d_lo)):
                            for n in range(NCH):
                                ins = pe.matmul(acc[a][:, n * 512:n * 512 + CH], wt[:, at:at + P],
                                                mv[:, k, n * CH:(n + 1) * CH],
                                                start=(k == 0 and j == 0), stop=(k == 1 and j == 2))
                    ins.then_inc(result, 1)

            project_pair((0, 1), pw_used, 0)
            project(0)
            project(1)
            pool_products(0)
            with t.loop(pe, 1, 4, 6, (7, 7)) as g:
                project(0, pw_used)
                for a in (1, 0, 1):
                    project(a)
                out_project(2, y_hi, y_lo, (y_ready2, 2 * g))
                pool_products(g)
            with t.loop(pe, 0, 4, 10, (8, 8)) as g:
                project(0)
                project(1)
                project(0)
                out_project(2, y_hi, y_lo, (y_ready2, 2 * g + 8), (1, 0))
                for a in (1, 0, 1, 0, 1):
                    project(a)
            out_project(2, y_hi, y_lo, (y_ready2, 16))

            def rows_out(parts):
                begin(1)
                for n, (src, width, lo) in enumerate(parts):
                    for i in range(KT):
                        ins = pe.matmul(acc[1][32 * n:32 * n + width, i * P:(i + 1) * P], src[:, lo + i, :], ident,
                                        start=True, stop=True)
                ins.then_inc(result, 1)

            def attention(l, h, last):
                n = HEADS * l + h
                turned = [acc[1][:, 0:NM], acc[1][:, 512:512 + NM]]
                mixed = acc[1][:, 1024:1536]
                unit = [0]

                def queries(i, ks, extra=None):
                    if last:
                        return
                    marks = []
                    if ks[0] == 0:
                        unit[0], marks = take()
                        begin(0)
                    if extra is not None:
                        marks = [extra]
                    project_part(0, unit[0], marks, ks)

                def spread(r):
                    if r >= 2:
                        pe.wait_ge(qbc_ready, 4 * n + r - 1)
                    for b in range(2):
                        for k in range(2):
                            at = b * HD + k * P
                            for j, src in enumerate((q_hi, q_lo)):
                                ins = pe.matmul(MS[r % 2][:, at:at + P],
                                                src[:, k, TP + 2 * r + b:TP + 2 * r + b + 1].to_broadcast([P, P]), ident_r,
                                                start=(j == 0), stop=(j == 1))
                    ins.then_inc(qbc_done, 1)

                def scores(i):
                    if i >= 2:
                        pe.wait_ge(exped, 8 * n + i - 1)
                    else:
                        pe.wait_ge(qbc_ready, 4 * n + 3 + i)
                    for k in range(2):
                        for j, (a, b) in enumerate(three(q_hi, q_lo, kv_hi, kv_lo)):
                            ins = pe.matmul(MS[i % 2][:, 0:NM], a[:, k, i * P:(i + 1) * P], b[:, 0, k * NM:(k + 1) * NM],
                                            start=(k == 0 and j == 0), stop=(k == 1 and j == 2))
                    ins.then_inc(scored, 1)

                def turn(i):
                    pe.wait_ge(prob_ready, 8 * n + i + 1)
                    if i >= 2:
                        pe.wait_ge(pt_ready, 8 * n + i - 1)
                    for j in range(MT):
                        ins = pe.transpose(turned[i % 2][:, j * P:(j + 1) * P], prob[:, i % 2, j * P:(j + 1) * P], ident)
                    ins.then_inc(prob_turned, 1)

                def mix(half, k):
                    pe.wait_ge(pt_ready, 8 * n + 4 * half + 4)
                    if half or k:
                        pe.wait_ge(mixed_out, 4 * n + 2 * half + k)
                    for m in range(MT):
                        for j, (a, b) in enumerate(three(kv_hi, kv_lo, pt_hi, pt_lo)):
                            at = m * HD + k * P
                            ins = pe.matmul(mixed, a[:, 1, at:at + P], b[:, m, :],
                                            start=(m == 0 and j == 0), stop=(m == 1 and j == 2))
                    ins.then_inc(mix_done, 1)

                pe.wait_ge(kv_split, 2 * n + 2)
                all_moved(0)
                all_moved(1)
                spread(0)
                spread(1)
                queries(0, (0,))
                spread(2)
                spread(3)
                for i in range(TT + 2):
                    if i < TT:
                        scores(i)
                    if i == 6:
                        mix(0, 0)
                        queries(0, (7,))
                        mix(0, 1)
                    if i >= 2:
                        turn(i - 2)
                    if i < 6:
                        queries(0, (i + 1,))
                    elif i >= TT:
                        queries(1, (2 * i - 16, 2 * i - 15))
                mix(1, 0)
                queries(1, (4,))
                mix(1, 1)
                queries(1, (5,), attended)
                pe.wait_ge(ss_ready, n + 1)
                for m in range(MT):
                    ins = pe.transpose(M0[0:NB, m * P:(m + 1) * P], ss[:, m, :], ident)
                ins.then_inc(ss_turned, 1)
                queries(1, (6,))
                pe.wait_ge(sp_ready, n + 1)
                for m in range(MT):
                    ins = pe.matmul(M1[:, m * NB:(m + 1) * NB], sp[0:NB, m * P:(m + 1) * P], ident[0:NB, 0:NB],
                                    start=True, stop=True)
                ins.then_inc(sp_turned, 1)
                pe.wait_ge(spt_ready, n + 1)
                pe.wait_ge(v_loaded, 16 * n + 16)
                for b in range(NB):
                    for m in range(MT):
                        ins = pe.matmul(M0[0:NB, 0:HD], spt[:, m, b * NB:(b + 1) * NB], cache[:, b * MT + m, :],
                                        start=(b == 0 and m == 0), stop=(b == NB - 1 and m == MT - 1))
                ins.then_inc(smix_done, 1)
                queries(1, (7,))
                pe.wait_ge(so_ready, n + 1)
                for k in range(2):
                    ins = pe.matmul(M1[:, k * NB:(k + 1) * NB], sp[0:NB, k * P:(k + 1) * P], ident[0:NB, 0:NB],
                                    start=True, stop=True)
                ins.then_inc(so_turned, 1)
                pe.wait_ge(mixed_out, 4 * n + 4)
                out_project(2, y_hi, y_lo, (xy_ready, n + 1), (0, 1) if last else (1, 0))

            def cross(l, n_th, rows):
                norm(n_th, rows)
                project_pair((0, 1), attended, KT * (n_th - 1))
                with t.loop(pe, 0, HEADS - 1, 4, (6, 4)) as h:
                    attention(l, h, False)
                attention(l, HEADS - 1, True)

            cross(0, 2, ((u_keep, 23, 0), (c_keep, 10, 0)))

            norm(3)
            pe.wait_ge(sc_loaded, 16)
            for i in range(3):
                state_rows(sc_rows, 24, 8 * i, i % 2)
            project_pair((0, 1), None, 2 * KT)
            s, marks = take()
            begin(0)
            project_part(0, s, marks, range(0, 4))
            pe.wait_ge(dt_padded, 1)
            for i in range(TT + 1):
                ins = pe.transpose(M0[:, i * 32:(i + 1) * 32], dt_rows[96:128, i * P:(i + 1) * P], ident[96:128, 96:128])
            ins.then_inc(dt_done, 1)
            project_part(0, s, marks, range(4, KT))
            pe.wait_ge(dta_ready, 1)
            pe.matmul(M1[:, 0:256], tri, dta[:, 0:TT, :].rearrange("p c h -> p (c h)"), start=True, stop=True).then_inc(acs_done, 1)
            for j, src in enumerate((dt_all, dta)):
                for i in range(16):
                    at = j * P + i * NB
                    for half in range(2):
                        head = 2 * i + half
                        ins = pe.matmul(M0[64 * half:64 * half + 64, at:at + NB],
                                        src[0:NB, TT, head:head + 1].to_broadcast([NB, 64]),
                                        ident[0:NB, 0:NB], start=True, stop=True)
            ins.then_inc(dtb_done, 1)

            def ssm_group(g, last):
                def first_stage(c):
                    n = 8 * g + c
                    cs = slice(c * P, (c + 1) * P)
                    if c == 0:
                        pe.wait_ge(conved, 6 * g + 6)
                        pe.wait_ge(g_ready, g + 1)
                        all_moved(1)
                    else:
                        pe.wait_ge(y_back, n)
                        if c % 2:
                            pe.wait_ge(bc_ready, 4 * g + c // 2 + 1)
                    for i in range(XT):
                        ins = pe.transpose(M0[:, i * P:(i + 1) * P], xb[:, i, cs], ident)
                    ins.then_inc(x_turned, 1)
                    if c:
                        pe.wait_ge(mm_ready, n)
                    pe.matmul(M1[:, 0:P], bc[:, 0, cs], bc[:, 1, cs], start=True, stop=True)
                    pe.transpose(M1[:, P:2 * P], bc[:, 0, cs], ident).then_inc(cb_done, 1)
                    if c:
                        pe.wait_ge(s_ready, 9 * g + c + 1)
                    for q in range(2):
                        pe.matmul(acc[1][:, q * 512:(q + 1) * 512], ident_r, mask_r, start=True, stop=False,
                                  skip_group_check=True)
                        for e in range(4 * q, 4 * q + 4):
                            for j, src in enumerate((g_dhi, g_dlo)):
                                ins = pe.matmul(acc[1][:, e * P:(e + 1) * P], src[:, c, e:e + 1].to_broadcast([P, P]), tri_r,
                                                start=False, stop=(e % 4 == 3 and j == 1), skip_group_check=True)
                    ins.then_inc(a_spread, 1)
                    pe.wait_ge(s_ready, 9 * g + c + 1)
                    pe.matmul(acc[1][:, 1024:1536], bc[:, 1, cs], S[:, :], start=True, stop=True).then_inc(yoff_done, 1)

                def second_stage(c):
                    n = 8 * g + c + 1
                    pe.wait_ge(mm_ready, n)
                    pe.wait_ge(xdt_ready, n)
                    for e in range(E):
                        ins = pe.matmul(acc[1][:, e * 64:(e + 1) * 64], dec[:, e, :], xdt[:, e * 64:(e + 1) * 64],
                                        start=True, stop=True)
                    ins.then_inc(ydiag_done, 1)
                    pe.wait_ge(xde_ready, n)
                    pe.wait_ge(bnat_ready, n)
                    pe.matmul(acc[1][:, 512:1024], b_nat[:, :], xde[:, :], start=True, stop=True).then_inc(s_done, 1)

                def third_stage(c):
                    n = 8 * g + c + 1
                    pe.wait_ge(ynat_ready, n)
                    for i in range(XT):
                        ins = pe.transpose(M0[:, i * P:(i + 1) * P], y_nat[:, i * P:(i + 1) * P], ident)
                    ins.then_inc(y_turned, 1)

                def sample_spread(q):
                    pe.wait_ge(y_back, 8 * g + 2 * q + 1)
                    for j in range(2):
                        for b in range(2):
                            at = (2 * j + b) * P
                            ins = pe.matmul(M0[:, at:at + P], bc[:, j, TP + 2 * q + b:TP + 2 * q + b + 1].to_broadcast([P, P]),
                                            ident, start=True, stop=True)
                    ins.then_inc(bc_spread, 1)

                for a in (1, 0, 1, 0, 1):
                    project(a)
                fills = ((2, 0, 1), (2, 0, 1), (2, 0, 0), (2, 0, 1), (2, 0, 1), (2, 0, 0), (2, 1, 1), (2, 1, 1))
                k = KT
                for c in range(TT):
                    if k == KT:
                        k = 0
                    at = [k, k + fills[c][0], k + fills[c][0] + fills[c][1]]
                    first_stage(c)
                    if k == 0:
                        s, marks = take()
                        begin(0)
                    project_part(0, s, marks, range(at[0], at[1]))
                    second_stage(c)
                    project_part(0, s, marks, range(at[1], at[2]))
                    third_stage(c)
                    k += sum(fills[c])
                    project_part(0, s, marks, range(at[2], k))
                    if c % 2 == 0:
                        sample_spread(c // 2)
                pe.wait_ge(s_ready, 9 * g + 9)
                pe.wait_ge(y_back, 8 * g + 8)
                for i in range(XT):
                    ins = pe.transpose(M0[:, i * P:(i + 1) * P], S[:, i * P:(i + 1) * P], ident)
                ins.then_inc(s_turned, 1)
                if not last:
                    pe.wait_ge(ynat_ready, 8 * g + 8)
                    project(1)
                pe.wait_ge(t_added, XT * g + XT)
                pe.wait_ge(s_out_ready, g + 1)
                token_sums(t_sum, M1)
                if not last:
                    s, marks = take()
                    begin(0)
                    project_part(0, s, marks, (0, 1))
                spread_scales(g + 4, 1)
                if not last:
                    project_part(0, s, [], range(2, KT))
                out_project(4, o_hi, o_lo, sets=(0, 1) if last else (1, 0), by_tile=(o_ready, XT * g))

            with t.loop(pe, 0, G - 1, 14, (10, 9)) as g:
                ssm_group(g, False)
            ssm_group(G - 1, True)
            cross(1, 4, [(s_keep, 11, 8 * i) for i in range(3)])
            norm(5)
            for i in range(TT + 1):
                rows = P if i < TT else NB
                if i < 2:
                    a = begin(i % 2 ^ 1)
                    pe.wait_ge(fin_ready, KT)
                else:
                    a, _, _ = t.next(i % 2 ^ 1)
                    pe.wait_ge(y_ready, i - 1)
                for k in range(KT):
                    ins = pe.transpose(acc[a][0:rows, k * P:(k + 1) * P], x[:, k, i * P:i * P + rows], ident)
                ins.then_inc(result, 1)

        @block.scalar
        def _(act):
            t = Tally()

            def copy(out, in_, done):
                return act.activation(out, in_, ACT.Copy).then_inc(done, 1)

            def root(bank, n_all, n):
                act.wait_ge(summed, n_all)
                act.activation(sd[:, 0:TT], bank[:, 0:TT], ACT.Sqrt, bias=eps, scale=1.0 / n).then_inc(root_ready, 1)
                act.activation(sd[0:NB, TT:TT + 1], bank[0:NB, TT:TT + 1], ACT.Sqrt, bias=eps[0:NB], scale=1.0 / n)\
                    .then_inc(root_ready, 1)

            def scales_in(where, dst):
                a, r, _ = where
                act.wait_ge(result, r)
                copy(dst[:, :], acc[a][:, 0:T], moved[a])

            act.dma_start(st_rows[0:NB * POOL_BUF, :], ins["state_pool"][0].rearrange("b t c -> (b t) c")).then_inc(st_rows_in, 16)
            act.dma_start(cst_rows[0:NB * 2, :], ins["state_conv"][0].rearrange("b t c -> (b t) c")).then_inc(st_rows_in, 16)
            act.dma_start(outs["pool_sample"][0, :, 0:POOL_BUF - 1, :], ins["state_pool"][0, :, 1:POOL_BUF, :]).then_inc(stored, 16)
            act.dma_start(outs["conv_sample"][0, :, 0:1, :], ins["state_conv"][0, :, 1:2, :]).then_inc(stored, 16)
            act.dma_start(outs["ssm_conv_sample"][0, :, 0:2, :], ins["state_ssm_conv"][0, :, 1:3, :]).then_inc(stored, 16)
            act.wait_ge(tables, 16 * 9)
            copy(table[:, :], table_in[:, 0:C_INV], table_r)
            copy(cst[:, :], table_in[:, C_INV:C_N], table_r)
            t.next(0)

            for i in range(MT):
                a, r, _ = t.next((i + 1) % 2)
                act.wait_ge(result, r)
                copy(m_hi[:, :, i * P:(i + 1) * P], acc[a][:, 0:1024].rearrange("p (k m) -> p k m", k=KT), m_hi_ready)
            for i in range(TT + 1):
                rows = P if i < TT else NB
                a, _, k = t.next((i + 1) % 2)
                act.wait_ge(moved[a], k + 1)
                if i >= 2:
                    act.wait_ge(sq1_added, i - 1)
                act.activation(sq[:, i % 2, 0:KT * rows].rearrange("p (k t) -> p k t", k=KT), x[:, :, i * P:i * P + rows],
                               ACT.Square).then_inc(sq1_ready, 1)
            t.next(0)
            t.next(1)
            root(M0, 1, D)
            scales_in(t.next(0), sq_sum)

            def hi_half(s, n):
                act.wait_ge(w_loaded[s], 16 * n)
                act.wait_ge(w_used[s], n)
                copy(w_hi[:, s, :], w_raw[:, s, :], mw_hi_done)

            def memory_pair(row, i, first, keys, n, last=False):
                for s in range(2):
                    a, r, _ = t.next(s)
                    act.wait_ge(result, r)
                    if not first:
                        act.wait_ge(kt_stored[s], row)
                    copy(kt_out[:, s, :], acc[a][:, 0:NM], moved[a])
                    if keys is not None:
                        act.wait_ge(moved[a], t.taken[a] + 1)
                        act.dma_start(keys[ds(2 * i + s, 1)].rearrange("a p m -> (a p) m"), kt_out[:, s, :]).then_inc(kt_stored[s], 16)
                    if not last:
                        hi_half(s, n + 2)

            hi_half(0, 1)
            hi_half(1, 1)
            for l in range(2):
                keys = scratch[l].rearrange("(j p) m -> j p m", p=P)
                if l == 0:
                    memory_pair(0, 0, True, keys, 0)
                with t.loop(act, 1 - l, 4, 2, (1, 1)) as i:
                    memory_pair(64 * l + 16 * i if l == 0 else 64 + 16 * i, i, False, keys, 8 * l + i)
                with t.loop(act, 0, 4 - l, 2, (1, 1)) as i:
                    memory_pair(64 * (l + 1), i, False, None, 8 * l + 4 + i)
                if l:
                    memory_pair(128, 3, False, None, 15, True)
                for j, name in enumerate(("mem_k", "mem_v")):
                    act.wait_ge(kv_nat, 16 * l + 8 * j + 9)
                    act.dma_start(outs[name][l, 0].rearrange("(m p) h d -> p m (h d)", p=P), kv_nat_sb[:, j]).then_inc(kv_stored[j], 16)

            def hi_halves(n_th, rows=None):
                for j in range(KT):
                    act.wait_ge(h32_ready, 8 * (n_th - 1) + j + 1)
                    copy(h_hi[:, j, :], h32[:, j % 2, :], hi_ready)
                    if j == 0 and rows:
                        rows()

            def norm(n_th, waits, split=True, rows=None):
                for j in range(KT):
                    if waits:
                        act.wait_ge(*waits[j])
                    if j >= 2:
                        act.wait_ge(sq_added, 7 * (n_th - 2) + j - 1)
                    act.activation(sq[:, j % 2, :], x[:, j, :], ACT.Square).then_inc(sq_ready, 1)
                root(M0, scales_at(n_th), D)
                scales_in(t.next(0), sq_sum)
                if split:
                    hi_halves(n_th, rows)

            def out_chunk():
                for m in range(KT):
                    t.next(m % 2)

            def x_tiles():
                base = [t.taken[0] - 4, t.taken[1] - 4]
                return [(moved[j % 2], base[j % 2] + j // 2 + 2) for j in range(KT)]

            hi_halves(1)
            for s in range(2):
                act.wait_ge(kt_stored[s], 128)
                act.wait_ge(kv_stored[s], 32)

            def pool_group(g, first):
                for i in range(2):
                    a, r, _ = t.next(i)
                    act.wait_ge(result, r)
                    if not first:
                        act.wait_ge(d_ready, 2 * g)
                    copy(t3(u_pad[:, i, WARM:WARM + T]), a3(a), moved[a])
                    act.wait_ge(d32_ready, 2 * g + i + 1)
                    copy(d_hi[:, i, :], y32[:, :], d_hi_ready)
                for i in range(2):
                    a, r, _ = t.next(i)
                    act.wait_ge(result, r)
                    act.activation(t3(gate[:, i, :]), a3(a), ACT.Silu).then_inc(moved[a], 1)
                if not first:
                    out_chunk()
                for i in range(2):
                    t.next(i)
                    act.wait_ge(moved[i], t.taken[i] + 1)
                    copy(y_hi[:, i, :], y32[:, :], y_hi_ready)

            pool_group(0, True)
            with t.loop(act, 1, 4, 6, (7, 7)) as g:
                pool_group(g, False)

            def conv_pair(g):
                for i in range(2):
                    a, r, _ = t.next(0)
                    act.wait_ge(result, r)
                    act.wait_ge(cv_ready, 2 * g + i + 1)
                    copy(t3(c_sb[:, :]), a3(a), moved[a])
                    t.next(1)
                    a, r, _ = t.next(0)
                    act.wait_ge(result, r)
                    act.activation(t3(c_gate[:, i, :]), a3(a), ACT.Silu).then_inc(moved[a], 1)
                    if i == 0:
                        for m in range(KT):
                            t.next((m + 1) % 2)
                    t.next(1)
                    act.wait_ge(cy32_ready, 2 * g + i + 1)
                    copy(y_hi[:, i, :], cy32[:, i, :], y_hi_ready)

            act.wait_ge(y_ready2, 8)
            with t.loop(act, 0, 4, 10, (8, 8)) as g:
                conv_pair(g)
            out_chunk()
            waits = x_tiles()
            def rows_from(parts):
                a, r, _ = t.next(1)
                act.wait_ge(result, r)
                for n, (width, _) in enumerate(parts):
                    q = slice(32 * n, 32 * n + width)
                    copy(row_out[q, :], acc[a][q, 0:D], moved[a] if n == len(parts) - 1 else rows_copied)
                act.wait_ge(moved[a], t.taken[a] + 1)
                for n, (_, dsts) in enumerate(parts):
                    for dst, lo, hi in dsts:
                        act.dma_start(dst, row_out[32 * n + lo:32 * n + hi, :]).then_inc(stored, 16)

            def mixer_rows():
                rows_from(((23, ((outs["pool_prompt"][0, 0], 0, 15), (outs["pool_sample"][0, :, 14, :], 15, 23))),
                           (10, ((outs["conv_prompt"][0, 0], 0, 2), (outs["conv_sample"][0, :, 1, :], 2, 10)))))

            def cross(l, n_th, waits, rows):
                norm(n_th, waits, rows=rows)
                act.wait_ge(stored, 16 * (7 if l == 0 else 13))
                kt = scratch[l].rearrange("(a p) m -> p a m", p=P)
                vn = outs["mem_v"][l, 0].rearrange("(a p) h d -> p a h d", p=P)
                ck = ins["cache_mem_k"][l].rearrange("b (m p) h d -> p (b m) h d", p=P)
                cv_ = ins["cache_mem_v"][l].rearrange("b (m p) h d -> p (b m) h d", p=P)

                def load_memory(h):
                    act.dma_start(kv_raw[:, 0, :].rearrange("p (a m) -> p a m", a=2), kt[:, ds(2 * h, 2), :]).then_inc(kv_loaded, 16)
                    act.dma_start(kv_raw[:, 1, :].rearrange("p (a d) -> p a d", a=2),
                                  vn[:, :, ds(h, 1), :].rearrange("p a h d -> p a (h d)")).then_inc(kv_loaded, 16)

                def load_cache(src, h, done):
                    act.dma_start(cache[:, :, :], src[:, :, ds(h, 1), :].rearrange("p b h d -> p b (h d)")).then_inc(done, 16)

                def queries(i, a):
                    a, r, _ = t.next(a)
                    act.wait_ge(result, r)
                    copy(t3(q_hi[:, i, :]), a3(a), q_hi_ready)

                def attention(h, last):
                    n = HEADS * l + h
                    for r in range(4):
                        act.wait_ge(qbc_done, 4 * n + r + 1)
                        copy(q_bc[:, 2 * r:2 * r + 2, :], MS[r % 2][:, :].rearrange("p (b d) -> p b d", b=2), qbc_ready)

                    def mix_out(half):
                        for k in range(2):
                            act.wait_ge(mix_done, 4 * n + 2 * half + k + 1)
                            copy(y_hi[:, k, half * 512:half * 512 + 512], acc[1][:, 1024:1536], y_hi_ready)

                    for i in range(TT + 2):
                        if i == 6:
                            mix_out(0)
                        if i < TT:
                            if i >= 2:
                                act.wait_ge(prob_turned, 8 * n + i - 1)
                            act.wait_ge(nmx_ready, 8 * n + i + 1)
                            act.activation(prob[:, i % 2, :], MS[i % 2][:, 0:NM], ACT.Exp,
                                           bias=nmx[:, i:i + 1], scale=HD ** -0.5, accum_out=rsum[:, i:i + 1]).then_inc(exped, 1)
                        if i == 0 and not last:
                            act.wait_ge(kv_split, 2 * n + 2)
                            load_memory(h + 1)
                        if i >= 2:
                            j = i - 2
                            act.wait_ge(prob_turned, 8 * n + j + 1)
                            if j >= 4:
                                act.wait_ge(mix_done, 4 * n + 2)
                            copy(pt_hi[:, :, (j % 4) * P:(j % 4 + 1) * P],
                                 acc[1][:, (j % 2) * 512:(j % 2) * 512 + NM].rearrange("p (m t) -> p m t", m=2), pt_hi_ready)
                        if i == TT - 1 and not last:
                            queries(0, 0)
                        if i == TT:
                            act.wait_ge(ss_ready, n + 1)
                            load_cache(cv_, h, v_loaded)
                    mix_out(1)
                    act.wait_ge(snmx_ready, n + 1)
                    act.activation(sp[0:NB, :], M0[0:NB, 0:NM], ACT.Exp, bias=s4[0:NB, 1:2], scale=HD ** -0.5,
                                   accum_out=s4[0:NB, 2:3]).then_inc(s_exped, 1)
                    act.wait_ge(smix_done, n + 1)
                    copy(sp[0:NB, :], M0[0:NB, 0:HD], so_ready)
                    if not last:
                        load_cache(ck, h + 1, k_loaded)
                        queries(1, 0)
                    act.wait_ge(so_turned, n + 1)
                    copy(y_hi[:, :, TP:T], M1[:, 0:2 * NB].rearrange("p (k b) -> p k b", k=2), sy_hi_ready)

                load_memory(0)
                act.wait_ge(lo_ready, 8 * n_th)
                load_cache(ck, 0, k_loaded)
                queries(0, 0)
                queries(1, 1)
                with t.loop(act, 0, HEADS - 1, 4, (6, 4)) as h:
                    attention(h, False)
                    for m in range(KT):
                        t.next((m + 1) % 2)
                attention(HEADS - 1, True)
                out_chunk()

            cross(0, 2, waits, mixer_rows)

            waits = x_tiles()
            act.dma_start(bias_bc[:, 0, :], ins["dt_bias"].partition_broadcast(P).rearrange("p a h -> p (a h)")).then_inc(dp_loaded, 16)
            act.dma_start(bias_bc[:, 1, :], ins["a_log"].partition_broadcast(P).rearrange("p a h -> p (a h)")).then_inc(dp_loaded, 16)
            act.dma_start(sc_rows[0:24, :], ins["state_ssm_conv"][0].rearrange("b t c -> (b t) c")).then_inc(sc_loaded, 16)
            act.dma_start(bias_bc[:, 2, :], ins["d_skip"].partition_broadcast(P).rearrange("p a h -> p (a h)")).then_inc(dp_loaded, 16)
            norm(3, waits)
            for i in range(3):
                t.next(i % 2)
            a, r, _ = t.next(0)
            act.wait_ge(result, r)
            copy(t3(dt_rows[96:128, 0:T]), a3(a)[96:128], moved[a])

            def conv_in(a, n):
                a, r, _ = t.next(a)
                act.wait_ge(result, r)
                act.wait_ge(tapped, n)
                copy(t3(raw[:, 3:3 + T]), a3(a), moved[a])

            def conv_finish(dst, bias_col, n):
                act.wait_ge(tapped, n + 1)
                act.activation(dst, dst, ACT.Silu, bias=g_prm[:, bias_col:bias_col + 1]).then_inc(conved, 1)

            def conv_tile(a, dst, bias_col, n):
                conv_in(a, n)
                conv_finish(dst, bias_col, n)

            conv_in(1, 1)
            act.wait_ge(dp_loaded, 48)
            act.activation(bias_bc[:, 1, :], bias_bc[:, 1, :], ACT.Exp).then_inc(a_ready, 1)
            act.wait_ge(dtx_ready, 1)
            act.activation(dte[:, :, :], dtx[:, :, :], ACT.Abs).then_inc(dt_step, 1)
            act.wait_ge(dt_step, 1)
            act.activation(dte[:, :, :], dte[:, :, :], ACT.Exp, scale=-1.0).then_inc(dt_step, 1)
            act.wait_ge(dt_step, 2)
            act.activation(dtl[:, :, :], dte[:, :, :], ACT.Ln, bias=one).then_inc(dt_step, 1)
            act.wait_ge(dta_ready, 1)
            copy(dta_hi[:, :, :], dta[:, 0:TT, :], dhi_ready)
            act.wait_ge(acs_done, 1)
            act.activation(acs_e[:, :, :], M1[:, 0:256].rearrange("p (c h) -> p c h", c=TT), ACT.Exp).then_inc(acs_e_ready, 1)
            act.wait_ge(dtb_done, 1)
            act.activation(dab[:, :, :], M0[:, P:2 * P].rearrange("p (a b) -> p a b", b=NB), ACT.Exp).then_inc(dab_ready, 1)
            conv_finish(bc[:, 0, :], 36, 1)
            conv_tile(0, bc[:, 1, :], 37, 2)

            def ssm_group(g, last):
                def chunk(c):
                    n = 8 * g + c + 1
                    act.wait_ge(cb_done, n)
                    copy(b_nat[:, :], M1[:, P:2 * P], bnat_ready)
                    act.wait_ge(a_spread, n)
                    if c:
                        act.wait_ge(ydiag_done, n - 1)
                    copy(aend[:, :], acc[1][:, P - 1:1024:P], aend_ready)
                    for e in range(E):
                        ins = act.activation(dec[:, e, :], acc[1][:, e * P:(e + 1) * P], ACT.Exp, bias=g_acn[:, c, e:e + 1])
                    ins.then_inc(dec_ready, 1)
                    act.wait_ge(aend_ready, n)
                    act.activation(cdec[:, :], aend[:, :], ACT.Exp).then_inc(cdec_ready, 1)
                    act.wait_ge(te_ready, n)
                    act.activation(toe[:, :], te[:, :], ACT.Exp).then_inc(toe_ready, 1)

                def z_in(i):
                    a, r, _ = t.next(0 if i else 1)
                    act.wait_ge(result, r)
                    act.activation(t3(zb[:, i, :]), a3(a), ACT.Silu).then_inc(moved[a], 1)

                for i, a in enumerate((1, 0, 1, 0)):
                    conv_tile(a, xb[:, i, :], 16 + i, 6 * g + 3 + i)
                z_in(0)
                for c in range(TT):
                    chunk(c)
                    if c in (2, 5, 7):
                        z_in({2: 1, 5: 2, 7: 3}[c])
                    if c % 2 == 0:
                        act.wait_ge(bc_spread, 4 * g + c // 2 + 1)
                        act.wait_ge(st_read, 4 * g + c // 2 + 1)
                        copy(bcs[:, :, :, :], M0[:, :].rearrange("p (j b n) -> p j b n", j=2, b=2), bc_ready)
                act.wait_ge(s_turned, g + 1)
                act.wait_ge(s_stored, 16 * g + 1)
                copy(s_out[:, :], M0[:, :], s_out_ready)
                act.wait_ge(s_out_ready, g + 1)
                act.dma_start(outs["ssm_prompt"][0, 0].rearrange("h p n -> (h p) n").rearrange("(a p) n -> p a n", p=P)[:, ds(XT * g, XT), :],
                              s_out[:, :].rearrange("p (a n) -> p a n", a=XT)).then_inc(s_stored, 16)
                for i in range(XT):
                    act.wait_ge(yz_ready, XT * g + i + 1)
                    if i:
                        act.wait_ge(t_added, XT * g + i)
                    act.activation(t_sq[:, :], xb[:, i, :], ACT.Square).then_inc(t_sq_ready, 1)
                if not last:
                    conv_in(1, 6 * g + 7)
                root(M1, g + 4, XT * P)
                if not last:
                    conv_finish(bc[:, 0, :], 36, 6 * g + 7)
                scales_in(t.next(1), t_sum)
                for i in range(XT):
                    act.wait_ge(yn_ready, XT * g + i + 1)
                    copy(o_hi[:, i, :], xb[:, i, :], o_hi_ready)
                if not last:
                    conv_tile(0, bc[:, 1, :], 37, 6 * g + 8)
                for m in range(KT):
                    t.next(m % 2 if last else (m + 1) % 2)

            with t.loop(act, 0, G - 1, 14, (10, 9)) as g:
                ssm_group(g, False)
            ssm_group(G - 1, True)
            waits = x_tiles()
            for q in range(2):
                act.wait_ge(st_stored[q], 64 * G + 1)
            act.wait_ge(s_stored, 16 * G + 1)
            def conv_rows():
                rows_from([(11, ((outs["ssm_conv_prompt"][0, 0, :, i * D:(i + 1) * D], 0, 3),
                                 (outs["ssm_conv_sample"][0, :, 2, i * D:(i + 1) * D], 3, 11))) for i in range(3)])

            cross(1, 4, waits, conv_rows)
            norm(5, x_tiles(), split=False)
            for i in range(TT + 1):
                a, r, _ = t.next(i % 2 ^ 1)
                rows = P if i < TT else NB
                act.wait_ge(result, r)
                if i >= 4:
                    act.wait_ge(y_stored[i % 4], 16 * (i // 4))
                act.activation(y_out[0:rows, i % 4, :], acc[a][0:rows, 0:D], ACT.Copy).then_inc(y_ready, 1)
            act.wait_ge(stored, 16 * (3 + 10))
            act.wait_ge(s_stored, 16 * G + 1)

        @block.vector
        def _(dve):
            t = Tally()
            steps, made = [0], [0]

            def step(ins):
                ins.then_inc(dve_step, 1)
                steps[0] += 1
                made[0] += 1
                dve.wait_ge(dve_step, steps[0])

            @contextmanager
            def loop(lo, hi, units, results, per):
                was, made[0] = steps[0], 0
                with t.loop(dve, lo, hi, units, results) as i:
                    steps[0] = was + (i - lo if lo else i) * per
                    yield i
                    assert made[0] == per, made
                steps[0] = was + (hi - lo) * per

            def prm_col(c):
                return prm[:, c:c + 1]

            step(dve.memset(sd[:, :], 1.0))
            for i, s in enumerate((moved[0], moved[1], kv_nat, cv_ready, tapped, st_read, st_stored[0], st_stored[1], s_stored)):
                dve.memset(credit[:, i:i + 1], 0.0).then_inc(s, 1)
            _, r, _ = t.next(0)
            dve.wait_ge(result, r)
            dve.tensor_copy(prm[:, :], acc[0][:, 0:PRM_N]).then_inc(moved[0], 1)
            dve.wait_ge(moved[0], 2)
            for i in range(MT):
                a, r, _ = t.next((i + 1) % 2)
                dve.wait_ge(m_hi_ready, i + 1)
                at = slice(i * P, (i + 1) * P)
                dve.tensor_tensor(m_lo[:, :, at], acc[a][:, 0:1024].rearrange("p (k m) -> p k m", k=KT),
                                  m_hi[:, :, at].bitcast(F32), ALU.subtract).then_inc(moved[a], 1)
            def square_sum(i):
                rows = P if i < TT else NB
                dve.wait_ge(sq1_ready, i + 1)
                dve.tensor_reduce(sq_sum[:, i * P:i * P + rows], sq[:, i % 2, 0:KT * rows].rearrange("p (k t) -> p t k", k=KT),
                                  AX, ALU.add).then_inc(sq1_added, 1)

            for i in range(TT + 1):
                rows = P if i < TT else NB
                a, r, _ = t.next((i + 1) % 2)
                dve.wait_ge(result, r)
                dve.tensor_copy(x[:, :, i * P:i * P + rows], acc[a][:, 0:1024].rearrange("p (k m) -> p k m", k=KT)[:, :, 0:rows])\
                   .then_inc(moved[a], 1)
                if i:
                    square_sum(i - 1)
            square_sum(TT)

            def scales(n_all):
                dve.wait_ge(root_ready, 2 * n_all)
                dve.reciprocal(rstd[:, :], sd[:, :]).then_inc(rstd_ready, 1)

            def take_rows(dst, rows, a):
                a, r, _ = t.next(a)
                dve.wait_ge(result, r)
                dve.tensor_copy(dst, acc[a][:, 0:1024].rearrange("p (k m) -> p k m", k=KT)[:, :, 0:rows]).then_inc(moved[a], 1)

            take_rows(st_pool[:, :, :], NB * POOL_BUF, 0)
            take_rows(st_conv[:, :, :], NB * 2, 1)
            scales(1)
            t.next(0)
            dve.wait_ge(moved[0], t.taken[0] + 1)

            def lo_of(s, n):
                dve.wait_ge(mw_hi_done, 2 * n + s + 1)
                dve.tensor_tensor(w_lo[:, s, :], w_raw[:, s, :], w_hi[:, s, :].bitcast(F32), ALU.subtract).then_inc(w_split[s], 1)

            def natural(l, j, i, s, n):
                dve.wait_ge(kv_turned, n)
                dve.tensor_scalar(kv_nat_sb[:, j, :, ds((2 * i + s) * P, P)], MS[s][:, 0:MT * P].rearrange("p (m d) -> p m d", m=MT),
                                  1.0, None, ALU.mult).then_inc(kv_nat, 1)

            lo_of(0, 0)
            lo_of(1, 0)
            for l in range(2):
                for j in range(2):
                    if l:
                        dve.wait_ge(kv_stored[j], 16)
                    last = l == 1 and j == 1
                    with t.loop(dve, 0, 3 if last else 4, 2, (1, 1)) as i:
                        for s in range(2):
                            lo_of(s, 4 * (2 * l + j) + i + 1)
                            natural(l, j, i, s, 2 * i + s + 1 + 8 * (2 * l + j))
            t.next(0)
            t.next(1)
            for s in range(2):
                natural(1, 1, 3, s, 31 + s)

            def add_tile(m, a):
                a, r, _ = t.next(a)
                dve.wait_ge(result, r)
                dve.tensor_tensor(t3(x[:, m, :]), a3(a), t3(x[:, m, :]), ALU.add).then_inc(moved[a], 1)

            def norm(n_th, gain, rows=None, rows_out=False):
                def add_square(j):
                    dve.wait_ge(sq_ready, 8 * (n_th - 2) + j + 1)
                    if j == 1:
                        ins = dve.tensor_tensor(sq_sum[:, :], sq[:, 0, :], sq[:, 1, :], ALU.add)
                    else:
                        dve.wait_ge(sq_added, 7 * (n_th - 2) + j - 1)
                        ins = dve.tensor_tensor(sq_sum[:, :], sq_sum[:, :], sq[:, j % 2, :], ALU.add)
                    ins.then_inc(sq_added, 1)

                for m in range(KT):
                    add_tile(m, m % 2)
                    if m >= 2:
                        add_square(m - 1)
                add_square(KT - 1)
                scales(scales_at(n_th))
                a, _, _ = t.next(0)
                dve.wait_ge(moved[a], t.taken[a] + 1)
                if rows_out:
                    t.next(1)
                if rows:
                    rows()
                scale_tiles(n_th, gain)

            def scale_tiles(n_th, gain):
                split = n_th < 5
                for j in range(KT):
                    if split and j >= 2:
                        dve.wait_ge(lo_ready, 8 * (n_th - 1) + j - 1)
                    ins = dve.scalar_tensor_tensor(out=h32[:, j % 2, :] if split else x[:, j, :], in0=x[:, j, :],
                                                   scalar=prm_col(gain + j), in1=sq_sum[:, :], op0=ALU.mult, op1=ALU.mult)
                    if split:
                        ins.then_inc(h32_ready, 1)
                        if j:
                            lo_half(n_th, j - 1)
                    else:
                        ins.then_inc(fin_ready, 1)
                if split:
                    lo_half(n_th, KT - 1)
                    dve.wait_ge(lo_ready, 8 * n_th)

            def lo_half(n_th, j):
                dve.wait_ge(hi_ready, 8 * (n_th - 1) + j + 1)
                dve.tensor_tensor(h_lo[:, j, :], h32[:, j % 2, :], h_hi[:, j, :].bitcast(F32), ALU.subtract).then_inc(lo_ready, 1)

            def add_chunk(sets=(0, 1)):
                for m in range(KT):
                    add_tile(m, sets[m % 2])

            scale_tiles(1, PRM_MIX)
            for s in range(2):
                dve.wait_ge(kt_stored[s], 128)
                dve.wait_ge(kv_stored[s], 32)

            step(dve.memset(u_pad[:, :, 0:WARM], 0.0))
            step(dve.memset(win_a[:, 0:WARM], 0.0))
            step(dve.memset(win_b[:, 0:WARM], 0.0))

            def window(g, i):
                w = WINDOWS[g]
                j = 2 * g + i
                k_in = t.taken[i]
                dve.wait_ge(moved[i], k_in + 1)
                step(dve.tensor_copy(u_keep[:, j, :], u_pad[:, i, WARM + TP - 15:WARM + T]))
                src, dst, other = u_pad[:, i, :], win_a, win_b
                for d in range(g + 1):
                    step(dve.tensor_tensor(dst[:, WARM:WARM + TP], src[:, WARM:WARM + TP],
                                           src[:, WARM - (1 << d):WARM + TP - (1 << d)], ALU.add))
                    src, dst, other = dst, other, dst
                state = st_pool[:, j, :].rearrange("p (b s) -> p b s", b=NB)
                step(dve.tensor_reduce(src[:, WARM + TP:WARM + T], state[:, :, POOL_BUF - w + 1:POOL_BUF], AX, ALU.add))
                step(dve.tensor_tensor(src[:, WARM + TP:WARM + T], src[:, WARM + TP:WARM + T], u_pad[:, i, WARM + TP:WARM + T], ALU.add))
                step(dve.tensor_tensor(src[:, WARM:WARM + 16], src[:, WARM:WARM + 16], cst[:, 16 * g:16 * g + 16], ALU.mult))
                dve.scalar_tensor_tensor(out=y32[:, :], in0=src[:, WARM:WARM + T], scalar=1.0 / w, in1=u_pad[:, i, WARM:WARM + T],
                                         op0=ALU.mult, op1=ALU.subtract).then_inc(d32_ready, 1)
                dve.wait_ge(d_hi_ready, j + 1)
                dve.tensor_tensor(d_lo[:, i, :], y32[:, :], d_hi[:, i, :].bitcast(F32), ALU.subtract).then_inc(d_ready, 1)
                dve.wait_ge(d_ready, j + 1)

            for g in range(4):
                t.next(0)
                t.next(1)
                for i in range(2):
                    window(g, i)
                t.next(0)
                t.next(1)
                gate_moved = [n + 1 for n in t.taken]
                if g:
                    add_chunk()
                for i in range(2):
                    j = 2 * g + i
                    dve.wait_ge(moved[i], gate_moved[i])
                    a, r, _ = t.next(i)
                    dve.wait_ge(result, r)
                    dve.scalar_tensor_tensor(out=t3(y32[:, :]), in0=a3(a), scalar=prm_col(PRM_PSC + j), in1=t3(gate[:, i, :]),
                                             op0=ALU.mult, op1=ALU.mult).then_inc(moved[a], 1)
                    dve.wait_ge(y_hi_ready, j + 1)
                    dve.tensor_tensor(y_lo[:, i, :], y32[:, :], y_hi[:, i, :].bitcast(F32), ALU.subtract).then_inc(y_ready2, 1)
                    dve.wait_ge(y_ready2, j + 1)

            step(dve.memset(cv[:, :, 0:2], 0.0))

            def conv_tile(i, j):
                t.next(0)
                a, r, _ = t.next(1)
                dve.wait_ge(moved[0], t.taken[0] + 1)
                dve.wait_ge(result, r)
                dve.tensor_tensor(t3(cv[:, i, 2:2 + T]), a3(a), t3(c_sb[:, :]), ALU.mult).then_inc(moved[a], 1)
                dve.wait_ge(moved[a], t.taken[a] + 1)
                taps = [prm_col(PRM_CW + 8 * k + j) for k in range(3)]
                state = st_conv[:, j, :].rearrange("p (b s) -> p b s", b=NB)
                dve.tensor_scalar(cc[:, 0:TP], cv[:, i, 0:TP], taps[0], None, ALU.mult).then_inc(cv_ready, 1)
                step(dve.tensor_copy(c_keep[:, j, :], cv[:, i, 2 + TP - 2:2 + T]))
                step(dve.tensor_scalar(cc[:, TP:T], state[:, :, 0], taps[0], None, ALU.mult))
                dve.wait_ge(cv_ready, j + 2)
                for k in (1, 2):
                    step(dve.scalar_tensor_tensor(out=cc[:, 0:TP], in0=cv[:, i, k:k + TP], scalar=taps[k], in1=cc[:, 0:TP],
                                                  op0=ALU.mult, op1=ALU.add))
                    step(dve.scalar_tensor_tensor(out=cc[:, TP:T], in0=state[:, :, 1] if k == 1 else cv[:, i, 2 + TP:2 + T],
                                                  scalar=taps[k], in1=cc[:, TP:T], op0=ALU.mult, op1=ALU.add))
                t.next(0)
                gate_moved = t.taken[0] + 1
                if i == 0:
                    add_chunk((1, 0))
                a, r, _ = t.next(1)
                dve.wait_ge(result, r)
                dve.wait_ge(moved[0], gate_moved)
                dve.tensor_tensor(t3(cy32[:, i, :]), a3(a), t3(cc[:, :]), ALU.mult).then_inc(moved[a], 1)
                dve.wait_ge(moved[a], t.taken[a] + 1)
                dve.tensor_tensor(cy32[:, i, :], cy32[:, i, :], c_gate[:, i, :], ALU.mult).then_inc(cy32_ready, 1)
                dve.wait_ge(y_hi_ready, 8 + j + 1)
                dve.tensor_tensor(y_lo[:, i, :], cy32[:, i, :], y_hi[:, i, :].bitcast(F32), ALU.subtract).then_inc(y_ready2, 1)

            for g in range(4):
                for i in range(2):
                    conv_tile(i, 2 * g + i)

            def cross(l, n_th, gain):
                norm(n_th, gain, rows_out=True)

                def queries(i, a, n):
                    a, r, _ = t.next(a)
                    dve.wait_ge(q_hi_ready, 2 * n + i + 1)
                    dve.tensor_tensor(t3(q_lo[:, i, :]), a3(a), t3(q_hi[:, i, :].bitcast(F32)), ALU.subtract).then_inc(moved[a], 1)

                def attention(n, last):
                    def mix_out(half):
                        for k in range(2):
                            cols = slice(half * 512, half * 512 + 512)
                            dve.wait_ge(y_hi_ready, 16 + 4 * n + 2 * half + k + 1)
                            dve.tensor_tensor(y_lo[:, k, cols], acc[1][:, 1024:1536],
                                              y_hi[:, k, cols].bitcast(F32), ALU.subtract).then_inc(mixed_out, 1)

                    for i in range(TT + 2):
                        if i < TT:
                            dve.wait_ge(scored, 8 * n + i + 1)
                            dve.tensor_reduce(mx[:, i:i + 1], MS[i % 2][:, 0:NM], AX, ALU.max).then_inc(mx_ready, 1)
                            dve.wait_ge(mx_ready, 8 * n + i + 1)
                            dve.tensor_scalar(nmx[:, i:i + 1], mx[:, i:i + 1], -HD ** -0.5, None, ALU.mult).then_inc(nmx_ready, 1)
                        if 1 <= i <= TT:
                            j = i - 1
                            dve.wait_ge(exped, 8 * n + j + 1)
                            dve.reciprocal(rinv[:, j:j + 1], rsum[:, j:j + 1]).then_inc(rinv_ready, 1)
                            dve.wait_ge(rinv_ready, 8 * n + j + 1)
                            dve.tensor_scalar(prob[:, j % 2, :], prob[:, j % 2, :], rinv[:, j:j + 1], None, ALU.mult).then_inc(prob_ready, 1)
                        if i == 6:
                            mix_out(0)
                        if i >= 2:
                            j = i - 2
                            dve.wait_ge(pt_hi_ready, 8 * n + j + 1)
                            cols = slice((j % 4) * P, (j % 4 + 1) * P)
                            dve.tensor_tensor(pt_lo[:, :, cols], acc[1][:, (j % 2) * 512:(j % 2) * 512 + NM].rearrange("p (m t) -> p m t", m=2),
                                              pt_hi[:, :, cols].bitcast(F32), ALU.subtract).then_inc(pt_ready, 1)
                        if i < NB:
                            if i == 0:
                                dve.wait_ge(k_loaded, 16 * n + 16)
                                dve.wait_ge(qbc_ready, 4 * n + 4)
                            for m in range(MT):
                                kb = cache[:, i * MT + m, :]
                                ins = dve.tensor_tensor_reduce(out=kb, in0=kb, in1=q_bc[:, i, :], scale=1.0, scalar=0.0,
                                                               op0=ALU.mult, op1=ALU.add, accum_out=ss[:, m, i:i + 1])
                            if i == NB - 1:
                                ins.then_inc(ss_ready, 1)
                        if i == TT - 1 and not last:
                            queries(0, 0, n + 1)
                    mix_out(1)
                    dve.wait_ge(ss_turned, n + 1)
                    dve.tensor_reduce(s4[0:NB, 0:1], M0[0:NB, 0:NM], AX, ALU.max).then_inc(smx_ready, 1)
                    dve.wait_ge(smx_ready, n + 1)
                    dve.tensor_scalar(s4[0:NB, 1:2], s4[0:NB, 0:1], -HD ** -0.5, None, ALU.mult).then_inc(snmx_ready, 1)
                    dve.wait_ge(s_exped, n + 1)
                    dve.reciprocal(s4[0:NB, 3:4], s4[0:NB, 2:3]).then_inc(srinv_ready, 1)
                    dve.wait_ge(srinv_ready, n + 1)
                    dve.tensor_scalar(sp[0:NB, :], sp[0:NB, :], s4[0:NB, 3:4], None, ALU.mult).then_inc(sp_ready, 1)
                    dve.wait_ge(sp_turned, n + 1)
                    dve.tensor_copy(spt[:, :, 0:NB * NB:NB + 1], M1[:, 0:MT * NB].rearrange("p (m b) -> p m b", m=MT)).then_inc(spt_ready, 1)
                    if not last:
                        queries(1, 0, n + 1)
                    dve.wait_ge(sy_hi_ready, n + 1)
                    dve.tensor_tensor(y_lo[:, :, TP:T], M1[:, 0:2 * NB].rearrange("p (k b) -> p k b", k=2),
                                      y_hi[:, :, TP:T].bitcast(F32), ALU.subtract).then_inc(xy_ready, 1)

                n = HEADS * l
                queries(0, 0, n)
                queries(1, 1, n)
                step(dve.memset(spt[:, :, :], 0.0))
                with t.loop(dve, 0, HEADS - 1, 4, (6, 4)) as h:
                    attention(HEADS * l + h, False)
                    add_chunk((1, 0))
                attention(HEADS * l + HEADS - 1, True)

            cross(0, 2, PRM_XA)

            def conv_state():
                for i in range(3):
                    take_rows(st_sc[:, 8 * i:8 * i + 8, :], NB * 3, i % 2)

            norm(3, PRM_MIX + KT, rows=conv_state)
            dve.memset(dt_rows[96:128, T:9 * P], 0.0).then_inc(dt_padded, 1)
            t.next(0)
            step(dve.memset(raw[:, 0:3], 0.0))
            sw = prm[:, PRM_SW:PRM_SW + 96].rearrange("p (k j) -> p k j", k=4)

            def gather(lo, n, taps, bias, state, src):
                step(dve.tensor_copy(g_prm[:, taps:taps + 4 * n].rearrange("p (k j) -> p k j", k=4), sw[:, :, ds(src, n)]))
                step(dve.tensor_copy(g_prm[:, bias:bias + n], prm[:, ds(PRM_SB + src, n)]))
                step(dve.tensor_copy(g_st[:, state:state + n, :], st_sc[:, ds(src, n), :]))

            def taps_of(a, dst, taps, n_tiles, i, state, keep, n):
                t.next(a)
                dve.wait_ge(moved[a], t.taken[a] + 1)
                tap = [g_prm[:, taps + k * n_tiles + i:taps + k * n_tiles + i + 1] for k in range(4)]
                st3 = g_st[:, state, :].rearrange("p (b s) -> p b s", b=NB)
                step(dve.tensor_copy(s_keep[:, ds(keep, 1), :], raw[:, 3 + TP - 3:3 + T].unsqueeze(1)))
                step(dve.tensor_scalar(dst[:, 0:TP], raw[:, 0:TP], tap[0], None, ALU.mult))
                step(dve.tensor_scalar(dst[:, TP:T], st3[:, :, 0], tap[0], None, ALU.mult))
                for k in (1, 2, 3):
                    ins = dve.scalar_tensor_tensor(out=dst[:, TP:T], in0=st3[:, :, k] if k < 3 else raw[:, 3 + TP:3 + T],
                                                   scalar=tap[k], in1=dst[:, TP:T], op0=ALU.mult, op1=ALU.add)
                    step(ins)
                    ins = dve.scalar_tensor_tensor(out=dst[:, 0:TP], in0=raw[:, k:k + TP], scalar=tap[k], in1=dst[:, 0:TP],
                                                   op0=ALU.mult, op1=ALU.add)
                    if k < 3:
                        step(ins)
                    else:
                        ins.then_inc(tapped, 1)

            gather(0, 1, 28, 36, 4, 16)
            gather(0, 1, 32, 37, 5, 20)
            dve.wait_ge(a_ready, 1)
            for i in range(2):
                step(dve.tensor_copy(dsk[64 * i:64 * i + 64, :], bias_bc[64 * i:64 * i + 64, 2, i:32:2]))
            dve.wait_ge(dt_done, 1)
            dve.tensor_tensor(dtx[:, :, :], M0[:, 0:9 * 32].rearrange("p (i h) -> p i h", h=32),
                              bias_bc[:, 0, :].unsqueeze(1).to_broadcast([P, 9, 32]), ALU.add).then_inc(dtx_ready, 1)
            taps_of(1, bc[:, 0, :], 28, 1, 0, 4, 16, 1)
            dve.wait_ge(dt_step, 3)
            step(dve.scalar_tensor_tensor(out=dt_all[:, :, :], in0=dtx[:, :, :], scalar=0.0, in1=dtl[:, :, :],
                                          op0=ALU.max, op1=ALU.add))
            dve.scalar_tensor_tensor(out=dta[:, :, :], in0=dt_all[:, :, :], scalar=-1.0,
                                     in1=bias_bc[:, 1, :].unsqueeze(1).to_broadcast([P, 9, 32]),
                                     op0=ALU.mult, op1=ALU.mult).then_inc(dta_ready, 1)
            dve.wait_ge(dta_ready, 1)
            dve.wait_ge(dhi_ready, 1)
            dve.tensor_tensor(dta_lo[:, :, :], dta[:, 0:TT, :], dta_hi[:, :, :].bitcast(F32), ALU.subtract).then_inc(dlo_ready, 1)
            dve.wait_ge(acs_e_ready, 1)
            step(dve.tensor_scalar(acs_n[:, :, :], M1[:, 0:256].rearrange("p (c h) -> p c h", c=TT), -1.0, None, ALU.mult))
            dve.wait_ge(dab_ready, 1)
            step(dve.tensor_copy(dtb[:, :, :], M0[:, 0:P].rearrange("p (a b) -> p a b", b=NB)))
            dve.wait_ge(dlo_ready, 1)
            def v8(b):
                return b.rearrange("p (e c) -> p e c", e=E)

            taps_of(0, bc[:, 1, :], 32, 1, 0, 5, 20, 2)

            def ssm_group(g, last):
                gather(0, XT, 0, 16, 0, XT * g)
                step(dve.tensor_copy(g_prm[:, 20:24], dsk[:, ds(XT * g, XT)]))
                step(dve.tensor_copy(g_prm[:, 24:28], prm[:, ds(PRM_NW + XT * g, XT)]))
                for dst, src in ((g_dt, dt_all), (g_acn, acs_n), (g_ace, acs_e), (g_dhi, dta_hi), (g_dlo, dta_lo)):
                    s = src[:, 0:TT, ds(E * g, E)]
                    step(dve.tensor_copy(dst[:, :, :], s.bitcast(F32) if src.dtype == F32R else s))
                step(dve.tensor_copy(g_dtb[:, :, :], dtb[:, ds(XT * g, XT), :]))
                dve.memset(S[:, :], 0.0).then_inc(s_ready, 1)
                dve.tensor_copy(g_dab[:, :, :], dab[:, ds(XT * g, XT), :]).then_inc(g_ready, 1)
                for i, a in enumerate((1, 0, 1, 0)):
                    taps_of(a, xb[:, i, :], 0, XT, i, i, XT * g + i, 0)
                for a in (1, 0, 0, 0):
                    t.next(a)
                dve.wait_ge(conved, 6 * g + 6)
                if not last:
                    gather(0, 1, 28, 36, 4, 17 + g)
                    gather(0, 1, 32, 37, 5, 21 + g)
                dve.tensor_tensor(xd[:, :, :], xb[:, :, TP:T], g_dtb[:, :, :], ALU.mult).then_inc(xd_ready, 1)

                def sample(q):
                    b = q % 2
                    dve.wait_ge(st_new, 4 * g + q + 1)
                    for i in range(2):
                        step(dve.tensor_tensor(bx[:, i], st[:, b, i], bcs[:, 1, i, :].unsqueeze(1).to_broadcast([P, XT, N]), ALU.mult))
                    dve.tensor_reduce(yss[:, :, 2 * q:2 * q + 2].rearrange("p a b -> p b a"), bx[:, :], AX, ALU.add).then_inc(st_read, 1)

                for c in range(TT):
                    n = 8 * g + c + 1
                    cs = slice(c * P, (c + 1) * P)
                    dve.wait_ge(x_turned, n)
                    if c:
                        dve.wait_ge(ydiag_done, n - 1)
                    dve.tensor_tensor(v8(xdt[:, :]), v8(M0[:, :]), g_dt[:, c, :].unsqueeze(2).to_broadcast([P, E, 64]), ALU.mult)\
                       .then_inc(xdt_ready, 1)
                    dve.wait_ge(aend_ready, n)
                    dve.tensor_tensor(te[:, :], aend[:, :], g_acn[:, c, :], ALU.add).then_inc(te_ready, 1)
                    dve.wait_ge(dec_ready, n)
                    dve.tensor_tensor(dec[:, :, :], M1[:, 0:P].unsqueeze(1).to_broadcast([P, E, P]), dec[:, :, :], ALU.mult)\
                       .then_inc(mm_ready, 1)
                    if c:
                        dve.wait_ge(y_turned, n - 1)
                    else:
                        dve.wait_ge(s_stored, 16 * g + 1)
                    dve.wait_ge(yoff_done, n)
                    step(dve.tensor_tensor(v8(y_nat[:, :]), v8(acc[1][:, 1024:1536]), g_ace[:, c, :].unsqueeze(2).to_broadcast([P, E, 64]),
                                           ALU.mult))
                    dve.wait_ge(toe_ready, n)
                    if c:
                        dve.wait_ge(s_done, n - 1)
                    dve.tensor_tensor(v8(xde[:, :]), v8(xdt[:, :]), toe[:, :].unsqueeze(2).to_broadcast([P, E, 64]), ALU.mult)\
                       .then_inc(xde_ready, 1)
                    dve.wait_ge(cdec_ready, n)
                    dve.tensor_tensor(v8(S[:, :]), v8(S[:, :]), cdec[:, :].unsqueeze(2).to_broadcast([P, E, 64]), ALU.mult)\
                       .then_inc(s_decayed, 1)
                    dve.wait_ge(ydiag_done, n)
                    dve.tensor_tensor(y_nat[:, :], acc[1][:, 0:512], y_nat[:, :], ALU.add).then_inc(ynat_ready, 1)
                    dve.wait_ge(s_done, n)
                    dve.wait_ge(s_decayed, n)
                    dve.tensor_tensor(S[:, :], acc[1][:, 512:1024], S[:, :], ALU.add).then_inc(s_ready, 1)
                    dve.wait_ge(y_turned, n)
                    for i in range(XT):
                        ins = dve.scalar_tensor_tensor(out=xb[:, i, cs], in0=xb[:, i, cs], scalar=g_prm[:, 20 + i:21 + i],
                                                       in1=M0[:, i * P:(i + 1) * P], op0=ALU.mult, op1=ALU.add)
                    ins.then_inc(y_back, 1)
                    if c % 2:
                        sample(c // 2)
                dve.wait_ge(st_read, 4 * g + 5)
                for i in range(XT):
                    step(dve.scalar_tensor_tensor(out=xb[:, i, TP:T], in0=xb[:, i, TP:T], scalar=g_prm[:, 20 + i:21 + i],
                                                  in1=yss[:, i, :], op0=ALU.mult, op1=ALU.add))
                dve.wait_ge(moved[0], t.taken[0] + 1)
                dve.wait_ge(y_back, 8 * g + 8)
                for i in range(XT):
                    dve.tensor_tensor(xb[:, i, :], xb[:, i, :], zb[:, i, :], ALU.mult).then_inc(yz_ready, 1)
                    if i:
                        t_add(g, i - 1)
                t_add(g, XT - 1)
                if not last:
                    taps_of(1, bc[:, 0, :], 28, 1, 0, 4, 17 + g, 0)
                scales(g + 4)
                a, _, _ = t.next(1)
                dve.wait_ge(moved[a], t.taken[a] + 1)
                for i in range(XT):
                    dve.scalar_tensor_tensor(out=xb[:, i, :], in0=xb[:, i, :], scalar=g_prm[:, 24 + i:25 + i], in1=t_sum[:, :],
                                             op0=ALU.mult, op1=ALU.mult).then_inc(yn_ready, 1)
                    if i:
                        o_half(g, i - 1)
                o_half(g, XT - 1)
                if not last:
                    taps_of(0, bc[:, 1, :], 32, 1, 0, 5, 21 + g, 0)
                    add_chunk((1, 0))

            def t_add(g, i):
                dve.wait_ge(t_sq_ready, XT * g + i + 1)
                if i == 0:
                    dve.tensor_copy(t_sum[:, :], t_sq[:, :]).then_inc(t_added, 1)
                else:
                    dve.wait_ge(t_added, XT * g + i)
                    dve.tensor_tensor(t_sum[:, :], t_sum[:, :], t_sq[:, :], ALU.add).then_inc(t_added, 1)

            def o_half(g, i):
                dve.wait_ge(o_hi_ready, XT * g + i + 1)
                dve.tensor_tensor(o_lo[:, i, :], xb[:, i, :], o_hi[:, i, :].bitcast(F32), ALU.subtract).then_inc(o_ready, 1)

            with loop(0, G - 1, 14, (10, 9), 85) as g:
                ssm_group(g, False)
            ssm_group(G - 1, True)
            cross(1, 4, PRM_XA + KT)
            norm(5, PRM_FIN)


_INS = ['x_prompt', 'x_sample', 'mem_prompt', 'cache_mem_k', 'cache_mem_v', 'state_pool', 'state_conv',
        'state_ssm_conv', 'state_ssm', 'norm_mix', 'norm_xa', 'norm_final', 'w_in_even', 'pool_w', 'pool_scale',
        'conv_w', 'w_out_even', 'w_in_odd', 'ssm_conv_w', 'ssm_conv_b', 'dt_bias', 'a_log', 'd_skip', 'ssm_norm',
        'w_out_odd', 'w_xa_q', 'w_xa_k', 'w_xa_v', 'w_xa_o']
_OUTS = [('y_prompt', (1, 1024, 1024)), ('y_sample', (8, 1, 1024)), ('mem_k', (2, 1, 256, 4, 256)),
         ('mem_v', (2, 1, 256, 4, 256)), ('pool_prompt', (1, 1, 15, 1024)), ('pool_sample', (1, 8, 15, 1024)),
         ('conv_prompt', (1, 1, 2, 1024)), ('conv_sample', (1, 8, 2, 1024)), ('ssm_conv_prompt', (1, 1, 3, 3072)),
         ('ssm_conv_sample', (1, 8, 3, 3072)), ('ssm_prompt', (1, 1, 32, 64, 128)), ('ssm_sample', (1, 8, 32, 64, 128))]


def kernel(**inputs):
    import numpy as _np
    import concourse.bacc as _bacc
    from concourse import mybir as _mybir
    from concourse.bass_utils import run_bass_kernel_spmd as _run

    nc = _bacc.Bacc("TRN2", target_bir_lowering=False, num_devices=1)
    arrays, ins, outs = {}, {}, {}
    for name in _INS:
        a = _np.ascontiguousarray(inputs[name])
        arrays[f"in_{name}"] = a
        ins[name] = nc.dram_tensor(f"in_{name}", a.shape, _mybir.dt.from_np(a.dtype), kind="ExternalInput").ap()
    arrays["in_constants"] = constants()
    ins["constants"] = nc.dram_tensor("in_constants", (P, C_N), _mybir.dt.float32, kind="ExternalInput").ap()
    for name, shape in _OUTS:
        outs[name] = nc.dram_tensor(f"out_{name}", shape, _mybir.dt.float32, kind="ExternalOutput").ap()
    mem_kt = nc.dram_tensor("mem_kt", (2, D, NM), _mybir.dt.float32).ap()
    build(nc, ins, outs, mem_kt)
    r = _run(nc, [arrays], core_ids=[0])
    return tuple(r.results[0][f"out_{name}"] for name, _ in _OUTS)
```
